# Optimizing a Trainium2 kernel written in Bass

```python
import math
import jax, jax.numpy as jnp
from jax import lax
import numpy as np

D_MODEL = 1024
BATCH = 1
SEQ = 512
DEPTH = 1
DEC_BATCH = 8
DEC_SEQ = 4
PAST_LEN = 2048
PAGE_SIZE = 128

N_HEADS = 8
N_KV_HEADS = 2
HEAD_DIM = 64
GQA_GROUP = N_HEADS // N_KV_HEADS
D_ATTN = N_HEADS * HEAD_DIM
D_CONV = D_MODEL - D_ATTN
D_MIX = D_ATTN + D_CONV
D_KV = N_KV_HEADS * HEAD_DIM
D_IN = D_ATTN + 2 * D_KV + 3 * D_CONV
CONV_WIDTH = 3
WINDOW = 128
BLOCK = 128
N_META = 16
N_BUCKETS = 32
MAX_DISTANCE = 128
D_FF = 2816
DN_ALPHA = (2 * DEPTH) ** 0.25
DN_BETA = (8 * DEPTH) ** -0.25
LN_EPS = 1e-5

kernel_name = "hymba_swa_shortconv_macaron_deepnorm_step"

def layer_norm(x, g, b):
    xf = x.astype(jnp.float32)
    mu = jnp.mean(xf, axis=-1, keepdims=True)
    var = jnp.mean(jnp.square(xf - mu), axis=-1, keepdims=True)
    y = (xf - mu) * lax.rsqrt(var + LN_EPS) * g.astype(jnp.float32) + b.astype(jnp.float32)
    return y.astype(x.dtype)

def swiglu(x, wg, wu, wd):
    return (jax.nn.silu(x @ wg) * (x @ wu)) @ wd

def t5_bucket(d):
    d = jnp.maximum(d, 0)
    max_exact = N_BUCKETS // 2
    df = jnp.maximum(d, 1).astype(jnp.float32)
    large = max_exact + (jnp.log(df / max_exact) / math.log(MAX_DISTANCE / max_exact)
                         * (N_BUCKETS - max_exact)).astype(jnp.int32)
    large = jnp.minimum(large, N_BUCKETS - 1)
    return jnp.where(d < max_exact, d, large)

def rel_bias_heads(d, rel_tab):
    b = rel_tab[t5_bucket(d)].astype(jnp.float32)
    b = jnp.moveaxis(b, -1, 0)
    return b.reshape((N_KV_HEADS, GQA_GROUP) + d.shape)

def sink_softmax(s, sink):
    sk = sink.astype(jnp.float32).reshape(N_KV_HEADS, GQA_GROUP, 1, 1)
    m = jnp.maximum(jnp.max(s, axis=-1, keepdims=True), sk)
    p = jnp.exp(s - m)
    return p / (jnp.sum(p, axis=-1, keepdims=True) + jnp.exp(sk - m))

def project(x, w):
    z = x @ w
    cuts = [D_ATTN, D_ATTN + D_KV, D_ATTN + 2 * D_KV,
            D_ATTN + 2 * D_KV + D_CONV, D_ATTN + 2 * D_KV + 2 * D_CONV]
    q, k, v, bg, cg, h = jnp.split(z, cuts, axis=-1)
    lead = x.shape[:-1]
    q = q.reshape(lead + (N_HEADS, HEAD_DIM))
    k = k.reshape(lead + (N_KV_HEADS, HEAD_DIM))
    v = v.reshape(lead + (N_KV_HEADS, HEAD_DIM))
    return q, k, v, bg, cg, h

def swa_prompt(q, k, v, sink, rel_tab):
    B, L = q.shape[0], q.shape[1]
    pad = (-L) % BLOCK
    nb = (L + pad) // BLOCK
    padf = lambda t: jnp.pad(t, ((0, 0), (pad, 0), (0, 0), (0, 0)))
    qb = padf(q).reshape(B, nb, BLOCK, N_KV_HEADS, GQA_GROUP, HEAD_DIM)
    kb = padf(k).reshape(B, nb, BLOCK, N_KV_HEADS, HEAD_DIM)
    vb = padf(v).reshape(B, nb, BLOCK, N_KV_HEADS, HEAD_DIM)

    def band(t):
        prev = jnp.pad(t, ((0, 0), (1, 0), (0, 0), (0, 0), (0, 0)))[:, :nb]
        return jnp.concatenate([prev, t], axis=2)

    kk, vv = band(kb), band(vb)
    s = jnp.einsum('bnqkgd,bnskd->bnkgqs', qb, kk).astype(jnp.float32) * (HEAD_DIM ** -0.5)
    qi = jnp.arange(BLOCK)
    sj = jnp.arange(2 * BLOCK)
    d = qi[:, None] + BLOCK - sj[None, :]
    key_idx = (jnp.arange(nb)[:, None] - 1) * BLOCK + sj[None, :]
    valid = ((d >= 0) & (d <= WINDOW))[None] & (key_idx >= pad)[:, None, :]
    s = jnp.where(valid[None, :, None, None], s + rel_bias_heads(d, rel_tab), -jnp.inf)
    p = sink_softmax(s, sink).astype(vv.dtype)
    o = jnp.einsum('bnkgqs,bnskd->bnqkgd', p, vv).reshape(B, nb * BLOCK, D_ATTN)[:, pad:]
    return o, k[:, -WINDOW:], v[:, -WINDOW:]

def swa_sample(q, k, v, k_buf, v_buf, sink, rel_tab):
    B, T = q.shape[0], q.shape[1]
    W = k_buf.shape[1]
    kk = jnp.concatenate([k_buf.astype(k.dtype), k], axis=1)
    vv = jnp.concatenate([v_buf.astype(v.dtype), v], axis=1)
    qg = q.reshape(B, T, N_KV_HEADS, GQA_GROUP, HEAD_DIM)
    s = jnp.einsum('btkgd,bskd->bkgts', qg, kk).astype(jnp.float32) * (HEAD_DIM ** -0.5)
    d = jnp.arange(T)[:, None] + W - jnp.arange(W + T)[None, :]
    valid = (d >= 0) & (d <= WINDOW)
    s = jnp.where(valid, s + rel_bias_heads(d, rel_tab), -jnp.inf)
    p = sink_softmax(s, sink).astype(vv.dtype)
    o = jnp.einsum('bkgts,bskd->btkgd', p, vv).reshape(B, T, D_ATTN)
    return o, kk[:, -WINDOW:], vv[:, -WINDOW:]

def short_conv(u, prev, w):
    T = u.shape[1]
    full = jnp.concatenate([prev.astype(u.dtype), u], axis=1)
    out = sum(w[j] * full[:, j:j + T] for j in range(CONV_WIDTH))
    return out, full[:, -(CONV_WIDTH - 1):]

def token_mixer(x, attend, conv_prev, w_in_l, conv_w_l, w_out_l):
    q, k, v, bg, cg, h = project(x, w_in_l)
    a, k_state, v_state = attend(q, k, v)
    c, conv_state = short_conv(cg * h, conv_prev, conv_w_l)
    y = jnp.concatenate([a, bg * c], axis=-1) @ w_out_l
    return y, k_state, v_state, conv_state

def trunk_layer(x, attend, conv_prev, w_in_l, conv_w_l, w_out_l, wg_l, wu_l, wd_l, g_l, b_l):
    x = layer_norm(DN_ALPHA * x + 0.5 * swiglu(x, wg_l[0], wu_l[0], wd_l[0]), g_l[0], b_l[0])
    y, ks, vs, cs = token_mixer(x, attend, conv_prev, w_in_l, conv_w_l, w_out_l)
    x = layer_norm(DN_ALPHA * x + y, g_l[1], b_l[1])
    x = layer_norm(DN_ALPHA * x + 0.5 * swiglu(x, wg_l[1], wu_l[1], wd_l[1]), g_l[2], b_l[2])
    return x, ks, vs, cs

def setup_inputs(seed: int = 0) -> dict:
    key = jax.random.key(seed)
    ks = jax.random.split(key, 16)
    nrm = lambda k, shape: jax.random.normal(k, shape, jnp.float32)
    x_prompt = nrm(ks[0], (BATCH, SEQ, D_MODEL))
    x_sample = nrm(ks[1], (DEC_BATCH, DEC_SEQ, D_MODEL))
    cache_k = nrm(ks[2], (DEPTH, DEC_BATCH, WINDOW, N_KV_HEADS, HEAD_DIM))
    cache_v = nrm(ks[3], (DEPTH, DEC_BATCH, WINDOW, N_KV_HEADS, HEAD_DIM)) * DN_BETA
    state_conv = nrm(ks[4], (DEPTH, DEC_BATCH, CONV_WIDTH - 1, D_CONV)) * DN_BETA
    meta_tokens = nrm(ks[5], (N_META, D_MODEL))
    rel_bias = 0.5 * nrm(ks[6], (N_BUCKETS, N_HEADS))
    col_scale = jnp.concatenate([
        jnp.ones((D_ATTN + D_KV,), jnp.float32),
        jnp.full((D_KV,), DN_BETA, jnp.float32),
        jnp.ones((2 * D_CONV,), jnp.float32),
        jnp.full((D_CONV,), DN_BETA, jnp.float32)])
    w_in = nrm(ks[7], (DEPTH, D_MODEL, D_IN)) * (D_MODEL ** -0.5) * col_scale
    conv_w = nrm(ks[8], (DEPTH, CONV_WIDTH, D_CONV)) * (CONV_WIDTH ** -0.5)
    attn_sink = nrm(ks[9], (DEPTH, N_HEADS))
    w_out = nrm(ks[10], (DEPTH, D_MIX, D_MODEL)) * (D_MIX ** -0.5) * DN_BETA
    ffn_w_gate = nrm(ks[11], (DEPTH, 2, D_MODEL, D_FF)) * (D_MODEL ** -0.5)
    ffn_w_up = nrm(ks[12], (DEPTH, 2, D_MODEL, D_FF)) * (D_MODEL ** -0.5) * DN_BETA
    ffn_w_down = nrm(ks[13], (DEPTH, 2, D_FF, D_MODEL)) * (D_FF ** -0.5) * DN_BETA
    ln_g = 1.0 + 0.02 * nrm(ks[14], (DEPTH, 3, D_MODEL))
    ln_b = 0.02 * nrm(ks[15], (DEPTH, 3, D_MODEL))
    return {"x_prompt": x_prompt, "x_sample": x_sample, "cache_k": cache_k,
            "cache_v": cache_v, "state_conv": state_conv, "meta_tokens": meta_tokens,
            "rel_bias": rel_bias, "w_in": w_in, "conv_w": conv_w, "attn_sink": attn_sink,
            "w_out": w_out, "ffn_w_gate": ffn_w_gate, "ffn_w_up": ffn_w_up,
            "ffn_w_down": ffn_w_down, "ln_g": ln_g, "ln_b": ln_b}

def reference(x_prompt, x_sample, cache_k, cache_v, state_conv, meta_tokens, rel_bias,
              w_in, conv_w, attn_sink, w_out, ffn_w_gate, ffn_w_up, ffn_w_down, ln_g, ln_b):
    Bp = x_prompt.shape[0]
    meta = jnp.broadcast_to(meta_tokens.astype(x_prompt.dtype)[None], (Bp, N_META, D_MODEL))
    xp = jnp.concatenate([meta, x_prompt], axis=1)
    xs = x_sample
    conv_zero = jnp.zeros((Bp, CONV_WIDTH - 1, D_CONV), xp.dtype)

    kp_l, vp_l, cp_l, ks_l, vs_l, cs_l = [], [], [], [], [], []
    for l in range(DEPTH):
        def attend_p(q, k, v, l=l):
            return swa_prompt(q, k, v, attn_sink[l], rel_bias)

        def attend_s(q, k, v, l=l):
            return swa_sample(q, k, v, cache_k[l], cache_v[l], attn_sink[l], rel_bias)

        xp, kp, vp, cp = trunk_layer(xp, attend_p, conv_zero, w_in[l], conv_w[l], w_out[l],
                                     ffn_w_gate[l], ffn_w_up[l], ffn_w_down[l], ln_g[l], ln_b[l])
        xs, kss, vss, css = trunk_layer(xs, attend_s, state_conv[l], w_in[l], conv_w[l], w_out[l],
                                        ffn_w_gate[l], ffn_w_up[l], ffn_w_down[l], ln_g[l], ln_b[l])
        kp_l.append(kp); vp_l.append(vp); cp_l.append(cp)
        ks_l.append(kss); vs_l.append(vss); cs_l.append(css)

    y_prompt = xp[:, N_META:]
    y_sample = xs
    new_k_prompt = jnp.stack(kp_l, axis=0)
    new_v_prompt = jnp.stack(vp_l, axis=0)
    new_conv_prompt = jnp.stack(cp_l, axis=0)
    new_k_sample = jnp.stack(ks_l, axis=0)
    new_v_sample = jnp.stack(vs_l, axis=0)
    new_conv_sample = jnp.stack(cs_l, axis=0)
    return (y_prompt, y_sample, new_k_prompt, new_v_prompt, new_conv_prompt,
            new_k_sample, new_v_sample, new_conv_sample)


_drawn_inputs = setup_inputs


def setup_inputs(seed=0):
    import zlib

    import numpy as np

    out = dict(_drawn_inputs(seed))
    spreads = {}
    factors = {'meta_tokens': 3.589, 'rel_bias': 3.87, 'attn_sink': 8.0}
    for name, (base, spread) in spreads.items():
        noise = np.random.default_rng([zlib.crc32(name.encode()), seed]).standard_normal(out[name].shape)
        drawn = base * np.exp(spread * noise) if base else spread * noise
        out[name] = __import__('jax').numpy.asarray(drawn.astype(out[name].dtype))
    for name, factor in factors.items():
        out[name] = (out[name] * factor).astype(out[name].dtype)
    return out
```

```python
from contextlib import ExitStack

import numpy as np

import concourse.bass as bass
from concourse import mybir
from concourse.alu_op_type import AluOpType as ALU

ACT = mybir.ActivationFunctionType
F32 = mybir.dt.float32
F32R = mybir.dt.float32r
AX_X = mybir.AxisListType.X

P = 128
D_MODEL = 1024
SEQ = 512
N_META = 16
DEC_BATCH = 8
DEC_SEQ = 4
N_HEADS = 8
N_KV = 2
GQA = N_HEADS // N_KV
HEAD_DIM = 64
D_ATTN = N_HEADS * HEAD_DIM
D_CONV = D_MODEL - D_ATTN
D_KV = N_KV * HEAD_DIM
WINDOW = 128
N_BUCKETS = 32
MAX_DISTANCE = 128
D_FF = 2816
ALPHA = float(2.0 ** 0.25)
LN_EPS = 1e-5
SCALE = HEAD_DIM ** -0.5
MASKED = -1.0e30

PROMPT = N_META + SEQ
SAMPLE = DEC_BATCH * DEC_SEQ
TOK = PROMPT + SAMPLE
HALF = TOK // 2
KT = D_MODEL // P
FT = D_FF // P
CT = D_CONV // P
XT = 112
N_XT = TOK // XT
LAST_KEYS = PROMPT - WINDOW

SLOTS = 4
GU_UNITS = 2 * FT
DN_CUT = (0, 6, 12, 17, 22)
DN_UNITS = 4 * KT
WI_ORDER = (("k", 0), ("v", 0), ("q", 0), ("q", 1), ("q", 2), ("q", 3),
            ("cg", 0), ("h", 0), ("bg", 0), ("cg", 1), ("h", 1), ("bg", 1),
            ("cg", 2), ("h", 2), ("bg", 2), ("cg", 3), ("h", 3), ("bg", 3))
WI_GROUPS = (4, 2, 4, 4, 4)
U_GU = (0, GU_UNITS + 2 * DN_UNITS + len(WI_ORDER) + KT)
U_DN = (U_GU[0] + GU_UNITS, U_GU[1] + GU_UNITS)
U_WI = U_DN[0] + 2 * DN_UNITS
U_WO = U_WI + len(WI_ORDER)
U_END = U_DN[1] + 2 * DN_UNITS
GU_GROUPS = FT // 2
T_GU = (0, 2 * GU_UNITS + 2 * DN_UNITS + 2 * len(WI_ORDER) + 2 * KT)
T_DN = (T_GU[0] + 2 * GU_UNITS, T_GU[1] + 2 * GU_UNITS)
T_WI = T_DN[0] + 2 * DN_UNITS
T_WO = T_WI + 2 * len(WI_ORDER)

COL0 = {"q": 0, "k": D_ATTN, "v": D_ATTN + D_KV, "bg": D_ATTN + 2 * D_KV,
        "cg": D_ATTN + 2 * D_KV + D_CONV, "h": D_ATTN + 2 * D_KV + 2 * D_CONV}

BLOCKS = ((0, 96), (96, 96), (192, 88), (280, 124), (404, 124))
ITEMS = [(b, g) for b in range(len(BLOCKS)) for g in range(N_KV)] + [("s", 0), ("s", 1)]
ITEMS_H0 = 6
QMAX = 124
SPAN = QMAX + WINDOW
S_COLS = WINDOW + SAMPLE
T_W = WINDOW - 1 + SPAN + 1


def wi_steps():
    out, u0 = [], 0
    for size in WI_GROUPS:
        for half in range(2):
            out += [(u0 + u, half) for u in range(size)]
        u0 += size
    return out


WI_STEPS = wi_steps()

Y_TILES = [(0, 0, 112), (0, 112, 112), (0, 224, 56), (1, 280, 56), (1, 336, 112), (1, 448, 112)]
X_DMAS = [2, 1, 1, 1, 2]
N_CONSTS = 3 + 3 + 1 + 1 + 4
V_TILES = ([(0, "v", 0, 96), (1, "v", 0, 96), (2, "v", 96, 96), (3, "v", 64, 128), (4, "v", 192, 88)],
           [(5, "v", 152, 128), (6, "v", 280, 124), (7, "v", 276, 128), (8, "v", 404, 124),
            (9, "v", PROMPT, SAMPLE), (10, "k", LAST_KEYS, P), (11, "v", LAST_KEYS, P),
            (12, "k", PROMPT, SAMPLE)])
PREP = 2 * WI_GROUPS[0] - 1
Z_KV = (1, WI_GROUPS[0] + 1)
CONV_ORDER = [(WI_ORDER[u][1], half) for u, half in WI_STEPS if WI_ORDER[u][0] == "h"]
BG_ORDER = [(WI_ORDER[u][1], half) for u, half in WI_STEPS if WI_ORDER[u][0] == "bg"]


def free_after(n):
    for f in range(2):
        if U_GU[f] <= n < U_GU[f] + GU_UNITS:
            i, u = divmod(n - U_GU[f], 4)
            return T_GU[f] + 8 * i + 4 + u + 1
        if U_DN[f] <= n < U_DN[f] + 2 * DN_UNITS:
            return T_DN[f] + n - U_DN[f] + 1
    if n < U_WO:
        return T_WI + WI_STEPS.index((n - U_WI, 1)) + 1
    i, u = divmod(n - U_WO, 4)
    return T_WO + 8 * i + 4 + u + 1


def tiles_of(n):
    for f in range(2):
        if U_DN[f] <= n < U_DN[f] + 2 * DN_UNITS:
            d = (n - U_DN[f]) % 4
            return DN_CUT[d + 1] - DN_CUT[d]
    return KT


def arrived_values():
    total, out = [0] * SLOTS, []
    for n in range(U_END):
        is_q = U_WI <= n < U_WO and WI_ORDER[n - U_WI][0] == "q"
        total[n % SLOTS] += 48 if U_WO <= n < U_WO + KT else 32 if is_q else 16
        out.append(total[n % SLOTS])
    return out


ARRIVED = arrived_values()


def bias_constants():
    d = 2 * WINDOW - 1 - np.arange(T_W)
    valid = (d >= 0) & (d <= WINDOW)
    exact = N_BUCKETS // 2
    df = np.maximum(d, 1).astype(np.float32)
    large = exact + (np.log(df / np.float32(exact)) / np.float32(np.log(MAX_DISTANCE / exact))
                     * np.float32(N_BUCKETS - exact)).astype(np.int32)
    bucket = np.where(d < exact, np.maximum(d, 0), np.minimum(large, N_BUCKETS - 1))
    one_hot = ((np.arange(N_BUCKETS)[:, None] == bucket[None, :]) & valid[None, :]).astype(np.float32)
    mask = np.broadcast_to(np.where(valid, 0.0, MASKED).astype(np.float32), (N_HEADS, T_W))
    return one_hot, np.ascontiguousarray(mask)


def build(nc, x_prompt, x_sample, cache_k, cache_v, state_conv, meta_tokens, rel_bias, w_in, conv_w,
          attn_sink, w_out, w_gate, w_up, w_down, ln_g, ln_b, identity, one_hot, mask_row,
          y_prompt, y_sample, new_k_prompt, new_v_prompt, new_conv_prompt,
          new_k_sample, new_v_sample, new_conv_sample):
    ctx = ExitStack()
    with ctx:
        def sb(name, shape, dt=F32, stack=ctx):
            return stack.enter_context(nc.sbuf_tensor(name, shape, dt))

        def sem(name):
            return ctx.enter_context(nc.semaphore(name))

        x_res = sb("x_res", [P, KT, TOK])
        w_raw = sb("w_raw", [P, SLOTS, KT, P])
        w_hi = sb("w_hi", [P, SLOTS, KT, P], F32R)
        w_lo = sb("w_lo", [P, SLOTS, KT, P], F32R)
        ident = sb("ident", [P, P])
        mean_of = sb("mean_of", [P, P])
        coef = sb("coef", [P, 64])
        sinks = sb("sinks", [P, N_HEADS])
        sink_row = sb("sink_row", [P, 1])
        eps = sb("eps", [P, 1])
        ln_sum = sb("ln_sum", [P, 2, HALF])
        ln_sq = sb("ln_sq", [P, 2, HALF])
        rstd = sb("rstd", [P, HALF])
        silu_g = sb("silu_g", [P, 2, HALF])
        h_f32 = sb("h_f32", [P, 2, HALF])
        ffn = ExitStack()
        x_hi = sb("x_hi", [P, KT, TOK], F32R, ffn)
        x_lo = sb("x_lo", [P, KT, TOK], F32R, ffn)
        h_hi = sb("h_hi", [P, FT, TOK], F32R, ffn)
        h_lo = sb("h_lo", [P, FT, TOK], F32R, ffn)
        ffn.close()
        late = ExitStack()
        y_rows = sb("y_rows", [XT, 6, D_MODEL], F32, late)
        sb("pad_to_h", [P, 2 * KT * TOK - 6 * D_MODEL], F32, late)
        early = ExitStack()
        x_rows = sb("x_rows", [XT, N_XT, D_MODEL], F32, early)
        param_rows = sb("param_rows", [60, P], F32, early)
        rel_tab = sb("rel_tab", [N_BUCKETS, N_HEADS], F32, early)
        hot = sb("hot", [N_BUCKETS, T_W], F32, early)
        mask_sb = sb("mask_sb", [N_HEADS, T_W], F32, early)
        bias_row = sb("bias_row", [N_HEADS, T_W], F32, early)
        early.close()
        mix_hi = sb("mix_hi", [P, KT, TOK], F32R, late)
        mix_lo = sb("mix_lo", [P, KT, TOK], F32R, late)
        q_t = sb("q_t", [P, GQA, TOK], F32, late)
        k_t = sb("k_t", [P, TOK], F32, late)
        v_t = sb("v_t", [P, TOK], F32, late)
        bias = sb("bias", [P, N_HEADS, SPAN], F32, late)
        bias_s = sb("bias_s", [P, 2, S_COLS], F32, late)
        u_p = sb("u_p", [P, CT, PROMPT + 2], F32, late)
        u_s = sb("u_s", [P, CT, DEC_BATCH, DEC_SEQ + 2], F32, late)
        v_tok = sb("v_tok", [P, 13, P], F32, late)
        kc_t = sb("kc_t", [P, DEC_BATCH, P], F32, late)
        vc = sb("vc", [P, DEC_BATCH, P], F32, late)
        q_diag = sb("q_diag", [P, 2, P], F32, late)
        p_t = sb("p_t", [P, 2, GQA * QMAX], F32, late)
        ut = ExitStack()
        u_rows = sb("u_rows", [DEC_BATCH, 3, D_CONV], F32, ut)
        ut.close()
        taps = sb("taps", [P, 3, HALF], F32, late)
        conv = sb("conv", [P, 2, 2, HALF], F32, late)
        cg_sb = sb("cg_sb", [P, 2, 2, HALF], F32, late)
        row_max = sb("row_max", [P, 3, GQA], F32, late)
        neg_max = sb("neg_max", [P, 3, GQA], F32, late)
        row_sum = sb("row_sum", [P, 3, GQA], F32, late)
        sink_exp = sb("sink_exp", [P, 3, GQA], F32, late)
        r_den = sb("r_den", [P, 3, GQA], F32, late)
        kc = ExitStack()
        kc_rows = sb("kc_rows", [P, DEC_BATCH, P], F32, kc)
        st_rows = sb("st_rows", [DEC_BATCH * 2, D_CONV], F32, kc)
        kc.close()
        probs = sb("probs", [P, 3, GQA, SPAN], F32, late)
        late.close()

        acc = [ctx.enter_context(nc.psum_tensor(f"acc{i}", [P, 512], F32)) for i in range(4)]
        aux = [ctx.enter_context(nc.psum_tensor(f"aux{i}", [P, 512], F32)) for i in range(4)]
        bias_dram = nc.dram_tensor("bias_dram", (N_HEADS, QMAX, T_W), F32, kind="Internal").ap()

        weights_in = [sem(f"weights_in{i}") for i in range(SLOTS)]
        x_in = [sem(f"x_in{i}") for i in range(N_XT)]
        consts_in = sem("consts_in")
        bias_out = sem("bias_out")
        bias_in = sem("bias_in")
        bias_s_in = sem("bias_s_in")
        kc_in = sem("kc_in")
        vc_in = sem("vc_in")
        outputs_out = sem("outputs_out")
        hi_ready = sem("hi_ready")
        lo_ready = sem("lo_ready")
        steps_done = sem("steps_done")
        memset_done = sem("memset_done")
        params_t = sem("params_t")
        coef_ready = sem("coef_ready")
        table_ready = sem("table_ready")
        xt_done = sem("xt_done")
        x0_res = sem("x0_res")
        x_hi_done = sem("x_hi_done")
        x_ready = sem("x_ready")
        res_biased = sem("res_biased")
        silu_done = sem("silu_done")
        h_done = sem("h_done")
        h_hi_done = sem("h_hi_done")
        h_ready = sem("h_ready")
        r_done = sem("r_done")
        sum_done = sem("sum_done")
        mean_done = sem("mean_done")
        centered = sem("centered")
        squared = sem("squared")
        sq_added = sem("sq_added")
        var_done = sem("var_done")
        std_done = sem("std_done")
        rstd_done = sem("rstd_done")
        scaled = sem("scaled")
        y_biased = sem("y_biased")
        y_t = sem("y_t")
        y_rows_act = sem("y_rows_act")
        y_rows_dve = sem("y_rows_dve")
        zero_done = sem("zero_done")
        z_act = sem("z_act")
        z_dve = sem("z_dve")
        kct_done = sem("kct_done")
        kct_copied = sem("kct_copied")
        vt_done = sem("vt_done")
        vt_copied = sem("vt_copied")
        qd_ready = sem("qd_ready")
        taps_done = sem("taps_done")
        taps_added = sem("taps_added")
        gated_hi = sem("gated_hi")
        gated_lo = sem("gated_lo")
        ut_done = sem("ut_done")
        ut_copied = sem("ut_copied")
        scores_done = sem("scores_done")
        masked = sem("masked")
        max_done = sem("max_done")
        max_sink = sem("max_sink")
        neg_ready = sem("neg_ready")
        exps_done = sem("exps_done")
        den_done = sem("den_done")
        rden_done = sem("rden_done")
        probs_ready = sem("probs_ready")
        pt_done = sem("pt_done")
        pt_copied = sem("pt_copied")
        att_done = sem("att_done")
        att_hi = sem("att_hi")
        att_lo = sem("att_lo")

        def cols(half):
            return slice(half * HALF, (half + 1) * HALF)

        def bcast(ap, n):
            return ap.unsqueeze(1).to_broadcast([P, n, HALF])

        G0, B0, C0 = 0, 24, 48

        def z_reader(m):
            return "act" if WI_ORDER[WI_STEPS[m][0]][0] in ("k", "v", "q", "cg") else "dve"

        def z_count(m, who):
            return sum(z_reader(i) == who for i in range(m + 1))

        def step_count(kind, c, half):
            return z_count(WI_STEPS.index((WI_ORDER.index((kind, c)), half)), "dve")

        AB = 2 * (WI_GROUPS[0] + WI_GROUPS[1])

        def z_bank(m):
            return m % 4 if m < AB else (m - AB) % 3

        def z_before(m):
            for i in range(m - 1, -1, -1):
                if z_bank(i) == z_bank(m):
                    return i
            return None

        def wo_bank(k):
            return k % 3 if k < KT else k % 4

        def wo_before(k):
            for i in range(k - 1, -1, -1):
                if wo_bank(i) == wo_bank(k):
                    return i
            return None

        WO_ORDER = [(4 * g + u, half) for g in range(2) for half in range(2) for u in range(4)]

        def sum_need(L):
            return {0: 8, 1: 16, 2: 28, 3: 32, 4: 40, 5: 48}[L]

        def copy_v_tiles(eng, part):
            eng.wait_ge(vt_done, part + 1)
            for i, (slot, src, t0, w) in enumerate(V_TILES[part]):
                last = nc.scalar.activation(v_tok[0:w, slot, :], aux[2 + i // 4][0:w, (i % 4) * P:(i % 4 + 1) * P], ACT.Copy)
            last.then_inc(vt_copied, 1)

        def item_shape(a):
            b, g = ITEMS[a]
            if b == "s":
                return P, 1, S_COLS
            return BLOCKS[b][1], GQA, min(WINDOW, BLOCKS[b][0]) + BLOCKS[b][1]

        def sample_cols(t, rows, h, j):
            at = PROMPT + 16 * j
            return t[rows, h, at:at + 16].rearrange("p (b t) -> p b t", b=4)

        def sample_out(rows, kv, h):
            return acc[3][rows, 0:P].rearrange("p (b g t) -> p b g t", b=4, t=DEC_SEQ)[:, :, GQA * kv + h]

        block = ctx.enter_context(nc.Block())

        @block.sync
        def _(sp):
            def gate_up(f, i, u, wait):
                n0 = U_GU[f] + u
                w = (w_gate, w_up)[u % 2][0, f].rearrange("(k p) n -> p k n", p=P)
                if wait:
                    sp.wait_ge(lo_ready, n0 + 4 * i - SLOTS + 1)
                sp.dma_start(w_raw[:, n0 % SLOTS, :, :],
                             w[:, :, bass.ds(2 * P * i + (u // 2) * P, P)]).then_inc(weights_in[n0 % SLOTS], 16)

            def down(f, half, c, d):
                n0 = U_DN[f] + DN_UNITS * half + d
                w = w_down[0, f].rearrange("(k p) n -> p k n", p=P)
                sp.wait_ge(lo_ready, n0 + 4 * c - SLOTS + 1)
                sp.dma_start(w_raw[:, n0 % SLOTS, 0:DN_CUT[d + 1] - DN_CUT[d], :],
                             w[:, DN_CUT[d]:DN_CUT[d + 1], bass.ds(P * c, P)]).then_inc(weights_in[n0 % SLOTS], 16)

            def feed_forward(f):
                for u in range(4):
                    gate_up(f, 0, u, wait=f > 0)
                if f == 0:
                    sp.wait_ge(table_ready, 1)
                    sp.dma_start(bias_dram, bias_row[:, :].unsqueeze(1).to_broadcast([N_HEADS, QMAX, T_W])
                                 ).then_inc(bias_out, 16)
                with sp.Fori(1, GU_GROUPS) as i:
                    for u in range(4):
                        gate_up(f, i, u, wait=True)
                for half in range(2):
                    with sp.Fori(0, KT) as c:
                        for d in range(4):
                            down(f, half, c, d)

            feed_forward(0)
            w_in_k = w_in[0].rearrange("(k p) n -> p k n", p=P)
            for n, (kind, c) in enumerate(WI_ORDER):
                n += U_WI
                sp.wait_ge(lo_ready, n - SLOTS + 1)
                if kind == "q":
                    for g in range(N_KV):
                        at = (GQA * g + c) * HEAD_DIM
                        sp.dma_start(w_raw[:, n % SLOTS, :, g * HEAD_DIM:(g + 1) * HEAD_DIM],
                                     w_in_k[:, :, at:at + HEAD_DIM]).then_inc(weights_in[n % SLOTS], 16)
                else:
                    at = COL0[kind] + c * P
                    sp.dma_start(w_raw[:, n % SLOTS, :, :], w_in_k[:, :, at:at + P]).then_inc(weights_in[n % SLOTS], 16)
                if n == U_WI + 7:
                    sp.wait_ge(steps_done, T_WI)
                    sp.dma_start(kc_rows[:, :, :], cache_k[0].rearrange("b s g e -> s b (g e)")).then_inc(kc_in, 16)
                    sp.dma_start(st_rows[:, :], state_conv[0].rearrange("b j n -> (b j) n")).then_inc(kc_in, 16)
                    sp.wait_ge(bias_out, 16)
                    sp.dma_start(bias[0:QMAX, :, :],
                                 bass.AP(tensor=bias_dram.tensor, offset=WINDOW - 1,
                                         ap=[[T_W - 1, QMAX], [QMAX * T_W, N_HEADS], [1, SPAN]])).then_inc(bias_in, 16)
                    for b in range(4):
                        rows = slice(32 * b, 32 * b + 32)
                        for j in range(2):
                            sp.dma_start(bias_s[rows, j, 0:WINDOW],
                                         bass.AP(tensor=bias_dram.tensor, offset=WINDOW - 1,
                                                 ap=[[QMAX * T_W, N_HEADS], [T_W - 1, DEC_SEQ], [1, WINDOW]])).then_inc(bias_s_in, 16)
                    sp.wait_ge(zero_done, 2)
                    for b in range(4):
                        rows = slice(32 * b, 32 * b + 32)
                        for j in range(2):
                            at = WINDOW + (4 * j + b) * DEC_SEQ
                            sp.dma_start(bias_s[rows, j, at:at + DEC_SEQ],
                                         bass.AP(tensor=bias_dram.tensor, offset=2 * WINDOW - 1,
                                                 ap=[[QMAX * T_W, N_HEADS], [T_W - 1, DEC_SEQ], [1, DEC_SEQ]])).then_inc(bias_s_in, 16)
                    sp.dma_start(vc[:, :, :], cache_v[0].rearrange("b s g e -> s b (g e)")).then_inc(vc_in, 16)
                    for new, old in ((new_k_sample, cache_k), (new_v_sample, cache_v)):
                        sp.dma_start(new[0][:, 0:WINDOW - DEC_SEQ], old[0][:, DEC_SEQ:WINDOW]).then_inc(outputs_out, 16)
            for n in range(U_WO, U_WO + KT):
                c = n - U_WO
                sp.wait_ge(lo_ready, n - SLOTS + 1)
                for g in range(N_KV):
                    src = w_out[0][g * GQA * HEAD_DIM:(g + 1) * GQA * HEAD_DIM, c * P:(c + 1) * P]
                    sp.dma_start(w_raw[g * HEAD_DIM:(g + 1) * HEAD_DIM, n % SLOTS, 0:GQA, :],
                                 src.rearrange("(k p) n -> p k n", p=HEAD_DIM)).then_inc(weights_in[n % SLOTS], 16)
                sp.dma_start(w_raw[:, n % SLOTS, GQA:KT, :],
                             w_out[0][D_ATTN:, c * P:(c + 1) * P].rearrange("(k p) n -> p k n", p=P)
                             ).then_inc(weights_in[n % SLOTS], 16)
            n_out = 2 + 2 + 2 * DEC_BATCH + 3
            sp.wait_ge(vt_copied, 2)
            kv = slice(0, N_KV * HEAD_DIM)
            sp.dma_start(new_k_prompt[0, 0].rearrange("s g e -> s (g e)"), v_tok[:, 10, kv]).then_inc(outputs_out, 16)
            sp.dma_start(new_v_prompt[0, 0].rearrange("s g e -> s (g e)"), v_tok[:, 11, kv]).then_inc(outputs_out, 16)
            for new, at in ((new_k_sample, 12), (new_v_sample, 9)):
                for b in range(DEC_BATCH):
                    sp.dma_start(new[0, b, WINDOW - DEC_SEQ:].rearrange("t g e -> t (g e)"),
                                 v_tok[b * DEC_SEQ:(b + 1) * DEC_SEQ, at, kv]).then_inc(outputs_out, 16)
            sp.wait_ge(ut_copied, 3)
            for j in range(2):
                sp.dma_start(new_conv_sample[0][:, j, :], u_rows[:, j, :]).then_inc(outputs_out, 16)
            sp.dma_start(new_conv_prompt[0, 0], u_rows[0:2, 2, :]).then_inc(outputs_out, 16)
            sp.wait_ge(outputs_out, 16 * n_out)
            feed_forward(1)
            for t, (half, t0, w) in enumerate(Y_TILES):
                sp.wait_ge(y_rows_act, t + 1)
                sp.wait_ge(y_rows_dve, t + 1)
                first, end = max(t0, N_META), min(t0 + w, PROMPT)
                sp.dma_start(y_prompt[0, first - N_META:end - N_META, :],
                             y_rows[first - t0:end - t0, t, :]).then_inc(outputs_out, 16)
                n_out += 1
                if t0 + w > PROMPT:
                    sp.dma_start(y_sample.rearrange("b t n -> (b t) n"),
                                 y_rows[PROMPT - t0:w, t, :]).then_inc(outputs_out, 16)
                    n_out += 1
            sp.wait_ge(outputs_out, 16 * n_out)


        @block.tensor
        def _(pe):
            def products(out, slot, tiles, rhs_hi, rhs_lo, k0=0, last_k=KT - 1):
                for t in range(tiles):
                    k = k0 + t
                    for w, x in ((w_hi, rhs_hi), (w_hi, rhs_lo), (w_lo, rhs_hi)):
                        mm = nc.tensor.matmul(out[:, 0:HALF], w[:, slot, t, :], x(k),
                                              start=(k == 0 and w is w_hi and x is rhs_hi),
                                              stop=(k == last_k and w is w_lo))
                return mm

            def x_operands(half):
                return (lambda k: x_hi[:, k, cols(half)]), (lambda k: x_lo[:, k, cols(half)])

            def ln_mean(L):
                pe.wait_ge(sum_done, sum_need(L))
                if L >= 1:
                    pe.wait_ge(centered, 4 * L)
                nc.tensor.matmul(aux[0][:, 0:HALF], mean_of[:, :], ln_sum[:, L % 2, :],
                                 start=True, stop=True).then_inc(mean_done, 1)

            def ln_var(L):
                pe.wait_ge(sq_added, 7 * (L + 1))
                if L >= 1:
                    pe.wait_ge(std_done, L)
                nc.tensor.matmul(aux[1][:, 0:HALF], mean_of[:, :], ln_sum[:, L % 2, :],
                                 start=True, stop=True).then_inc(var_done, 1)

            def transpose_rows(L):
                for t, (half, t0, w) in enumerate(Y_TILES):
                    if half != L - 4:
                        continue
                    for b in range(2):
                        bank = aux[2 + b] if t % 2 == 0 else acc[2 + b]
                        if t >= 2:
                            pe.wait_ge((y_rows_dve, y_rows_act)[b], t - 1)
                        for c in range(4 * b, 4 * b + 4):
                            pe.wait_ge(y_biased, 8 * (L - 4) + c + 1)
                            tr = nc.tensor.transpose(bank[0:w, (c % 4) * P:(c % 4 + 1) * P],
                                                     x_res[:, c, t0:t0 + w], ident[:, :])
                        tr.then_inc(y_t, 1)

            def gate_up_group(f, i, first):
                for half in range(2):
                    if first and half == 1 or first and f == 0 and half == 0:
                        pe.wait_ge(x_ready, 8 if f == 0 else 8 + 8 * 4)
                    elif first and half == 0:
                        pe.wait_ge(x_ready, 8 + 8 * 3)
                        pe.wait_ge(r_done, 32)
                    hi, lo = x_operands(half)
                    for u in range(4):
                        n0 = U_GU[f] + u
                        if half == 0:
                            pe.wait_ge(lo_ready, n0 + 4 * i + 1)
                        m0 = 44 * f + 2 * half + u // 2
                        if not (first and half == 0):
                            pe.wait_ge((silu_done, h_done)[u % 2], m0 + 4 * i - 1)
                        products(acc[u], n0 % SLOTS, KT, hi, lo).then_inc(steps_done, 1)
                        if first and half == 0 and f == 1:
                            if u == 0:
                                ln_mean(3)
                            if u == 2:
                                ln_var(3)

            def down_chunk(f, half, c, c2, loop):
                hi, lo = (lambda k: h_hi[:, k, cols(half)]), (lambda k: h_lo[:, k, cols(half)])
                for d in range(4):
                    n0 = U_DN[f] + DN_UNITS * half + d
                    pe.wait_ge(lo_ready, n0 + 4 * c + 1)
                    if d == 0 and (loop or half == 1 or c2 != c):
                        pe.wait_ge(r_done, 32 * f + 8 * half + c - 1)
                    products(acc[c2], n0 % SLOTS, DN_CUT[d + 1] - DN_CUT[d], hi, lo,
                             k0=DN_CUT[d], last_k=FT - 1).then_inc(steps_done, 1)
                    if half == 1 and not loop and c == 0 and d == 1:
                        ln_mean(4 * f)
                    if half == 1 and not loop and c == 1 and d == 0:
                        ln_var(4 * f)

            def feed_forward(f):
                gate_up_group(f, 0, first=True)
                with pe.Fori(1, GU_GROUPS) as i:
                    gate_up_group(f, i, first=False)
                pe.wait_ge(h_ready, 44 * f + 42)
                pe.wait_ge(silu_done, 44 * f + 43)
                pe.wait_ge(h_done, 44 * f + 43)
                for c in range(2):
                    down_chunk(f, 0, c, c, loop=False)
                with pe.Fori(1, KT // 2) as i:
                    for c2 in range(2):
                        down_chunk(f, 0, 2 * i + c2, c2, loop=True)
                pe.wait_ge(h_ready, 44 * f + 44)
                for c in range(2):
                    down_chunk(f, 1, c, c, loop=False)
                if f == 0:
                    with pe.Fori(1, KT // 2) as i:
                        for c2 in range(2):
                            down_chunk(f, 1, 2 * i + c2, c2, loop=True)
                else:
                    with pe.Fori(1, KT // 2 - 1) as i:
                        for c2 in range(2):
                            down_chunk(f, 1, 2 * i + c2, c2, loop=True)
                    transpose_rows(4)
                    for c in range(KT - 2, KT):
                        down_chunk(f, 1, c, c % 2, loop=True)

            pe.wait_ge(consts_in, 16 * N_CONSTS)
            nc.tensor.transpose(aux[0][:, 0:60], param_rows[:, :], ident[0:60, 0:60]).then_inc(params_t, 1)
            nc.tensor.matmul(aux[1][0:N_HEADS, 0:T_W], rel_tab[:, :], hot[:, :],
                             start=True, stop=True).then_inc(params_t, 1)
            for t in range(N_XT):
                pe.wait_ge(x_in[t], 16 * X_DMAS[t])
            for c in range(KT):
                if c >= 2:
                    pe.wait_ge(x_hi_done, c - 1)
                a, b = acc[2 * (c % 2)], acc[2 * (c % 2) + 1]
                for t in range(N_XT):
                    out = a[:, t * XT:(t + 1) * XT] if t < 4 else b[:, 0:XT]
                    tr = nc.tensor.transpose(out, x_rows[:, t, c * P:(c + 1) * P], ident[0:XT, 0:XT])
                tr.then_inc(xt_done, 1)
            pe.wait_ge(memset_done, 2)

            feed_forward(0)

            def wi_step(m):
                u, half = WI_STEPS[m]
                n = U_WI + u
                pe.wait_ge(lo_ready, n + 1)
                before = z_before(m)
                if before is not None:
                    who = z_reader(before)
                    pe.wait_ge(z_act if who == "act" else z_dve, z_count(before, who))
                hi, lo = x_operands(half)
                products(acc[z_bank(m)], n % SLOTS, KT, hi, lo).then_inc(steps_done, 1)

            def cache_transposes():
                pe.wait_ge(kc_in, 32)
                pe.wait_ge(std_done, 2)
                for b in range(DEC_BATCH):
                    nc.tensor.transpose(aux[b // 4][:, (b % 4) * P:(b % 4 + 1) * P], kc_rows[:, b, :], ident[:, :])
                for c in range(CT):
                    tr = nc.tensor.transpose(aux[2][:, c * 16:(c + 1) * 16], st_rows[:, c * P:(c + 1) * P],
                                             ident[0:16, 0:16])
                tr.then_inc(kct_done, 1)

            def v_transposes(part):
                pe.wait_ge(z_act, z_count(Z_KV[part], "act"))
                if part == 0:
                    pe.wait_ge(kct_copied, 1)
                else:
                    pe.wait_ge(vt_copied, 1)
                for i, (slot, src, t0, w) in enumerate(V_TILES[part]):
                    tr = nc.tensor.transpose(aux[2 + i // 4][0:w, (i % 4) * P:(i % 4 + 1) * P],
                                             (k_t if src == "k" else v_t)[:, t0:t0 + w], ident[:, :])
                tr.then_inc(vt_done, 1)

            def scores(a):
                b, g = ITEMS[a]
                if a >= 1:
                    pe.wait_ge(masked, a)
                if b == "s":
                    pe.wait_ge(qd_ready, 1)
                    nc.tensor.matmul(aux[0][:, WINDOW:S_COLS], q_diag[:, g, :], k_t[:, PROMPT:TOK],
                                     start=True, stop=True)
                    for i in range(4):
                        rows = slice(32 * i, 32 * i + 32)
                        mm = nc.tensor.matmul(aux[0][rows, 0:WINDOW], q_diag[:, g, rows], kc_t[:, 4 * g + i, :],
                                              start=True, stop=True)
                else:
                    q0, nq = BLOCKS[b]
                    la = min(WINDOW, q0)
                    if a == 0:
                        pe.wait_ge(z_act, z_count(AB - 1, "act"))
                        pe.wait_ge(kct_copied, 1)
                    head = slice(g * HEAD_DIM, (g + 1) * HEAD_DIM)
                    for h in range(GQA):
                        mm = nc.tensor.matmul(aux[h // 2][0:nq, (h % 2) * 256:(h % 2) * 256 + la + nq],
                                              q_t[head, h, q0:q0 + nq], k_t[head, q0 - la:q0 + nq],
                                              start=True, stop=True)
                mm.then_inc(scores_done, 1)

            def prob_transposes(a):
                b, g = ITEMS[a]
                pe.wait_ge(probs_ready, a + 1)
                pe.wait_ge(pt_copied, 2 * a) if a else pe.wait_ge(vt_copied, 2)
                if b == "s":
                    nc.tensor.transpose(aux[2][:, 0:P], probs[:, a % 3, 0, 0:WINDOW], ident[:, :])
                    tr = nc.tensor.transpose(aux[3][0:SAMPLE, 0:P], probs[:, a % 3, 0, WINDOW:S_COLS], ident[:, :])
                else:
                    q0, nq = BLOCKS[b]
                    la = min(WINDOW, q0)
                    for h in range(GQA):
                        if la:
                            nc.tensor.transpose(aux[2][0:la, h * nq:(h + 1) * nq], probs[0:nq, a % 3, h, 0:la],
                                                ident[0:nq, 0:nq])
                        tr = nc.tensor.transpose(aux[3][0:nq, h * nq:(h + 1) * nq], probs[0:nq, a % 3, h, la:la + nq],
                                                 ident[0:nq, 0:nq])
                tr.then_inc(pt_done, 1)

            def values(a):
                b, g = ITEMS[a]
                pe.wait_ge(pt_copied, 2 * a + 2)
                if a >= 1:
                    pe.wait_ge(att_lo, a)
                else:
                    pe.wait_ge(z_act, z_count(AB - 1, "act"))
                if b == "s":
                    if g == 0:
                        pe.wait_ge(vc_in, 16)
                    nc.tensor.matmul(acc[3][:, 0:P], v_tok[0:SAMPLE, 9, :], p_t[0:SAMPLE, 1, 0:P],
                                     start=True, stop=False)
                    for i in range(4):
                        rows = slice(32 * i, 32 * i + 32)
                        mm = nc.tensor.matmul(acc[3][:, rows], vc[:, 4 * g + i, :], p_t[:, 0, rows],
                                              start=False, stop=i == 3)
                else:
                    q0, nq = BLOCKS[b]
                    la = min(WINDOW, q0)
                    if la:
                        nc.tensor.matmul(acc[3][:, 0:GQA * nq], v_tok[0:la, 2 * b - 1, :], p_t[0:la, 0, 0:GQA * nq],
                                         start=True, stop=False)
                    mm = nc.tensor.matmul(acc[3][:, 0:GQA * nq], v_tok[0:nq, 2 * b, :], p_t[0:nq, 1, 0:GQA * nq],
                                          start=not la, stop=True)
                mm.then_inc(att_done, 1)

            def attention_slot(k):
                if k < len(ITEMS):
                    scores(k)
                if 2 <= k < len(ITEMS) + 2:
                    prob_transposes(k - 2)
                if 3 <= k < len(ITEMS) + 3:
                    values(k - 3)

            pe.wait_ge(x_ready, 8 + 8 * 1)
            pe.wait_ge(r_done, 16)
            for m in range(len(WI_STEPS)):
                if m == WI_GROUPS[0]:
                    pe.wait_ge(x_ready, 8 + 8 * 2)
                wi_step(m)
                if m == 0:
                    ln_mean(1)
                if m == 2:
                    ln_var(1)
                if m == PREP:
                    cache_transposes()
                if m == PREP + 1:
                    v_transposes(0)
                if m == PREP + 3:
                    v_transposes(1)
                if m > AB and (m - AB) % 2 == 1:
                    attention_slot((m - AB) // 2)

            for k, (c, half) in enumerate(WO_ORDER):
                n = U_WO + c
                if half == 0:
                    pe.wait_ge(lo_ready, n + 1)
                if k == 0:
                    pe.wait_ge(gated_lo, 2 * CT)
                    pe.wait_ge(att_lo, ITEMS_H0)
                if k == 4:
                    pe.wait_ge(att_lo, len(ITEMS))
                if wo_before(k) is not None:
                    pe.wait_ge(r_done, 16 + wo_before(k) + 1)
                else:
                    pe.wait_ge(z_dve, z_count(len(WI_STEPS) - 1, "dve"))
                    pe.wait_ge(z_act, z_count(len(WI_STEPS) - 1, "act"))
                products(acc[wo_bank(k)], n % SLOTS, KT,
                         (lambda t: mix_hi[:, t, cols(half)]), (lambda t: mix_lo[:, t, cols(half)])
                         ).then_inc(steps_done, 1)
                if k < 3:
                    attention_slot(len(WI_STEPS[AB:]) // 2 + k)
                if k == 4:
                    pe.wait_ge(pt_copied, 2 * len(ITEMS))
                    for ch in range(CT):
                        for j in range(2):
                            nc.tensor.transpose(aux[2 + j][0:DEC_BATCH, ch * P:(ch + 1) * P],
                                                u_s[:, ch, :, DEC_SEQ + j], ident[:, :])
                        tr = nc.tensor.transpose(aux[1][0:2, ch * P:(ch + 1) * P],
                                                 u_p[:, ch, PROMPT:PROMPT + 2], ident[:, :])
                    tr.then_inc(ut_done, 1)
                if k == 12:
                    ln_mean(2)
                if k == 14:
                    ln_var(2)

            feed_forward(1)
            ln_mean(5)
            ln_var(5)
            transpose_rows(5)


        @block.scalar
        def _(act):
            def weight_hi(n):
                tiles = tiles_of(n)
                act.wait_ge(weights_in[n % SLOTS], ARRIVED[n])
                if n >= SLOTS:
                    act.wait_ge(steps_done, free_after(n - SLOTS))
                nc.scalar.activation(w_hi[:, n % SLOTS, 0:tiles, :], w_raw[:, n % SLOTS, 0:tiles, :],
                                     ACT.Copy).then_inc(hi_ready, 1)

            def gate_up_hi(f, i, u):
                n0 = U_GU[f] + 4 + u
                act.wait_ge(weights_in[n0 % SLOTS], ARRIVED[n0] + 16 * i)
                act.wait_ge(steps_done, free_after(n0 - SLOTS) + 8 * i)
                nc.scalar.activation(w_hi[:, n0 % SLOTS, :, :], w_raw[:, n0 % SLOTS, :, :],
                                     ACT.Copy).then_inc(hi_ready, 1)

            def silu(f, i, half, ab, first=False):
                m0 = 44 * f + 2 * half + ab
                act.wait_ge(steps_done, T_GU[f] + 4 * half + 2 * ab + 1 + 8 * i)
                if m0 >= 2 or not first:
                    act.wait_ge(h_done, m0 - 1 + 4 * i)
                nc.scalar.activation(silu_g[:, ab, :], acc[2 * ab][:, 0:HALF], ACT.Silu).then_inc(silu_done, 1)

            def hidden_hi(f, i, half, ab):
                m0 = 44 * f + 2 * half + ab
                act.wait_ge(h_done, m0 + 1 + 4 * i)
                nc.scalar.activation(h_hi[:, bass.ds(2 * i + ab, 1), cols(half)], h_f32[:, ab:ab + 1, :],
                                     ACT.Copy).then_inc(h_hi_done, 1)

            def gate_up_group(f, i, split, first=False):
                silu(f, i, 0, 0, first)
                hidden_hi(f, i, 0, 0)
                silu(f, i, 0, 1, first)
                hidden_hi(f, i, 0, 1)
                silu(f, i, 1, 0)
                split(0)
                hidden_hi(f, i, 1, 0)
                split(1)
                silu(f, i, 1, 1)
                split(2)
                hidden_hi(f, i, 1, 1)
                split(3)

            def ln_square(L):
                for c in range(KT):
                    act.wait_ge(centered, 4 * L + c // 2 + 1)
                    used = 7 * L + (max(1, c - 2) if c >= 2 else 0)
                    if used:
                        act.wait_ge(sq_added, used)
                    nc.scalar.activation(ln_sq[:, c % 2, :], x_res[:, c, cols(L % 2)], ACT.Square
                                         ).then_inc(squared, 1)

            def ln_std(L):
                act.wait_ge(var_done, L + 1)
                if L >= 1:
                    act.wait_ge(scaled, 8 * L)
                nc.scalar.activation(rstd[:, :], aux[1][:, 0:HALF], ACT.Sqrt, bias=eps[:, :]).then_inc(std_done, 1)

            def ln_hi(L, chunks):
                for c in chunks:
                    act.wait_ge(scaled, 8 * L + c + 1)
                    b = B0 + 8 * (L // 2) + c
                    nc.scalar.activation(x_hi[:, c, cols(L % 2)], x_res[:, c, cols(L % 2)], ACT.Identity,
                                         bias=coef[:, b:b + 1]).then_inc(x_hi_done, 1)

            def ln_out(L, chunks):
                for c in chunks:
                    act.wait_ge(scaled, 8 * L + c + 1)
                    b = B0 + 8 * (L // 2) + c
                    nc.scalar.activation(x_res[:, c, cols(L % 2)], x_res[:, c, cols(L % 2)], ACT.Identity,
                                         bias=coef[:, b:b + 1]).then_inc(y_biased, 1)

            def copy_rows(L):
                for t, (half, t0, w) in enumerate(Y_TILES):
                    if half == L - 4:
                        bank = aux[3] if t % 2 == 0 else acc[3]
                        act.wait_ge(y_t, 2 * t + 2)
                        nc.scalar.activation(y_rows[0:w, t, 512:1024], bank[0:w, :], ACT.Copy).then_inc(y_rows_act, 1)

            def down(f):
                for half in range(2):
                    n0 = U_DN[f] + DN_UNITS * half
                    if half == 0:
                        with act.Fori(0, KT) as c:
                            for d in range(4):
                                n = n0 + 4 + d
                                act.wait_ge(weights_in[n % SLOTS], ARRIVED[n] + 16 * c)
                                act.wait_ge(steps_done, free_after(n - SLOTS) + 4 * c)
                                nc.scalar.activation(w_hi[:, n % SLOTS, 0:tiles_of(n), :],
                                                     w_raw[:, n % SLOTS, 0:tiles_of(n), :], ACT.Copy).then_inc(hi_ready, 1)
                    else:
                        L = 4 * f
                        for c in range(KT):
                            for d in range(4):
                                n = n0 + 4 * (c + 1) + d
                                if n < U_END:
                                    weight_hi(n)
                                if (c, d) == (0, 1):
                                    ln_square(L)
                                if (c, d) == (1, 0):
                                    ln_std(L)
                                if (c, d) in ((1, 1), (2, 1)):
                                    (ln_hi if f == 0 else ln_out)(L, range(4 * (c - 1), 4 * c))
                            if f == 1 and c == KT - 3:
                                copy_rows(4)

            def feed_forward(f):
                gate_up_group(f, 0, lambda u: gate_up_hi(f, 0, u), first=f == 0)
                with act.Fori(1, GU_GROUPS - 1) as i:
                    gate_up_group(f, i, lambda u: gate_up_hi(f, i, u))
                gate_up_group(f, GU_GROUPS - 1, lambda u: weight_hi(U_DN[f] + u))
                down(f)

            act.dma_start(x_rows[0:N_META, 0, :], meta_tokens).then_inc(x_in[0], 16)
            act.dma_start(x_rows[N_META:XT, 0, :], x_prompt[0, 0:XT - N_META, :]).then_inc(x_in[0], 16)
            for t in range(1, N_XT):
                first, end = t * XT - N_META, min((t + 1) * XT - N_META, SEQ)
                act.dma_start(x_rows[0:end - first, t, :], x_prompt[0, first:end, :]).then_inc(x_in[t], 16)
            act.dma_start(x_rows[XT - SAMPLE:XT, N_XT - 1, :],
                          x_sample.rearrange("b t n -> (b t) n")).then_inc(x_in[N_XT - 1], 16)
            for dst, src in ((ident, identity), (hot, one_hot), (mask_sb, mask_row), (rel_tab, rel_bias),
                             (param_rows[0:24, :], ln_g[0].rearrange("j (c p) -> (j c) p", p=P)),
                             (param_rows[24:48, :], ln_b[0].rearrange("j (c p) -> (j c) p", p=P)),
                             (param_rows[48:60, :], conv_w[0].rearrange("j (c p) -> (j c) p", p=P)),
                             (sinks[:, :], bass.AP(tensor=attn_sink.tensor, offset=0, ap=[[0, P], [1, N_HEADS]]))):
                act.dma_start(dst if isinstance(dst, bass.AP) else dst[:, :], src).then_inc(consts_in, 16)
            for b in range(4):
                act.dma_start(sink_row[32 * b:32 * b + 32, :],
                              bass.AP(tensor=attn_sink.tensor, offset=0,
                                      ap=[[1, N_HEADS], [0, DEC_SEQ], [1, 1]])).then_inc(consts_in, 16)
            for u in range(4):
                weight_hi(u)
            for c in range(KT):
                act.wait_ge(x0_res, c + 1)
                a, b = acc[2 * (c % 2)], acc[2 * (c % 2) + 1]
                nc.scalar.activation(x_hi[:, c, 0:4 * XT], a[:, 0:4 * XT], ACT.Copy)
                nc.scalar.activation(x_hi[:, c, 4 * XT:TOK], b[:, 0:XT], ACT.Copy).then_inc(x_hi_done, 1)

            act.wait_ge(bias_out, 16)
            feed_forward(0)

            ln_square(1)
            ln_std(1)
            ln_hi(1, range(KT))

            def evacuate(m):
                u, half = WI_STEPS[m]
                kind, c = WI_ORDER[u]
                act.wait_ge(steps_done, T_WI + m + 1)
                src = acc[z_bank(m)][:, 0:HALF]
                if kind == "cg":
                    if c >= 2:
                        act.wait_ge(z_dve, step_count("h", c - 2, half))
                    dst = cg_sb[:, half, c % 2, :]
                else:
                    dst = {"k": k_t, "v": v_t}[kind][:, cols(half)] if kind != "q" else q_t[:, c, cols(half)]
                nc.scalar.activation(dst, src, ACT.Copy).then_inc(z_act, 1)

            def gate_hi(m):
                u, half = WI_STEPS[m]
                c = WI_ORDER[u][1]
                e = BG_ORDER.index((c, half))
                act.wait_ge(z_dve, z_count(m, "dve"))
                nc.scalar.activation(mix_hi[:, 4 + c, cols(half)], h_f32[:, e % 2, :], ACT.Copy
                                     ).then_inc(gated_hi, 1)

            def copy_probs(a):
                b, g = ITEMS[a]
                act.wait_ge(pt_done, a + 1)
                if a >= 1:
                    act.wait_ge(att_done, a)
                if b == "s":
                    nc.scalar.activation(p_t[:, 0, 0:P], aux[2][:, 0:P], ACT.Copy).then_inc(pt_copied, 1)
                    nc.scalar.activation(p_t[0:SAMPLE, 1, 0:P], aux[3][0:SAMPLE, 0:P], ACT.Copy).then_inc(pt_copied, 1)
                    return
                q0, nq = BLOCKS[b]
                la = min(WINDOW, q0) or nq
                src = aux[2] if q0 else aux[3]
                nc.scalar.activation(p_t[0:la, 0, 0:GQA * nq], src[0:la, 0:GQA * nq], ACT.Copy).then_inc(pt_copied, 1)
                nc.scalar.activation(p_t[0:nq, 1, 0:GQA * nq], aux[3][0:nq, 0:GQA * nq], ACT.Copy).then_inc(pt_copied, 1)

            def attended_hi(a):
                b, g = ITEMS[a]
                act.wait_ge(att_done, a + 1)
                if b == "s":
                    for kv in range(N_KV):
                        rows = slice(kv * HEAD_DIM, (kv + 1) * HEAD_DIM)
                        for h in range(GQA):
                            hi = nc.scalar.activation(sample_cols(mix_hi, rows, h, g), sample_out(rows, kv, h), ACT.Copy)
                else:
                    q0, nq = BLOCKS[b]
                    rows = slice(g * HEAD_DIM, (g + 1) * HEAD_DIM)
                    hi = nc.scalar.activation(mix_hi[rows, 0:GQA, q0:q0 + nq],
                                              acc[3][rows, 0:GQA * nq].rearrange("p (h q) -> p h q", h=GQA), ACT.Copy)
                hi.then_inc(att_hi, 1)

            def exps(a):
                b, g = ITEMS[a]
                act.wait_ge(neg_ready, a + 1)
                rows, heads, span = item_shape(a)
                for h in range(heads):
                    nc.scalar.activation(probs[0:rows, a % 3, h, 0:span], probs[0:rows, a % 3, h, 0:span], ACT.Exp,
                                         bias=neg_max[0:rows, a % 3, h:h + 1], accum_out=row_sum[0:rows, a % 3, h:h + 1])
                for h in range(heads):
                    sk = sink_row[:, :] if b == "s" else sinks[0:rows, 4 * g + h:4 * g + h + 1]
                    e = nc.scalar.activation(sink_exp[0:rows, a % 3, h:h + 1], sk, ACT.Exp,
                                             bias=neg_max[0:rows, a % 3, h:h + 1])
                e.then_inc(exps_done, 1)

            def attention(k, odd):
                if odd:
                    if 2 <= k < len(ITEMS) + 2:
                        copy_probs(k - 2)
                    if 3 <= k < len(ITEMS) + 3:
                        attended_hi(k - 3)
                elif 1 <= k < len(ITEMS) + 1:
                    exps(k - 1)

            def split_after(m):
                for n in range(U_WI + SLOTS, U_WO + SLOTS):
                    if free_after(n - SLOTS) == T_WI + m + 1:
                        weight_hi(n)

            for m in range(len(WI_STEPS)):
                kind = WI_ORDER[WI_STEPS[m][0]][0]
                if m >= AB and (m - AB) % 2 == 0:
                    attention((m - AB) // 2, odd=False)
                if kind == "bg":
                    gate_hi(m)
                elif kind != "h":
                    evacuate(m)
                split_after(m)
                if m == PREP:
                    act.wait_ge(kct_done, 1)
                    for i in range(2):
                        nc.scalar.activation(kc_t[:, 4 * i:4 * i + 4, :],
                                             aux[i][:, :].rearrange("p (b s) -> p b s", b=4), ACT.Copy)
                    nc.scalar.activation(u_s[:, :, :, 0:2], aux[2][:, 0:64].rearrange("p (c b j) -> p c b j", c=CT, b=DEC_BATCH),
                                         ACT.Copy).then_inc(kct_copied, 1)
                if m == PREP + 1:
                    copy_v_tiles(act, 0)
                if m == PREP + 3:
                    copy_v_tiles(act, 1)
                if m > AB and (m - AB) % 2 == 1:
                    attention((m - AB) // 2, odd=True)

            n_slots = len(WI_STEPS[AB:]) // 2
            for k, (c, half) in enumerate(WO_ORDER):
                if k < 3:
                    attention(n_slots + k, odd=False)
                    attention(n_slots + k, odd=True)
                if k == 4:
                    act.wait_ge(ut_done, 1)
                    for j in range(2):
                        nc.scalar.activation(u_rows[:, j, :], aux[2 + j][0:DEC_BATCH, :], ACT.Copy).then_inc(ut_copied, 1)
                    nc.scalar.activation(u_rows[0:2, 2, :], aux[1][0:2, :], ACT.Copy).then_inc(ut_copied, 1)
                if k in (4, 5, 6, 7):
                    weight_hi(U_WO + k)
                if k == 12:
                    weight_hi(U_GU[1])
                    ln_square(2)
                    ln_std(2)
                    ln_hi(2, range(KT))
                    weight_hi(U_GU[1] + 1)
                if k in (14, 15):
                    weight_hi(U_GU[1] + k - 12)
            ln_square(3)
            ln_std(3)
            ln_hi(3, range(KT))
            feed_forward(1)
            ln_square(5)
            ln_std(5)
            ln_out(5, range(KT))
            copy_rows(5)


        @block.vector
        def _(dve):
            def weight_lo(n, i=0):
                tiles = tiles_of(n)
                dve.wait_ge(hi_ready, n + 1 + SLOTS * i)
                nc.vector.tensor_tensor(w_lo[:, n % SLOTS, 0:tiles, :], w_raw[:, n % SLOTS, 0:tiles, :],
                                        w_hi[:, n % SLOTS, 0:tiles, :].bitcast(F32), ALU.subtract).then_inc(lo_ready, 1)

            def hidden(f, i, half, ab, first=False):
                m0 = 44 * f + 2 * half + ab
                dve.wait_ge(silu_done, m0 + 1 + 4 * i)
                dve.wait_ge(steps_done, T_GU[f] + 4 * half + 2 * ab + 2 + 8 * i)
                if m0 >= 2 or not first:
                    dve.wait_ge(h_hi_done, m0 - 1 + 4 * i)
                    dve.wait_ge(h_ready, m0 - 1 + 4 * i)
                nc.vector.scalar_tensor_tensor(h_f32[:, ab, :], silu_g[:, ab, :], 0.5, acc[2 * ab + 1][:, 0:HALF],
                                               ALU.mult, ALU.mult).then_inc(h_done, 1)

            def hidden_lo(f, i, half, ab):
                m0 = 44 * f + 2 * half + ab
                dve.wait_ge(h_hi_done, m0 + 1 + 4 * i)
                at = bass.ds(2 * i + ab, 1)
                nc.vector.tensor_tensor(h_lo[:, at, cols(half)], h_f32[:, ab:ab + 1, :],
                                        h_hi[:, at, cols(half)].bitcast(F32), ALU.subtract).then_inc(h_ready, 1)

            def gate_up_group(f, i, split, first=False):
                hidden(f, i, 0, 0, first)
                hidden_lo(f, i, 0, 0)
                hidden(f, i, 0, 1, first)
                hidden_lo(f, i, 0, 1)
                hidden(f, i, 1, 0)
                split(0)
                hidden_lo(f, i, 1, 0)
                split(1)
                hidden(f, i, 1, 1)
                split(2)
                hidden_lo(f, i, 1, 1)
                split(3)

            def residual(which, half, c, k, bank, step, first):
                dve.wait_ge(steps_done, step)
                x = x_res[:, bass.ds(c, 1), cols(half)]
                a = acc[bank][:, 0:HALF].unsqueeze(1)
                s = ln_sum[:, half:half + 1, :]
                nc.vector.scalar_tensor_tensor(x, x, ALPHA, a, ALU.mult, ALU.add).then_inc(r_done, 1)
                dve.wait_ge(r_done, 16 * which + k + 1)
                if first:
                    if which:
                        dve.wait_ge(var_done, 2 * which - 1 + half)
                    nc.vector.tensor_copy(s, x).then_inc(sum_done, 1)
                else:
                    dve.wait_ge(sum_done, 16 * which + k)
                    nc.vector.tensor_tensor(s, s, x, ALU.add).then_inc(sum_done, 1)

            def ln_center(L):
                dve.wait_ge(mean_done, L + 1)
                for c in range(0, KT, 2):
                    x = x_res[:, c:c + 2, cols(L % 2)]
                    nc.vector.tensor_tensor(x, x, bcast(aux[0][:, 0:HALF], 2), ALU.subtract).then_inc(centered, 1)

            def ln_sum_squares(L):
                s = ln_sum[:, L % 2, :]
                for c in range(1, KT):
                    dve.wait_ge(squared, 8 * L + c + 1)
                    if c >= 2:
                        dve.wait_ge(sq_added, 7 * L + c - 1)
                    nc.vector.tensor_tensor(s, ln_sq[:, 0, :] if c == 1 else s, ln_sq[:, c % 2, :], ALU.add
                                            ).then_inc(sq_added, 1)

            def ln_rstd(L):
                dve.wait_ge(std_done, L + 1)
                nc.vector.reciprocal(rstd[:, :], rstd[:, :]).then_inc(rstd_done, 1)
                dve.wait_ge(rstd_done, L + 1)

            def ln_scale(L, chunks):
                for c in chunks:
                    x = x_res[:, c, cols(L % 2)]
                    g = G0 + 8 * (L // 2) + c
                    nc.vector.scalar_tensor_tensor(x, x, coef[:, g:g + 1], rstd[:, :], ALU.mult, ALU.mult
                                                   ).then_inc(scaled, 1)

            def ln_lo(L, chunks):
                for c in chunks:
                    b = B0 + 8 * (L // 2) + c
                    dve.wait_ge(x_hi_done, 8 + 8 * L + c + 1)
                    nc.vector.scalar_tensor_tensor(x_lo[:, c, cols(L % 2)], x_res[:, c, cols(L % 2)],
                                                   coef[:, b:b + 1], x_hi[:, c, cols(L % 2)].bitcast(F32),
                                                   ALU.add, ALU.subtract).then_inc(x_ready, 1)

            def layer_norm(L):
                ln_center(L)
                ln_sum_squares(L)
                ln_rstd(L)
                ln_scale(L, range(0, 4))
                ln_lo(L, range(0, 2)) if L < 4 else None
                ln_scale(L, range(4, 8))
                ln_lo(L, range(2, 8)) if L < 4 else None

            def copy_rows(L):
                for t, (half, t0, w) in enumerate(Y_TILES):
                    if half == L - 4:
                        bank = aux[2] if t % 2 == 0 else acc[2]
                        dve.wait_ge(y_t, 2 * t + 1)
                        nc.vector.tensor_copy(y_rows[0:w, t, 0:512], bank[0:w, :]).then_inc(y_rows_dve, 1)

            def down(f):
                W = 2 * f
                for half in range(2):
                    n0 = U_DN[f] + DN_UNITS * half
                    if f:
                        dve.wait_ge(res_biased, 16 + 8 * (half + 1))
                    if half == 0:
                        for d in range(4):
                            weight_lo(n0 + 4 + d)
                        residual(W, 0, 0, 0, 0, T_DN[f] + 4, first=True)
                        for d in range(4):
                            weight_lo(n0 + 8 + d)
                        residual(W, 0, 1, 1, 1, T_DN[f] + 8, first=False)
                        with dve.Fori(1, KT // 2) as i:
                            for c2 in range(2):
                                for d in range(4):
                                    weight_lo(n0 + 4 + 4 * c2 + d, 2 * i)
                                residual(W, 0, 2 * i + c2, 2 * i + c2, c2, T_DN[f] + 4 + 4 * c2 + 8 * i, first=False)
                    else:
                        L = 4 * f
                        for c in range(KT):
                            for d in range(4):
                                n = n0 + 4 * (c + 1) + d
                                if n < U_END:
                                    weight_lo(n)
                                if (c, d) == (0, 0):
                                    ln_center(L)
                                if (c, d) == (0, 1):
                                    ln_sum_squares(L)
                                if (c, d) == (1, 0):
                                    ln_rstd(L)
                                if (c, d) in ((1, 1), (2, 1)):
                                    ln_scale(L, range(4 * (c - 1), 4 * c))
                                    if f == 0:
                                        ln_lo(L, range(4 * (c - 1), 4 * c))
                            residual(W, 1, c, 8 + c, c % 2, T_DN[f] + DN_UNITS + 4 * c + 4, first=c == 0)
                            if f == 1 and c == KT - 3:
                                copy_rows(4)

            def feed_forward(f):
                gate_up_group(f, 0, lambda u: weight_lo(U_GU[f] + 4 + u), first=f == 0)
                with dve.Fori(1, GU_GROUPS - 1) as i:
                    gate_up_group(f, i, lambda u: weight_lo(U_GU[f] + 4 + u, i))
                gate_up_group(f, GU_GROUPS - 1, lambda u: weight_lo(U_DN[f] + u))
                down(f)

            nc.vector.memset(mean_of[:, :], 1.0 / D_MODEL).then_inc(memset_done, 1)
            nc.vector.memset(eps[:, :], LN_EPS).then_inc(memset_done, 1)
            dve.wait_ge(params_t, 1)
            nc.vector.tensor_copy(coef[:, 0:60], aux[0][:, 0:60]).then_inc(coef_ready, 1)
            dve.wait_ge(params_t, 2)
            nc.vector.tensor_tensor(bias_row[:, :], mask_sb[:, :], aux[1][0:N_HEADS, 0:T_W], ALU.add
                                    ).then_inc(table_ready, 1)
            for u in range(4):
                weight_lo(u)
            for c in range(KT):
                dve.wait_ge(xt_done, c + 1)
                a, b = acc[2 * (c % 2)], acc[2 * (c % 2) + 1]
                nc.vector.tensor_copy(x_res[:, c, 0:4 * XT], a[:, 0:4 * XT])
                nc.vector.tensor_copy(x_res[:, c, 4 * XT:TOK], b[:, 0:XT]).then_inc(x0_res, 1)
                dve.wait_ge(x_hi_done, c + 1)
                dve.wait_ge(x0_res, c + 1)
                nc.vector.tensor_tensor(x_lo[:, c, :], x_res[:, c, :], x_hi[:, c, :].bitcast(F32), ALU.subtract
                                        ).then_inc(x_ready, 1)

            feed_forward(0)
            layer_norm(1)

            def conv_input(m):
                u, half = WI_STEPS[m]
                c = WI_ORDER[u][1]
                dve.wait_ge(steps_done, T_WI + m + 1)
                cg_step = WI_STEPS.index((WI_ORDER.index(("cg", c)), half))
                dve.wait_ge(z_act, z_count(cg_step, "act"))
                cg = cg_sb[:, half, c % 2, :]
                src = acc[z_bank(m)]
                if half == 0:
                    last = nc.vector.tensor_tensor(u_p[:, c, 2:2 + HALF], cg, src[:, 0:HALF], ALU.mult)
                else:
                    n = PROMPT - HALF
                    nc.vector.tensor_tensor(u_p[:, c, 2 + HALF:2 + PROMPT], cg[:, 0:n], src[:, 0:n], ALU.mult)
                    last = nc.vector.tensor_tensor(
                        u_s[:, c, :, 2:2 + DEC_SEQ], cg[:, n:HALF].rearrange("p (b t) -> p b t", b=DEC_BATCH),
                        src[:, n:HALF].rearrange("p (b t) -> p b t", b=DEC_BATCH), ALU.mult)
                last.then_inc(z_dve, 1)

            def gate(m):
                u, half = WI_STEPS[m]
                c = WI_ORDER[u][1]
                e = BG_ORDER.index((c, half))
                dve.wait_ge(steps_done, T_WI + m + 1)
                dve.wait_ge(taps_added, 2 * CONV_ORDER.index((c, half)) + 2)
                if e >= 2:
                    dve.wait_ge(gated_hi, e - 1)
                    dve.wait_ge(gated_lo, e - 1)
                nc.vector.tensor_tensor(h_f32[:, e % 2, :], conv[:, half, c % 2, :], acc[z_bank(m)][:, 0:HALF], ALU.mult
                                        ).then_inc(z_dve, 1)
                dve.wait_ge(gated_hi, e + 1)
                nc.vector.tensor_tensor(mix_lo[:, 4 + c, cols(half)], h_f32[:, e % 2, :],
                                        mix_hi[:, 4 + c, cols(half)].bitcast(F32), ALU.subtract).then_inc(gated_lo, 1)

            def mask_and_max(a):
                b, g = ITEMS[a]
                rows, heads, span = item_shape(a)
                dve.wait_ge(scores_done, a + 1)
                if a == 0:
                    dve.wait_ge(bias_in, 16)
                    dve.wait_ge(kct_copied, 1)
                    dve.wait_ge(kct_done, 1)
                if a >= 3:
                    dve.wait_ge(pt_done, a - 2)
                if b == "s":
                    if g == 0:
                        dve.wait_ge(bias_s_in, 16 * 16)
                    nc.vector.scalar_tensor_tensor(probs[:, a % 3, 0, 0:span], aux[0][:, 0:span], SCALE,
                                                   bias_s[:, g, :], ALU.mult, ALU.add).then_inc(masked, 1)
                    sk = sink_row[:, :]
                else:
                    q0, nq = BLOCKS[b]
                    first = WINDOW - min(WINDOW, q0)
                    for i in range(2):
                        s = aux[i][0:rows, :].rearrange("p (h s) -> p h s", h=2)[:, :, 0:span]
                        last = nc.vector.scalar_tensor_tensor(
                            probs[0:rows, a % 3, 2 * i:2 * i + 2, 0:span], s, SCALE,
                            bias[0:rows, 4 * g + 2 * i:4 * g + 2 * i + 2, first:first + span], ALU.mult, ALU.add)
                    last.then_inc(masked, 1)
                    sk = sinks[0:rows, 4 * g:4 * g + 4]
                dve.wait_ge(masked, a + 1)
                mx, neg = row_max[0:rows, a % 3, 0:heads], neg_max[0:rows, a % 3, 0:heads]
                nc.vector.tensor_reduce(mx, probs[0:rows, a % 3, 0:heads, 0:span], AX_X, ALU.max).then_inc(max_done, 1)
                dve.wait_ge(max_done, a + 1)
                nc.vector.tensor_tensor(mx, mx, sk, ALU.max).then_inc(max_sink, 1)
                dve.wait_ge(max_sink, a + 1)
                nc.vector.tensor_scalar(neg, mx, -1.0, None, ALU.mult).then_inc(neg_ready, 1)

            def denominators(a):
                rows, heads, span = item_shape(a)
                dve.wait_ge(exps_done, a + 1)
                den, rd = row_sum[0:rows, a % 3, 0:heads], r_den[0:rows, a % 3, 0:heads]
                nc.vector.tensor_tensor(den, den, sink_exp[0:rows, a % 3, 0:heads], ALU.add).then_inc(den_done, 1)
                dve.wait_ge(den_done, a + 1)
                nc.vector.reciprocal(rd, den).then_inc(rden_done, 1)

            def attended_lo(a):
                b, g = ITEMS[a]
                dve.wait_ge(att_hi, a + 1)
                if b == "s":
                    for kv in range(N_KV):
                        rows = slice(kv * HEAD_DIM, (kv + 1) * HEAD_DIM)
                        for h in range(GQA):
                            lo = nc.vector.tensor_tensor(sample_cols(mix_lo, rows, h, g), sample_out(rows, kv, h),
                                                         sample_cols(mix_hi, rows, h, g).bitcast(F32), ALU.subtract)
                else:
                    q0, nq = BLOCKS[b]
                    rows = slice(g * HEAD_DIM, (g + 1) * HEAD_DIM)
                    lo = nc.vector.tensor_tensor(mix_lo[rows, 0:GQA, q0:q0 + nq],
                                                 acc[3][rows, 0:GQA * nq].rearrange("p (h q) -> p h q", h=GQA),
                                                 mix_hi[rows, 0:GQA, q0:q0 + nq].bitcast(F32), ALU.subtract)
                lo.then_inc(att_lo, 1)

            def attention(k, odd):
                if odd:
                    if k < len(ITEMS):
                        mask_and_max(k)
                    if 3 <= k < len(ITEMS) + 3:
                        attended_lo(k - 3)
                elif 1 <= k < len(ITEMS) + 1:
                    denominators(k - 1)

            def split_after(m):
                for n in range(U_WI + SLOTS, U_WO + SLOTS):
                    if free_after(n - SLOTS) == T_WI + m + 1:
                        weight_lo(n)

            dve.wait_ge(steps_done, T_WI)
            nc.vector.memset(bias_s[:, :, WINDOW:S_COLS], MASKED).then_inc(zero_done, 1)
            nc.vector.memset(q_diag[:, :, :], 0.0)
            nc.vector.memset(u_p[:, :, 0:2], 0.0).then_inc(zero_done, 1)
            for m in range(len(WI_STEPS)):
                kind = WI_ORDER[WI_STEPS[m][0]][0]
                if m >= AB and (m - AB) % 2 == 0:
                    attention((m - AB) // 2, odd=False)
                if kind == "h":
                    conv_input(m)
                if kind == "bg":
                    gate(m)
                split_after(m)
                if m == AB - 1:
                    dve.wait_ge(z_act, z_count(AB - 1, "act"))
                    dve.wait_ge(zero_done, 2)
                    for kv in range(N_KV):
                        rows = slice(kv * HEAD_DIM, (kv + 1) * HEAD_DIM)
                        for h in range(GQA):
                            dst = q_diag[rows, :, :].rearrange("p j (b g t) -> p (j b) g t", b=4, t=DEC_SEQ)[:, :, GQA * kv + h]
                            last = nc.vector.tensor_copy(
                                dst, q_t[rows, h, PROMPT:TOK].rearrange("p (b t) -> p b t", t=DEC_SEQ))
                    last.then_inc(qd_ready, 1)
                if m > AB and (m - AB) % 2 == 1:
                    attention((m - AB) // 2, odd=True)

            n_slots = len(WI_STEPS[AB:]) // 2
            dve.wait_ge(res_biased, 16)
            first_of = {0: 0, 1: 4}
            for k, (c, half) in enumerate(WO_ORDER):
                if k < 3:
                    attention(n_slots + k, odd=False)
                    attention(n_slots + k, odd=True)
                if k == 12:
                    weight_lo(U_GU[1])
                    layer_norm(2)
                    weight_lo(U_GU[1] + 1)
                residual(1, half, c, k, wo_bank(k), T_WO + k + 1, first=k == first_of[half])
                if k in (4, 5, 6, 7):
                    weight_lo(U_WO + k)
                if k in (14, 15):
                    weight_lo(U_GU[1] + k - 12)
            layer_norm(3)
            feed_forward(1)
            layer_norm(5)
            copy_rows(5)

        @block.gpsimd
        def _(pool):
            def residual_shift(L):
                for c in range(KT):
                    pool.wait_ge(x_ready, 8 + 8 * L + c + 1)
                    b = B0 + 8 * (L // 2) + c
                    x = x_res[:, c, cols(L % 2)]
                    nc.gpsimd.tensor_scalar(x, x, coef[:, b:b + 1], None, ALU.add).then_inc(res_biased, 1)

            def convolve(e):
                c, half = CONV_ORDER[e]
                pool.wait_ge(z_dve, step_count("h", c, half))
                if e >= 1:
                    pool.wait_ge(taps_added, 2 * e)
                if c >= 2:
                    pool.wait_ge(z_dve, step_count("bg", c - 2, half))
                n = HALF if half == 0 else PROMPT - HALF
                for j in range(3):
                    w = C0 + CT * j + c
                    at = half * HALF + j
                    last = nc.gpsimd.tensor_scalar(taps[:, j, 0:n], u_p[:, c, at:at + n], coef[:, w:w + 1], None, ALU.mult)
                    if half:
                        last = nc.gpsimd.tensor_scalar(
                            taps[:, j, n:HALF].rearrange("p (b t) -> p b t", b=DEC_BATCH),
                            u_s[:, c, :, j:j + DEC_SEQ], coef[:, w:w + 1], None, ALU.mult)
                last.then_inc(taps_done, 1)
                pool.wait_ge(taps_done, e + 1)
                nc.gpsimd.tensor_tensor(taps[:, 0, :], taps[:, 0, :], taps[:, 1, :], ALU.add).then_inc(taps_added, 1)
                pool.wait_ge(taps_added, 2 * e + 1)
                nc.gpsimd.tensor_tensor(conv[:, half, c % 2, :], taps[:, 0, :], taps[:, 2, :], ALU.add
                                        ).then_inc(taps_added, 1)

            def divide(a):
                rows, heads, span = item_shape(a)
                pool.wait_ge(rden_done, a + 1)
                for h in range(heads):
                    p = probs[0:rows, a % 3, h, 0:span]
                    last = nc.gpsimd.tensor_scalar(p, p, r_den[0:rows, a % 3, h:h + 1], None, ALU.mult)
                last.then_inc(probs_ready, 1)

            pool.wait_ge(coef_ready, 1)
            residual_shift(0)
            residual_shift(1)
            for m in range(AB, len(WI_STEPS)):
                u, half = WI_STEPS[m]
                if (m - AB) % 2 == 0 and (m - AB) // 2 >= 1:
                    divide((m - AB) // 2 - 1)
                if WI_ORDER[u][0] == "h":
                    if m == WI_STEPS.index((WI_ORDER.index(("h", 0)), 0)):
                        pool.wait_ge(zero_done, 2)
                        pool.wait_ge(kct_copied, 1)
                    convolve(CONV_ORDER.index((WI_ORDER[u][1], half)))
            divide(len(ITEMS) - 1)
            residual_shift(2)
            residual_shift(3)


_INS = ["x_prompt", "x_sample", "cache_k", "cache_v", "state_conv", "meta_tokens", "rel_bias", "w_in", "conv_w",
        "attn_sink", "w_out", "ffn_w_gate", "ffn_w_up", "ffn_w_down", "ln_g", "ln_b"]
_OUTS = [(1, SEQ, D_MODEL), (DEC_BATCH, DEC_SEQ, D_MODEL), (1, 1, WINDOW, N_KV, HEAD_DIM),
         (1, 1, WINDOW, N_KV, HEAD_DIM), (1, 1, 2, D_CONV), (1, DEC_BATCH, WINDOW, N_KV, HEAD_DIM),
         (1, DEC_BATCH, WINDOW, N_KV, HEAD_DIM), (1, DEC_BATCH, 2, D_CONV)]


def kernel(**inputs):
    import concourse.bacc as bacc
    from concourse.bass_utils import run_bass_kernel_spmd

    nc = bacc.Bacc("TRN2", target_bir_lowering=False, num_devices=1, dynamic_dma_scratch_size=1024)
    one_hot, mask = bias_constants()
    arrays = {name: np.ascontiguousarray(inputs[name]) for name in _INS}
    arrays |= {"identity": np.eye(P, dtype=np.float32), "one_hot": one_hot, "mask_row": mask}
    args = [nc.dram_tensor(f"in_{n}", a.shape, mybir.dt.from_np(a.dtype), kind="ExternalInput").ap()
            for n, a in arrays.items()]
    args += [nc.dram_tensor(f"out_{i}", s, F32, kind="ExternalOutput").ap() for i, s in enumerate(_OUTS)]
    build(nc, *args)
    r = run_bass_kernel_spmd(nc, [{f"in_{n}": a for n, a in arrays.items()}], core_ids=[0])
    return tuple(r.results[0][f"out_{i}"] for i in range(len(_OUTS)))
```

```python
from contextlib import ExitStack

import numpy as np

import concourse.bass as bass
from concourse import mybir
from concourse.alu_op_type import AluOpType as ALU

ACT = mybir.ActivationFunctionType
F32 = mybir.dt.float32
F32R = mybir.dt.float32r
AX_X = mybir.AxisListType.X

P = 128
D_MODEL = 1024
SEQ = 512
N_META = 16
DEC_BATCH = 8
DEC_SEQ = 4
N_HEADS = 8
N_KV = 2
GQA = N_HEADS // N_KV
HEAD_DIM = 64
D_ATTN = N_HEADS * HEAD_DIM
D_CONV = D_MODEL - D_ATTN
D_KV = N_KV * HEAD_DIM
WINDOW = 128
N_BUCKETS = 32
MAX_DISTANCE = 128
D_FF = 2816
ALPHA = float(2.0 ** 0.25)
LN_EPS = 1e-5
SCALE = HEAD_DIM ** -0.5
MASKED = -1.0e30

PROMPT = N_META + SEQ
SAMPLE = DEC_BATCH * DEC_SEQ
TOK = PROMPT + SAMPLE
HALF = TOK // 2
KT = D_MODEL // P
FT = D_FF // P
CT = D_CONV // P
XT = 112
N_XT = TOK // XT
LAST_KEYS = PROMPT - WINDOW

SLOTS = 4
GU_UNITS = 2 * FT
DN_CUT = (0, 6, 12, 17, 22)
DN_UNITS = 4 * KT
WI_ORDER = (("k", 0), ("v", 0), ("q", 0), ("q", 1), ("q", 2), ("q", 3),
            ("cg", 0), ("h", 0), ("cg", 1), ("h", 1), ("bg", 0), ("bg", 1),
            ("cg", 2), ("h", 2), ("cg", 3), ("h", 3), ("bg", 2), ("bg", 3))
WI_GROUPS = (4, 2, 4, 4, 4)
U_GU = (0, GU_UNITS + 2 * DN_UNITS + len(WI_ORDER) + 2 * KT)
U_DN = (U_GU[0] + GU_UNITS, U_GU[1] + GU_UNITS)
U_WI = U_DN[0] + 2 * DN_UNITS
U_WO = U_WI + len(WI_ORDER)
U_END = U_DN[1] + 2 * DN_UNITS
GU_GROUPS = FT // 2
T_GU = (0, 2 * GU_UNITS + 2 * DN_UNITS + 2 * len(WI_ORDER) + 2 * KT)
T_DN = (T_GU[0] + 2 * GU_UNITS, T_GU[1] + 2 * GU_UNITS)
T_WI = T_DN[0] + 2 * DN_UNITS
T_WO = T_WI + 2 * len(WI_ORDER)

COL0 = {"q": 0, "k": D_ATTN, "v": D_ATTN + D_KV, "bg": D_ATTN + 2 * D_KV,
        "cg": D_ATTN + 2 * D_KV + D_CONV, "h": D_ATTN + 2 * D_KV + 2 * D_CONV}

BLOCKS = ((0, 96), (96, 96), (192, 88), (280, 124), (404, 124))
ITEMS = [(b, g) for b in range(len(BLOCKS)) for g in range(N_KV)] + [("s", 0), ("s", 1)]
ITEMS_H0 = 6
QMAX = 124
SPAN = QMAX + WINDOW
S_COLS = WINDOW + SAMPLE
T_W = WINDOW - 1 + SPAN + 1


def wi_steps():
    out, u0 = [], 0
    for size in WI_GROUPS:
        for half in range(2):
            out += [(u0 + u, half) for u in range(size)]
        u0 += size
    return out


WI_STEPS = wi_steps()

Y_TILES = [(0, 0, 112), (0, 112, 112), (0, 224, 56), (1, 280, 56), (1, 336, 112), (1, 448, 112)]
X_DMAS = [2, 1, 1, 1, 2]
X_PARTS = ((0, 1, 2), (3, 4))
N_CONSTS = 2 + 1 + 3 + 1 + 4
V_TILES = ([(0, "v", 0, 96), (1, "v", 0, 96), (2, "v", 96, 96), (3, "v", 64, 128), (4, "v", 192, 88)],
           [(5, "v", 152, 128), (6, "v", 280, 124), (7, "v", 276, 128), (8, "v", 404, 124),
            (9, "v", PROMPT, SAMPLE), (10, "k", LAST_KEYS, P), (11, "v", LAST_KEYS, P),
            (12, "k", PROMPT, SAMPLE)])
PREP = 2 * WI_GROUPS[0] - 1
Z_KV = (1, WI_GROUPS[0] + 1)
CONV_ORDER = [(WI_ORDER[u][1], half) for u, half in WI_STEPS if WI_ORDER[u][0] == "h"]
BG_ORDER = [(WI_ORDER[u][1], half) for u, half in WI_STEPS if WI_ORDER[u][0] == "bg"]


def free_after(n):
    for f in range(2):
        if U_GU[f] <= n < U_GU[f] + GU_UNITS:
            i, u = divmod(n - U_GU[f], 4)
            return T_GU[f] + 8 * i + 4 + u + 1
        if U_DN[f] <= n < U_DN[f] + 2 * DN_UNITS:
            return T_DN[f] + n - U_DN[f] + 1
    if n < U_WO:
        return T_WI + WI_STEPS.index((n - U_WI, 1)) + 1
    return T_WO + n - U_WO + 1


def tiles_of(n):
    for f in range(2):
        if U_DN[f] <= n < U_DN[f] + 2 * DN_UNITS:
            d = (n - U_DN[f]) % 4
            return DN_CUT[d + 1] - DN_CUT[d]
    return KT


def arrived_values():
    total, out = [0] * SLOTS, []
    for n in range(U_END):
        is_q = U_WI <= n < U_WO and WI_ORDER[n - U_WI][0] == "q"
        total[n % SLOTS] += 48 if U_WO <= n < U_GU[1] else 32 if is_q else 16
        out.append(total[n % SLOTS])
    return out


ARRIVED = arrived_values()


def bias_constants():
    d = 2 * WINDOW - 1 - np.arange(T_W)
    valid = (d >= 0) & (d <= WINDOW)
    exact = N_BUCKETS // 2
    df = np.maximum(d, 1).astype(np.float32)
    large = exact + (np.log(df / np.float32(exact)) / np.float32(np.log(MAX_DISTANCE / exact))
                     * np.float32(N_BUCKETS - exact)).astype(np.int32)
    bucket = np.where(d < exact, np.maximum(d, 0), np.minimum(large, N_BUCKETS - 1))
    one_hot = ((np.arange(N_BUCKETS)[:, None] == bucket[None, :]) & valid[None, :]).astype(np.float32)
    mask = np.broadcast_to(np.where(valid, 0.0, MASKED).astype(np.float32), (N_HEADS, T_W))
    return one_hot, np.ascontiguousarray(mask)


def build(nc, x_prompt, x_sample, cache_k, cache_v, state_conv, meta_tokens, rel_bias, w_in, conv_w,
          attn_sink, w_out, w_gate, w_up, w_down, ln_g, ln_b, identity, one_hot, mask_row,
          y_prompt, y_sample, new_k_prompt, new_v_prompt, new_conv_prompt,
          new_k_sample, new_v_sample, new_conv_sample):
    ctx = ExitStack()
    with ctx:
        def sb(name, shape, dt=F32, stack=ctx):
            return stack.enter_context(nc.sbuf_tensor(name, shape, dt))

        def sem(name):
            return ctx.enter_context(nc.semaphore(name))

        x_res = sb("x_res", [P, KT, TOK])
        w_raw = sb("w_raw", [P, SLOTS, KT, P])
        w_hi = sb("w_hi", [P, SLOTS, KT, P], F32R)
        w_lo = sb("w_lo", [P, SLOTS, KT, P], F32R)
        ident = sb("ident", [P, P])
        mean_of = sb("mean_of", [P, P])
        coef = sb("coef", [P, 64])
        sinks = sb("sinks", [P, N_HEADS])
        sink_row = sb("sink_row", [P, 1])
        eps = sb("eps", [P, 1])
        ln_sum = sb("ln_sum", [P, 2, HALF])
        ln_sq = sb("ln_sq", [P, 2, HALF])
        rstd = sb("rstd", [P, HALF])
        warm = sb("warm", [P, 8])
        silu_g = sb("silu_g", [P, 2, HALF])
        h_f32 = sb("h_f32", [P, 2, HALF])
        ffn = ExitStack()
        x_hi = sb("x_hi", [P, KT, TOK], F32R, ffn)
        x_lo = sb("x_lo", [P, KT, TOK], F32R, ffn)
        h_hi = sb("h_hi", [P, FT, TOK], F32R, ffn)
        h_lo = sb("h_lo", [P, FT, TOK], F32R, ffn)
        ffn.close()
        late = ExitStack()
        y_rows = sb("y_rows", [XT, 6, D_MODEL], F32, late)
        sb("pad_to_h", [P, 2 * KT * TOK - 6 * D_MODEL], F32, late)
        early = ExitStack()
        x_rows = sb("x_rows", [XT, N_XT, D_MODEL], F32, early)
        sb("pad_to_last_h", [P, (FT - 2) * TOK - N_XT * D_MODEL], F32, early)
        param_rows = sb("param_rows", [60, P], F32, early)
        rel_tab = sb("rel_tab", [N_BUCKETS, N_HEADS], F32, early)
        hot = sb("hot", [N_BUCKETS, T_W], F32, early)
        bias_row = sb("bias_row", [N_HEADS, T_W], F32, early)
        early.close()
        mix_hi = sb("mix_hi", [P, KT, TOK], F32R, late)
        mix_lo = sb("mix_lo", [P, KT, TOK], F32R, late)
        q_t = sb("q_t", [P, GQA, TOK], F32, late)
        k_t = sb("k_t", [P, TOK], F32, late)
        v_t = sb("v_t", [P, TOK], F32, late)
        bias = sb("bias", [P, N_HEADS, SPAN], F32, late)
        bias_s = sb("bias_s", [P, 2, S_COLS], F32, late)
        u_p = sb("u_p", [P, CT, PROMPT + 2], F32, late)
        u_s = sb("u_s", [P, CT, DEC_BATCH, DEC_SEQ + 2], F32, late)
        v_tok = sb("v_tok", [P, 13, P], F32, late)
        kc_t = sb("kc_t", [P, DEC_BATCH, P], F32, late)
        vc = sb("vc", [P, DEC_BATCH, P], F32, late)
        q_diag = sb("q_diag", [P, 2, P], F32, late)
        p_t = sb("p_t", [P, 2, GQA * QMAX], F32, late)
        ut = ExitStack()
        u_rows = sb("u_rows", [DEC_BATCH, 3, D_CONV], F32, ut)
        ut.close()
        taps = sb("taps", [P, 3, HALF], F32, late)
        conv = sb("conv", [P, 2, 2, HALF], F32, late)
        cg_sb = sb("cg_sb", [P, 2, 2, HALF], F32, late)
        row_max = sb("row_max", [P, 3, GQA], F32, late)
        neg_max = sb("neg_max", [P, 3, GQA], F32, late)
        row_sum = sb("row_sum", [P, 3, GQA], F32, late)
        sink_exp = sb("sink_exp", [P, 3, GQA], F32, late)
        r_den = sb("r_den", [P, 3, GQA], F32, late)
        kc = ExitStack()
        kc_rows = sb("kc_rows", [P, DEC_BATCH, P], F32, kc)
        st_rows = sb("st_rows", [DEC_BATCH * 2, D_CONV], F32, kc)
        kc.close()
        probs = sb("probs", [P, 3, GQA, SPAN], F32, late)
        late.close()

        acc = [ctx.enter_context(nc.psum_tensor(f"acc{i}", [P, 512], F32)) for i in range(4)]
        aux = [ctx.enter_context(nc.psum_tensor(f"aux{i}", [P, 512], F32)) for i in range(4)]
        bias_dram = nc.dram_tensor("bias_dram", (N_HEADS, QMAX, T_W), F32, kind="Internal").ap()

        weights_in = [sem(f"weights_in{i}") for i in range(SLOTS)]
        x_in = [sem(f"x_in{i}") for i in range(N_XT)]
        consts_in = sem("consts_in")
        bias_out = sem("bias_out")
        bias_in = sem("bias_in")
        bias_s_in = sem("bias_s_in")
        kc_in = sem("kc_in")
        vc_in = sem("vc_in")
        outputs_out = sem("outputs_out")
        hi_ready = sem("hi_ready")
        lo_ready = sem("lo_ready")
        steps_done = sem("steps_done")
        memset_done = sem("memset_done")
        params_t = sem("params_t")
        coef_ready = sem("coef_ready")
        table_ready = sem("table_ready")
        xt_done = sem("xt_done")
        ident_in = sem("ident_in")
        x0_dve = sem("x0_dve")
        x0_act = sem("x0_act")
        x_hi_done = sem("x_hi_done")
        x_ready = sem("x_ready")
        res_biased = sem("res_biased")
        silu_done = sem("silu_done")
        h_done = sem("h_done")
        h_hi_done = sem("h_hi_done")
        h_ready = sem("h_ready")
        r_done = sem("r_done")
        sum_done = sem("sum_done")
        mean_done = sem("mean_done")
        centered = sem("centered")
        squared = sem("squared")
        sq_pool = sem("sq_pool")
        sq_dve = sem("sq_dve")
        var_done = sem("var_done")
        std_done = sem("std_done")
        rstd_done = sem("rstd_done")
        scaled = sem("scaled")
        y_biased = sem("y_biased")
        y_t = [sem(f"y_t{b}") for b in range(2)]
        y_rows_act = sem("y_rows_act")
        y_rows_dve = sem("y_rows_dve")
        zero_done = sem("zero_done")
        z_act = sem("z_act")
        z_dve = sem("z_dve")
        kct_done = sem("kct_done")
        kct_copied = sem("kct_copied")
        vt_done = sem("vt_done")
        vt_copied = sem("vt_copied")
        qd_ready = sem("qd_ready")
        taps_done = sem("taps_done")
        taps_added = sem("taps_added")
        gated_hi = sem("gated_hi")
        gated_lo = sem("gated_lo")
        ut_done = sem("ut_done")
        ut_copied = sem("ut_copied")
        scores_done = sem("scores_done")
        masked = sem("masked")
        max_done = sem("max_done")
        max_sink = sem("max_sink")
        neg_ready = sem("neg_ready")
        exps_done = sem("exps_done")
        den_done = sem("den_done")
        rden_done = sem("rden_done")
        probs_ready = sem("probs_ready")
        pt_done = sem("pt_done")
        pt_copied = sem("pt_copied")
        att_done = sem("att_done")
        att_hi = sem("att_hi")
        att_lo = sem("att_lo")

        def cols(half):
            return slice(half * HALF, (half + 1) * HALF)

        def bcast(ap, n):
            return ap.unsqueeze(1).to_broadcast([P, n, HALF])

        G0, B0, C0 = 0, 24, 48

        def z_reader(m):
            return "act" if WI_ORDER[WI_STEPS[m][0]][0] in ("k", "v", "q", "cg") else "dve"

        def z_count(m, who):
            return sum(z_reader(i) == who for i in range(m + 1))

        def step_count(kind, c, half):
            return z_count(WI_STEPS.index((WI_ORDER.index((kind, c)), half)), "dve")

        AB = 2 * (WI_GROUPS[0] + WI_GROUPS[1])

        def z_bank(m):
            return m % 4 if m < AB else (m - AB) % 3

        def z_before(m):
            for i in range(m - 1, -1, -1):
                if z_bank(i) == z_bank(m):
                    return i
            return None

        ATT_SLOTS = len(ITEMS) + 3
        WO_STEPS = 2 * KT
        LN_PIECES = {(1, 1): range(0, 2), (1, 2): range(2, 4), (1, 3): range(4, 6), (2, 0): range(6, 8)}
        WO_PIECES = {10: range(0, 2), 11: range(2, 4), 12: range(4, 6), 13: range(6, 8)}
        POOL_SUMS = (2, 3)
        L0, R0 = 7, 8

        def y_bank(t, b):
            return {0: aux[2 + b], 1: acc[2 + b], 2: aux[2 + b] if t < 3 else acc[b]}[t % 3]

        def y_again(t):
            return t in (2, 3, 4)

        def x_bank(part, c):
            return (acc + aux)[c] if part == 0 else aux[c % 4]

        def x_cols(part):
            return slice(X_PARTS[part][0] * XT, (X_PARTS[part][-1] + 1) * XT)

        def squares_of(c):
            return (ln_sq[:, c % 2, :] if c < 4 else silu_g[:, c - 4, :] if c < 6 else h_f32[:, c - 6, :])

        def copy_v_tiles(eng, part):
            eng.wait_ge(vt_done, part + 1)
            for i, (slot, src, t0, w) in enumerate(V_TILES[part]):
                last = nc.scalar.activation(v_tok[0:w, slot, :], aux[2 + i // 4][0:w, (i % 4) * P:(i % 4 + 1) * P], ACT.Copy)
            last.then_inc(vt_copied, 1)

        def item_shape(a):
            b, g = ITEMS[a]
            if b == "s":
                return P, 1, S_COLS
            return BLOCKS[b][1], GQA, min(WINDOW, BLOCKS[b][0]) + BLOCKS[b][1]

        def sample_cols(t, rows, h, j):
            at = PROMPT + 16 * j
            return t[rows, h, at:at + 16].rearrange("p (b t) -> p b t", b=4)

        def sample_out(rows, kv, h):
            return acc[3][rows, 0:P].rearrange("p (b g t) -> p b g t", b=4, t=DEC_SEQ)[:, :, GQA * kv + h]

        block = ctx.enter_context(nc.Block())

        @block.sync
        def _(sp):
            def gate_up(f, i, u, wait):
                n0 = U_GU[f] + u
                w = (w_gate, w_up)[u % 2][0, f].rearrange("(k p) n -> p k n", p=P)
                if wait:
                    sp.wait_ge(lo_ready, n0 + 4 * i - SLOTS + 1)
                sp.dma_start(w_raw[:, n0 % SLOTS, :, :],
                             w[:, :, bass.ds(2 * P * i + (u // 2) * P, P)]).then_inc(weights_in[n0 % SLOTS], 16)

            def down(f, half, c, d):
                n0 = U_DN[f] + DN_UNITS * half + d
                w = w_down[0, f].rearrange("(k p) n -> p k n", p=P)
                sp.wait_ge(lo_ready, n0 + 4 * c - SLOTS + 1)
                sp.dma_start(w_raw[:, n0 % SLOTS, 0:DN_CUT[d + 1] - DN_CUT[d], :],
                             w[:, DN_CUT[d]:DN_CUT[d + 1], bass.ds(P * c, P)]).then_inc(weights_in[n0 % SLOTS], 16)

            def load_constants():
                for dst, src in ((hot, one_hot), (bias_row, mask_row), (rel_tab, rel_bias),
                                 (param_rows[0:24, :], ln_g[0].rearrange("j (c p) -> (j c) p", p=P)),
                                 (param_rows[24:48, :], ln_b[0].rearrange("j (c p) -> (j c) p", p=P)),
                                 (param_rows[48:60, :], conv_w[0].rearrange("j (c p) -> (j c) p", p=P)),
                                 (sinks[:, :], bass.AP(tensor=attn_sink.tensor, offset=0, ap=[[0, P], [1, N_HEADS]]))):
                    sp.dma_start(dst if isinstance(dst, bass.AP) else dst[:, :], src).then_inc(consts_in, 16)
                for b in range(4):
                    sp.dma_start(sink_row[32 * b:32 * b + 32, :],
                                  bass.AP(tensor=attn_sink.tensor, offset=0,
                                          ap=[[1, N_HEADS], [0, DEC_SEQ], [1, 1]])).then_inc(consts_in, 16)

            def load_tokens(part):
                for t in X_PARTS[part]:
                    first, end = max(t * XT - N_META, 0), min((t + 1) * XT - N_META, SEQ)
                    at = N_META if t == 0 else 0
                    sp.dma_start(x_rows[at:at + end - first, t, :], x_prompt[0, first:end, :]).then_inc(x_in[t], 16)
                    if t == 0:
                        sp.dma_start(x_rows[0:N_META, 0, :], meta_tokens).then_inc(x_in[t], 16)
                    if t == N_XT - 1:
                        sp.dma_start(x_rows[XT - SAMPLE:XT, t, :],
                                     x_sample.rearrange("b t n -> (b t) n")).then_inc(x_in[t], 16)

            def feed_forward(f):
                if f == 0:
                    load_tokens(0)
                for u in range(4):
                    gate_up(f, 0, u, wait=f > 0)
                if f == 0:
                    load_tokens(1)
                    for u in range(4):
                        gate_up(f, 1, u, wait=True)
                    load_constants()
                    sp.wait_ge(table_ready, 1)
                    sp.dma_start(bias_dram, bias_row[:, :].unsqueeze(1).to_broadcast([N_HEADS, QMAX, T_W])
                                 ).then_inc(bias_out, 16)
                with sp.Fori(2 if f == 0 else 1, GU_GROUPS) as i:
                    for u in range(4):
                        gate_up(f, i, u, wait=True)
                for half in range(2):
                    with sp.Fori(0, KT) as c:
                        for d in range(4):
                            down(f, half, c, d)

            feed_forward(0)
            w_in_k = w_in[0].rearrange("(k p) n -> p k n", p=P)
            for n, (kind, c) in enumerate(WI_ORDER):
                n += U_WI
                sp.wait_ge(lo_ready, n - SLOTS + 1)
                if kind == "q":
                    for g in range(N_KV):
                        at = (GQA * g + c) * HEAD_DIM
                        sp.dma_start(w_raw[:, n % SLOTS, :, g * HEAD_DIM:(g + 1) * HEAD_DIM],
                                     w_in_k[:, :, at:at + HEAD_DIM]).then_inc(weights_in[n % SLOTS], 16)
                else:
                    at = COL0[kind] + c * P
                    sp.dma_start(w_raw[:, n % SLOTS, :, :], w_in_k[:, :, at:at + P]).then_inc(weights_in[n % SLOTS], 16)
                if n == U_WI + 7:
                    sp.wait_ge(steps_done, T_WI)
                    sp.dma_start(kc_rows[:, :, :], cache_k[0].rearrange("b s g e -> s b (g e)")).then_inc(kc_in, 16)
                    sp.dma_start(st_rows[:, :], state_conv[0].rearrange("b j n -> (b j) n")).then_inc(kc_in, 16)
                    sp.wait_ge(bias_out, 16)
                    sp.dma_start(bias[0:QMAX, :, :],
                                 bass.AP(tensor=bias_dram.tensor, offset=WINDOW - 1,
                                         ap=[[T_W - 1, QMAX], [QMAX * T_W, N_HEADS], [1, SPAN]])).then_inc(bias_in, 16)
                    for b in range(4):
                        rows = slice(32 * b, 32 * b + 32)
                        for j in range(2):
                            sp.dma_start(bias_s[rows, j, 0:WINDOW],
                                         bass.AP(tensor=bias_dram.tensor, offset=WINDOW - 1,
                                                 ap=[[QMAX * T_W, N_HEADS], [T_W - 1, DEC_SEQ], [1, WINDOW]])).then_inc(bias_s_in, 16)
                    sp.wait_ge(zero_done, 2)
                    for b in range(4):
                        rows = slice(32 * b, 32 * b + 32)
                        for j in range(2):
                            at = WINDOW + (4 * j + b) * DEC_SEQ
                            sp.dma_start(bias_s[rows, j, at:at + DEC_SEQ],
                                         bass.AP(tensor=bias_dram.tensor, offset=2 * WINDOW - 1,
                                                 ap=[[QMAX * T_W, N_HEADS], [T_W - 1, DEC_SEQ], [1, DEC_SEQ]])).then_inc(bias_s_in, 16)
                    sp.dma_start(vc[:, :, :], cache_v[0].rearrange("b s g e -> s b (g e)")).then_inc(vc_in, 16)
                    for new, old in ((new_k_sample, cache_k), (new_v_sample, cache_v)):
                        sp.dma_start(new[0][:, 0:WINDOW - DEC_SEQ], old[0][:, DEC_SEQ:WINDOW]).then_inc(outputs_out, 16)
            for n in range(U_WO, U_GU[1]):
                c = (n - U_WO) % KT
                sp.wait_ge(lo_ready, n - SLOTS + 1)
                for g in range(N_KV):
                    src = w_out[0][g * GQA * HEAD_DIM:(g + 1) * GQA * HEAD_DIM, c * P:(c + 1) * P]
                    sp.dma_start(w_raw[g * HEAD_DIM:(g + 1) * HEAD_DIM, n % SLOTS, 0:GQA, :],
                                 src.rearrange("(k p) n -> p k n", p=HEAD_DIM)).then_inc(weights_in[n % SLOTS], 16)
                sp.dma_start(w_raw[:, n % SLOTS, GQA:KT, :],
                             w_out[0][D_ATTN:, c * P:(c + 1) * P].rearrange("(k p) n -> p k n", p=P)
                             ).then_inc(weights_in[n % SLOTS], 16)
            n_out = 2 + 2 + 2 * DEC_BATCH + 3
            sp.wait_ge(vt_copied, 2)
            kv = slice(0, N_KV * HEAD_DIM)
            sp.dma_start(new_k_prompt[0, 0].rearrange("s g e -> s (g e)"), v_tok[:, 10, kv]).then_inc(outputs_out, 16)
            sp.dma_start(new_v_prompt[0, 0].rearrange("s g e -> s (g e)"), v_tok[:, 11, kv]).then_inc(outputs_out, 16)
            for new, at in ((new_k_sample, 12), (new_v_sample, 9)):
                for b in range(DEC_BATCH):
                    sp.dma_start(new[0, b, WINDOW - DEC_SEQ:].rearrange("t g e -> t (g e)"),
                                 v_tok[b * DEC_SEQ:(b + 1) * DEC_SEQ, at, kv]).then_inc(outputs_out, 16)
            sp.wait_ge(ut_copied, 3)
            for j in range(2):
                sp.dma_start(new_conv_sample[0][:, j, :], u_rows[:, j, :]).then_inc(outputs_out, 16)
            sp.dma_start(new_conv_prompt[0, 0], u_rows[0:2, 2, :]).then_inc(outputs_out, 16)
            sp.wait_ge(outputs_out, 16 * n_out)
            feed_forward(1)
            for half in range(2):
                tiles = range(3 * half, 3 * half + 3)
                for t, b in [(t, b) for t in tiles for b in range(2)] if half == 0 else [(t, b) for b in range(2) for t in tiles]:
                    _, t0, w = Y_TILES[t]
                    feats = slice(b * D_MODEL // 2, (b + 1) * D_MODEL // 2)
                    sp.wait_ge((y_rows_dve, y_rows_act)[b], t + 1)
                    first, end = max(t0, N_META), min(t0 + w, PROMPT)
                    sp.dma_start(y_prompt[0, first - N_META:end - N_META, feats],
                                 y_rows[first - t0:end - t0, t, feats]).then_inc(outputs_out, 16)
                    n_out += 1
                    if t0 + w > PROMPT:
                        sp.dma_start(y_sample.rearrange("b t n -> (b t) n")[:, feats],
                                     y_rows[PROMPT - t0:w, t, feats]).then_inc(outputs_out, 16)
                        n_out += 1
            sp.wait_ge(outputs_out, 16 * n_out)


        @block.tensor
        def _(pe):
            def products(out, slot, ks, rhs_hi, rhs_lo, t0=0, ends=(0, KT - 1)):
                for t, k in enumerate(ks, t0):
                    for w, x in ((w_hi, rhs_hi), (w_hi, rhs_lo), (w_lo, rhs_hi)):
                        mm = nc.tensor.matmul(out[:, 0:HALF], w[:, slot, t, :], x(k),
                                              start=(k == ends[0] and w is w_hi and x is rhs_hi),
                                              stop=(k == ends[1] and w is w_lo))
                return mm

            def x_operands(half):
                return (lambda k: x_hi[:, k, cols(half)]), (lambda k: x_lo[:, k, cols(half)])

            def ln_mean(L):
                half = L % 2
                pe.wait_ge(sum_done, L0 * (L + 1))
                pe.wait_ge(r_done, R0 * (L + 1))
                if L >= 1:
                    pe.wait_ge(centered, KT * L)
                nc.tensor.matmul(aux[0][:, 0:HALF], mean_of[:, :], ln_sum[:, half, :], start=True, stop=False)
                nc.tensor.matmul(aux[0][:, 0:HALF], mean_of[:, :], x_res[:, KT - 1, cols(half)],
                                 start=False, stop=True).then_inc(mean_done, 1)

            def ln_var(L):
                pe.wait_ge(sq_pool, 3 * (L + 1))
                pe.wait_ge(sq_dve, 3 * (L + 1))
                if L >= 1:
                    pe.wait_ge(std_done, L)
                nc.tensor.matmul(aux[1][:, 0:HALF], mean_of[:, :], ln_sum[:, L % 2, :], start=True, stop=False)
                nc.tensor.matmul(aux[1][:, 0:HALF], mean_of[:, :], squares_of(4),
                                 start=False, stop=True).then_inc(var_done, 1)

            def transpose_rows(L, order):
                for t, b in order:
                    if y_again(t):
                        pe.wait_ge((y_rows_dve, y_rows_act)[b], t - 1)
                    _, t0, w = Y_TILES[t]
                    for c in range(4 * b, 4 * b + 4):
                        pe.wait_ge(y_biased, KT * (L - 4) + c + 1)
                        tr = nc.tensor.transpose(y_bank(t, b)[0:w, (c % 4) * P:(c % 4 + 1) * P],
                                                 x_res[:, c, t0:t0 + w], ident[:, :])
                    tr.then_inc(y_t[b], 1)

            def unit_pair(n, accs, half, x0, run=1, chunks=range(KT)):
                hi, lo = x_operands(half)
                for k0 in chunks[::run]:
                    for u in range(2):
                        if k0 == 0:
                            pe.wait_ge(lo_ready, n + u + 1)
                        for k in range(k0, k0 + run):
                            pe.wait_ge(x_ready, x0 + k + 1)
                            mm = products(accs[u], (n + u) % SLOTS, range(k, k + 1), hi, lo, t0=k)
                        if k == KT - 1:
                            mm.then_inc(steps_done, 1)

            def parameters():
                pe.wait_ge(consts_in, 16 * N_CONSTS)
                pe.wait_ge(x0_dve, KT)
                pe.wait_ge(x0_act, KT)
                nc.tensor.transpose(aux[0][:, 0:60], param_rows[:, :], ident[0:60, 0:60]).then_inc(params_t, 1)
                nc.tensor.matmul(aux[1][0:N_HEADS, 0:T_W], rel_tab[:, :], hot[:, :],
                                 start=True, stop=True).then_inc(params_t, 1)

            def gate_up_first(f):
                if f == 0:
                    unit_pair(0, acc[0:2], 0, 0, run=4)
                    tokens(1, range(0, 4))
                    unit_pair(2, acc[2:4], 0, 0, run=4, chunks=range(0, 4))
                    tokens(1, range(4, KT))
                    unit_pair(2, acc[2:4], 0, 0, run=4, chunks=range(4, KT))
                else:
                    for v in range(4):
                        n = U_GU[f] + v
                        pe.wait_ge(lo_ready, n + 1)
                        for k in range(KT):
                            if v == 0:
                                pe.wait_ge(x_ready, 4 * KT + k + 1)
                            mm = products(acc[v], n % SLOTS, range(k, k + 1), *x_operands(0), t0=k)
                            if (v, k) == (0, 1):
                                ln_mean(3)
                            if (v, k) == (2, 1):
                                ln_var(3)
                        mm.then_inc(steps_done, 1)
                for u in (0, 2):
                    pe.wait_ge(silu_done, 44 * f + u // 2 + 1)
                    pe.wait_ge(h_done, 44 * f + u // 2 + 1)
                    unit_pair(U_GU[f] + u, acc[u:u + 2], 1, KT if f == 0 else 2 * KT + KT * 3)

            def gate_up_group(f, i):
                for half in range(2):
                    hi, lo = x_operands(half)
                    for u in range(4):
                        n0 = U_GU[f] + u
                        if half == 0:
                            pe.wait_ge(lo_ready, n0 + 4 * i + 1)
                        m0 = 44 * f + 2 * half + u // 2
                        pe.wait_ge((silu_done, h_done)[u % 2], m0 + 4 * i - 1)
                        products(acc[u], n0 % SLOTS, range(KT), hi, lo).then_inc(steps_done, 1)

            def down_chunk(f, half, c, c2, loop):
                hi, lo = (lambda k: h_hi[:, k, cols(half)]), (lambda k: h_lo[:, k, cols(half)])
                for d in range(4):
                    n0 = U_DN[f] + DN_UNITS * half + d
                    pe.wait_ge(lo_ready, n0 + 4 * c + 1)
                    if d == 0 and (loop or half == 1 or c2 != c):
                        pe.wait_ge(r_done, 32 * f + 8 * half + c - 1)
                    products(acc[c2], n0 % SLOTS, range(DN_CUT[d], DN_CUT[d + 1]), hi, lo,
                             ends=(0, FT - 1)).then_inc(steps_done, 1)
                    if half == 1 and not loop and c == 0 and d == 0:
                        ln_mean(4 * f)
                    if half == 1 and not loop and c == 1 and d == 0:
                        ln_var(4 * f)

            def feed_forward(f):
                gate_up_first(f)
                if f == 0:
                    parameters()
                with pe.Fori(1, GU_GROUPS) as i:
                    gate_up_group(f, i)
                pe.wait_ge(h_ready, 44 * f + 42)
                pe.wait_ge(silu_done, 44 * f + 43)
                pe.wait_ge(h_done, 44 * f + 43)
                for c in range(2):
                    down_chunk(f, 0, c, c, loop=False)
                with pe.Fori(1, KT // 2) as i:
                    for c2 in range(2):
                        down_chunk(f, 0, 2 * i + c2, c2, loop=True)
                pe.wait_ge(h_ready, 44 * f + 44)
                for c in range(2):
                    down_chunk(f, 1, c, c, loop=False)
                if f == 0:
                    with pe.Fori(1, KT // 2) as i:
                        for c2 in range(2):
                            down_chunk(f, 1, 2 * i + c2, c2, loop=True)
                else:
                    with pe.Fori(1, KT // 2 - 1) as i:
                        for c2 in range(2):
                            down_chunk(f, 1, 2 * i + c2, c2, loop=True)
                    transpose_rows(4, [(t, b) for t in range(3) for b in range(2)])
                    for c in range(KT - 2, KT):
                        down_chunk(f, 1, c, c % 2, loop=True)

            def tokens(part, chunks):
                for i, t in enumerate(X_PARTS[part]):
                    pe.wait_ge(x_in[t], 16 * X_DMAS[t])
                    for c in chunks:
                        if part and i == 0:
                            pe.wait_ge((x0_dve, x0_act)[c % 2], (KT + c) // 2 - 1)
                        tr = nc.tensor.transpose(x_bank(part, c)[:, i * XT:(i + 1) * XT], x_rows[:, t, c * P:(c + 1) * P],
                                                 ident[0:XT, 0:XT])
                        if t == X_PARTS[part][-1]:
                            tr.then_inc(xt_done, 1)

            pe.wait_ge(ident_in, 16)
            tokens(0, range(KT))
            pe.wait_ge(memset_done, 2)
            feed_forward(0)

            def wi_step(m):
                u, half = WI_STEPS[m]
                n = U_WI + u
                pe.wait_ge(lo_ready, n + 1)
                before = z_before(m)
                if before is not None:
                    who = z_reader(before)
                    pe.wait_ge(z_act if who == "act" else z_dve, z_count(before, who))
                hi, lo = x_operands(half)
                products(acc[z_bank(m)], n % SLOTS, range(0, 2), hi, lo)
                if m == 0:
                    ln_mean(1)
                if m == 2:
                    ln_var(1)
                products(acc[z_bank(m)], n % SLOTS, range(2, KT), hi, lo, t0=2).then_inc(steps_done, 1)

            def cache_transposes():
                pe.wait_ge(kc_in, 32)
                pe.wait_ge(std_done, 2)
                pe.wait_ge(centered, 2 * KT)
                for b in range(DEC_BATCH):
                    nc.tensor.transpose(aux[b // 4][:, (b % 4) * P:(b % 4 + 1) * P], kc_rows[:, b, :], ident[:, :])
                for c in range(CT):
                    tr = nc.tensor.transpose(aux[2][:, c * 16:(c + 1) * 16], st_rows[:, c * P:(c + 1) * P],
                                             ident[0:16, 0:16])
                tr.then_inc(kct_done, 1)

            def v_transposes(part):
                pe.wait_ge(z_act, z_count(Z_KV[part], "act"))
                if part == 0:
                    pe.wait_ge(kct_copied, 1)
                else:
                    pe.wait_ge(vt_copied, 1)
                for i, (slot, src, t0, w) in enumerate(V_TILES[part]):
                    tr = nc.tensor.transpose(aux[2 + i // 4][0:w, (i % 4) * P:(i % 4 + 1) * P],
                                             (k_t if src == "k" else v_t)[:, t0:t0 + w], ident[:, :])
                tr.then_inc(vt_done, 1)

            def scores(a):
                b, g = ITEMS[a]
                if a >= 1:
                    pe.wait_ge(masked, a)
                if b == "s":
                    pe.wait_ge(qd_ready, 1)
                    nc.tensor.matmul(aux[0][:, WINDOW:S_COLS], q_diag[:, g, :], k_t[:, PROMPT:TOK],
                                     start=True, stop=True)
                    for i in range(4):
                        rows = slice(32 * i, 32 * i + 32)
                        mm = nc.tensor.matmul(aux[0][rows, 0:WINDOW], q_diag[:, g, rows], kc_t[:, 4 * g + i, :],
                                              start=True, stop=True)
                else:
                    q0, nq = BLOCKS[b]
                    la = min(WINDOW, q0)
                    if a == 0:
                        pe.wait_ge(z_act, z_count(AB - 1, "act"))
                        pe.wait_ge(kct_copied, 1)
                    head = slice(g * HEAD_DIM, (g + 1) * HEAD_DIM)
                    for h in range(GQA):
                        mm = nc.tensor.matmul(aux[h // 2][0:nq, (h % 2) * 256:(h % 2) * 256 + la + nq],
                                              q_t[head, h, q0:q0 + nq], k_t[head, q0 - la:q0 + nq],
                                              start=True, stop=True)
                mm.then_inc(scores_done, 1)

            def prob_transposes(a):
                b, g = ITEMS[a]
                pe.wait_ge(probs_ready, a + 1)
                pe.wait_ge(pt_copied, 2 * a) if a else pe.wait_ge(vt_copied, 2)
                if b == "s":
                    nc.tensor.transpose(aux[2][:, 0:P], probs[:, a % 3, 0, 0:WINDOW], ident[:, :])
                    tr = nc.tensor.transpose(aux[3][0:SAMPLE, 0:P], probs[:, a % 3, 0, WINDOW:S_COLS], ident[:, :])
                else:
                    q0, nq = BLOCKS[b]
                    la = min(WINDOW, q0)
                    for h in range(GQA):
                        if la:
                            nc.tensor.transpose(aux[2][0:la, h * nq:(h + 1) * nq], probs[0:nq, a % 3, h, 0:la],
                                                ident[0:nq, 0:nq])
                        tr = nc.tensor.transpose(aux[3][0:nq, h * nq:(h + 1) * nq], probs[0:nq, a % 3, h, la:la + nq],
                                                 ident[0:nq, 0:nq])
                tr.then_inc(pt_done, 1)

            def values(a):
                b, g = ITEMS[a]
                pe.wait_ge(pt_copied, 2 * a + 2)
                if a >= 1:
                    pe.wait_ge(att_lo, a)
                else:
                    pe.wait_ge(z_act, z_count(AB - 1, "act"))
                if b == "s":
                    if g == 0:
                        pe.wait_ge(vc_in, 16)
                    nc.tensor.matmul(acc[3][:, 0:P], v_tok[0:SAMPLE, 9, :], p_t[0:SAMPLE, 1, 0:P],
                                     start=True, stop=False)
                    for i in range(4):
                        rows = slice(32 * i, 32 * i + 32)
                        mm = nc.tensor.matmul(acc[3][:, rows], vc[:, 4 * g + i, :], p_t[:, 0, rows],
                                              start=False, stop=i == 3)
                else:
                    q0, nq = BLOCKS[b]
                    la = min(WINDOW, q0)
                    if la:
                        nc.tensor.matmul(acc[3][:, 0:GQA * nq], v_tok[0:la, 2 * b - 1, :], p_t[0:la, 0, 0:GQA * nq],
                                         start=True, stop=False)
                    mm = nc.tensor.matmul(acc[3][:, 0:GQA * nq], v_tok[0:nq, 2 * b, :], p_t[0:nq, 1, 0:GQA * nq],
                                          start=not la, stop=True)
                mm.then_inc(att_done, 1)

            def attention_slot(k):
                if k < len(ITEMS):
                    scores(k)
                if 2 <= k < len(ITEMS) + 2:
                    prob_transposes(k - 2)
                if 3 <= k < len(ITEMS) + 3:
                    values(k - 3)

            pe.wait_ge(x_ready, 3 * KT)
            pe.wait_ge(r_done, 2 * R0)
            for m in range(4):
                wi_step(m)
            for u in (0, 2):
                pe.wait_ge(z_act, u + 2)
                unit_pair(U_WI + u, acc[u:u + 2], 1, 3 * KT)
            cache_transposes()
            for m in range(2 * WI_GROUPS[0], len(WI_STEPS)):
                wi_step(m)
                if m == PREP + 1:
                    v_transposes(0)
                if m == PREP + 3:
                    v_transposes(1)
                if m > AB and (m - AB) % 2 == 1:
                    attention_slot((m - AB) // 2)

            for k in range(WO_STEPS):
                half, n = k // KT, U_WO + k
                pe.wait_ge(lo_ready, n + 1)
                if k % KT == 0:
                    pe.wait_ge(gated_lo, 6 + 2 * half)
                    pe.wait_ge(att_lo, (ITEMS_H0, len(ITEMS))[half])
                if k >= 3:
                    pe.wait_ge(r_done, 2 * R0 + k - 2)
                elif k == 0:
                    pe.wait_ge(z_dve, z_count(len(WI_STEPS) - 1, "dve"))
                    pe.wait_ge(z_act, z_count(len(WI_STEPS) - 1, "act"))
                mix = (lambda t: mix_hi[:, t, cols(half)]), (lambda t: mix_lo[:, t, cols(half)])
                products(acc[k % 3], n % SLOTS, range(0, 2), *mix)
                if k == 8:
                    ln_mean(2)
                if k == 10:
                    pe.wait_ge(ut_copied, 3)
                    ln_var(2)
                products(acc[k % 3], n % SLOTS, range(2, KT), *mix, t0=2).then_inc(steps_done, 1)
                if k in (1, 3, 5):
                    attention_slot((len(WI_STEPS) - AB + k) // 2)
                if k == 6:
                    pe.wait_ge(pt_copied, 2 * len(ITEMS))
                    for ch in range(CT):
                        for j in range(2):
                            nc.tensor.transpose(aux[2 + j][0:DEC_BATCH, ch * P:(ch + 1) * P],
                                                u_s[:, ch, :, DEC_SEQ + j], ident[:, :])
                        tr = nc.tensor.transpose(aux[1][0:2, ch * P:(ch + 1) * P],
                                                 u_p[:, ch, PROMPT:PROMPT + 2], ident[:, :])
                    tr.then_inc(ut_done, 1)
            pe.wait_ge(r_done, 4 * R0)

            feed_forward(1)
            ln_mean(5)
            ln_var(5)
            transpose_rows(5, [(t, b) for b in range(2) for t in range(3, 6)])


        @block.scalar
        def _(act):
            def weight_hi(n):
                tiles = tiles_of(n)
                act.wait_ge(weights_in[n % SLOTS], ARRIVED[n])
                if n >= SLOTS:
                    act.wait_ge(steps_done, free_after(n - SLOTS))
                nc.scalar.activation(w_hi[:, n % SLOTS, 0:tiles, :], w_raw[:, n % SLOTS, 0:tiles, :],
                                     ACT.Copy).then_inc(hi_ready, 1)

            def gate_up_hi(f, i, u):
                n0 = U_GU[f] + 4 + u
                act.wait_ge(weights_in[n0 % SLOTS], ARRIVED[n0] + 16 * i)
                act.wait_ge(steps_done, free_after(n0 - SLOTS) + 8 * i)
                nc.scalar.activation(w_hi[:, n0 % SLOTS, :, :], w_raw[:, n0 % SLOTS, :, :],
                                     ACT.Copy).then_inc(hi_ready, 1)

            def silu(f, i, half, ab, first=False):
                m0 = 44 * f + 2 * half + ab
                act.wait_ge(steps_done, T_GU[f] + 4 * half + 2 * ab + 1 + 8 * i)
                if m0 >= 2 or not first:
                    act.wait_ge(h_done, m0 - 1 + 4 * i)
                nc.scalar.activation(silu_g[:, ab, :], acc[2 * ab][:, 0:HALF], ACT.Silu).then_inc(silu_done, 1)

            def hidden_hi(f, i, half, ab):
                m0 = 44 * f + 2 * half + ab
                act.wait_ge(h_done, m0 + 1 + 4 * i)
                nc.scalar.activation(h_hi[:, bass.ds(2 * i + ab, 1), cols(half)], h_f32[:, ab:ab + 1, :],
                                     ACT.Copy).then_inc(h_hi_done, 1)

            def gate_up_group(f, i, split, first=False, ahead=0):
                if ahead < 1:
                    silu(f, i, 0, 0, first)
                hidden_hi(f, i, 0, 0)
                if ahead < 2:
                    silu(f, i, 0, 1, first)
                hidden_hi(f, i, 0, 1)
                silu(f, i, 1, 0)
                split(0)
                hidden_hi(f, i, 1, 0)
                split(1)
                silu(f, i, 1, 1)
                split(2)
                hidden_hi(f, i, 1, 1)
                split(3)

            def ln_square(L, chunks=range(KT)):
                for c in chunks:
                    act.wait_ge(centered, KT * L + c + 1)
                    if c < 4 and 3 * L + c // 2:
                        act.wait_ge(sq_pool, 3 * L + c // 2)
                    nc.scalar.activation(squares_of(c), x_res[:, c, cols(L % 2)], ACT.Square).then_inc(squared, 1)

            def sqrt_table(L):
                nc.scalar.activation(warm[:, L:L + 1], eps[:, :], ACT.Sqrt)

            def ln_std(L):
                act.wait_ge(var_done, L + 1)
                if L >= 1:
                    act.wait_ge(scaled, KT * L)
                nc.scalar.activation(rstd[:, :], aux[1][:, 0:HALF], ACT.Sqrt, bias=eps[:, :]).then_inc(std_done, 1)

            def ln_hi(L, chunks):
                for c in chunks:
                    act.wait_ge(scaled, 8 * L + c + 1)
                    b = B0 + 8 * (L // 2) + c
                    nc.scalar.activation(x_hi[:, c, cols(L % 2)], x_res[:, c, cols(L % 2)], ACT.Identity,
                                         bias=coef[:, b:b + 1]).then_inc(x_hi_done, 1)

            def ln_out(L, chunks):
                for c in chunks:
                    act.wait_ge(scaled, 8 * L + c + 1)
                    b = B0 + 8 * (L // 2) + c
                    nc.scalar.activation(x_res[:, c, cols(L % 2)], x_res[:, c, cols(L % 2)], ACT.Identity,
                                         bias=coef[:, b:b + 1]).then_inc(y_biased, 1)

            def copy_rows(L):
                for t, (half, t0, w) in enumerate(Y_TILES):
                    if half == L - 4:
                        act.wait_ge(y_t[1], t + 1)
                        nc.scalar.activation(y_rows[0:w, t, 512:1024], y_bank(t, 1)[0:w, :], ACT.Copy
                                             ).then_inc(y_rows_act, 1)

            def down(f):
                for half in range(2):
                    n0 = U_DN[f] + DN_UNITS * half
                    if half == 0:
                        with act.Fori(0, KT) as c:
                            for d in range(4):
                                n = n0 + 4 + d
                                act.wait_ge(weights_in[n % SLOTS], ARRIVED[n] + 16 * c)
                                act.wait_ge(steps_done, free_after(n - SLOTS) + 4 * c)
                                nc.scalar.activation(w_hi[:, n % SLOTS, 0:tiles_of(n), :],
                                                     w_raw[:, n % SLOTS, 0:tiles_of(n), :], ACT.Copy).then_inc(hi_ready, 1)
                    else:
                        L = 4 * f
                        for c in range(KT):
                            for d in range(4):
                                n = n0 + 4 * (c + 1) + d
                                if n < U_END:
                                    weight_hi(n)
                                if (c, d) in ((0, 1), (0, 2)):
                                    ln_square(L, range(4 * d - 4, 4 * d))
                                if (c, d) == (0, 3):
                                    sqrt_table(L)
                                if (c, d) == (1, 0):
                                    ln_std(L)
                                if (c, d) in LN_PIECES:
                                    (ln_hi if f == 0 else ln_out)(L, LN_PIECES[c, d])
                            if f == 1 and c == KT - 3:
                                copy_rows(4)

            def feed_forward(f):
                if f == 1:
                    ln_square(3)
                    sqrt_table(3)
                    ln_std(3)
                    silu(f, 0, 0, 0)
                    silu(f, 0, 0, 1)
                    ln_hi(3, range(KT))
                gate_up_group(f, 0, lambda u: gate_up_hi(f, 0, u), first=f == 0, ahead=f + 1)
                with act.Fori(1, GU_GROUPS - 1) as i:
                    gate_up_group(f, i, lambda u: gate_up_hi(f, i, u))
                if f == 0:
                    act.wait_ge(bias_out, 16)
                gate_up_group(f, GU_GROUPS - 1, lambda u: weight_hi(U_DN[f] + u))
                down(f)

            act.dma_start(ident[:, :], identity).then_inc(ident_in, 16)
            def token_copy(part, c):
                cs = x_cols(part)
                act.wait_ge(xt_done, KT * part + c + 1)
                nc.scalar.activation(x_res[:, c, cs], x_bank(part, c)[:, 0:cs.stop - cs.start], ACT.Copy).then_inc(x0_act, 1)

            def token_hi(part, c):
                cs = x_cols(part)
                act.wait_ge((x0_dve, x0_act)[c % 2], (KT * part + c) // 2 + 1)
                nc.scalar.activation(x_hi[:, c, cs], x_res[:, c, cs], ACT.Copy).then_inc(x_hi_done, 1)

            act.wait_ge(memset_done, 2)
            nc.scalar.activation(warm[:, 7:8], eps[:, :], ACT.Silu)
            for c in range(1, KT, 2):
                token_copy(0, c)
                token_hi(0, c - 1)
                if c == 1:
                    weight_hi(0)
                token_hi(0, c)
                if c == 3:
                    weight_hi(1)
            weight_hi(2)
            weight_hi(3)
            for c in range(1, KT, 2):
                token_copy(1, c)
                token_hi(1, c - 1)
                token_hi(1, c)
                if c == 3:
                    silu(0, 0, 0, 0, first=True)
            feed_forward(0)


            def evacuate(m):
                u, half = WI_STEPS[m]
                kind, c = WI_ORDER[u]
                act.wait_ge(steps_done, T_WI + m + 1)
                src = acc[z_bank(m)][:, 0:HALF]
                if kind == "cg":
                    if c >= 2:
                        act.wait_ge(z_dve, step_count("h", c - 2, half))
                    dst = cg_sb[:, half, c % 2, :]
                else:
                    dst = {"k": k_t, "v": v_t}[kind][:, cols(half)] if kind != "q" else q_t[:, c, cols(half)]
                nc.scalar.activation(dst, src, ACT.Copy).then_inc(z_act, 1)

            def gate_hi(m):
                u, half = WI_STEPS[m]
                c = WI_ORDER[u][1]
                e = BG_ORDER.index((c, half))
                act.wait_ge(z_dve, z_count(m, "dve"))
                nc.scalar.activation(mix_hi[:, 4 + c, cols(half)], h_f32[:, e % 2, :], ACT.Copy
                                     ).then_inc(gated_hi, 1)

            def copy_probs(a):
                b, g = ITEMS[a]
                act.wait_ge(pt_done, a + 1)
                if a >= 1:
                    act.wait_ge(att_done, a)
                if b == "s":
                    nc.scalar.activation(p_t[:, 0, 0:P], aux[2][:, 0:P], ACT.Copy).then_inc(pt_copied, 1)
                    nc.scalar.activation(p_t[0:SAMPLE, 1, 0:P], aux[3][0:SAMPLE, 0:P], ACT.Copy).then_inc(pt_copied, 1)
                    return
                q0, nq = BLOCKS[b]
                la = min(WINDOW, q0) or nq
                src = aux[2] if q0 else aux[3]
                nc.scalar.activation(p_t[0:la, 0, 0:GQA * nq], src[0:la, 0:GQA * nq], ACT.Copy).then_inc(pt_copied, 1)
                nc.scalar.activation(p_t[0:nq, 1, 0:GQA * nq], aux[3][0:nq, 0:GQA * nq], ACT.Copy).then_inc(pt_copied, 1)

            def attended_hi(a):
                b, g = ITEMS[a]
                act.wait_ge(att_done, a + 1)
                if b == "s":
                    for kv in range(N_KV):
                        rows = slice(kv * HEAD_DIM, (kv + 1) * HEAD_DIM)
                        for h in range(GQA):
                            hi = nc.scalar.activation(sample_cols(mix_hi, rows, h, g), sample_out(rows, kv, h), ACT.Copy)
                else:
                    q0, nq = BLOCKS[b]
                    rows = slice(g * HEAD_DIM, (g + 1) * HEAD_DIM)
                    hi = nc.scalar.activation(mix_hi[rows, 0:GQA, q0:q0 + nq],
                                              acc[3][rows, 0:GQA * nq].rearrange("p (h q) -> p h q", h=GQA), ACT.Copy)
                hi.then_inc(att_hi, 1)

            def exps(a):
                b, g = ITEMS[a]
                act.wait_ge(neg_ready, a + 1)
                rows, heads, span = item_shape(a)
                for h in range(heads):
                    nc.scalar.activation(probs[0:rows, a % 3, h, 0:span], probs[0:rows, a % 3, h, 0:span], ACT.Exp,
                                         bias=neg_max[0:rows, a % 3, h:h + 1], accum_out=row_sum[0:rows, a % 3, h:h + 1])
                for h in range(heads):
                    sk = sink_row[:, :] if b == "s" else sinks[0:rows, 4 * g + h:4 * g + h + 1]
                    e = nc.scalar.activation(sink_exp[0:rows, a % 3, h:h + 1], sk, ACT.Exp,
                                             bias=neg_max[0:rows, a % 3, h:h + 1])
                e.then_inc(exps_done, 1)

            def attention(k, odd):
                if odd:
                    if 2 <= k < len(ITEMS) + 2:
                        copy_probs(k - 2)
                    if 3 <= k < len(ITEMS) + 3:
                        attended_hi(k - 3)
                elif 1 <= k < len(ITEMS) + 1:
                    exps(k - 1)

            def split_after(step):
                for n in range(U_WI + SLOTS, U_GU[1] + SLOTS):
                    if free_after(n - SLOTS) == step + 1:
                        weight_hi(n)

            ln_square(1)
            sqrt_table(1)
            for m in range(3):
                evacuate(m)
            ln_std(1)
            evacuate(3)
            ln_hi(1, range(KT))
            for m in range(4, len(WI_STEPS)):
                kind = WI_ORDER[WI_STEPS[m][0]][0]
                if m >= AB and (m - AB) % 2 == 0:
                    attention((m - AB) // 2, odd=False)
                if kind == "bg":
                    gate_hi(m)
                elif kind != "h":
                    evacuate(m)
                split_after(T_WI + m)
                if m == PREP:
                    act.wait_ge(kct_done, 1)
                    for i in range(2):
                        nc.scalar.activation(kc_t[:, 4 * i:4 * i + 4, :],
                                             aux[i][:, :].rearrange("p (b s) -> p b s", b=4), ACT.Copy)
                    nc.scalar.activation(u_s[:, :, :, 0:2], aux[2][:, 0:64].rearrange("p (c b j) -> p c b j", c=CT, b=DEC_BATCH),
                                         ACT.Copy).then_inc(kct_copied, 1)
                if m == PREP + 1:
                    copy_v_tiles(act, 0)
                if m == PREP + 3:
                    copy_v_tiles(act, 1)
                if m > AB and (m - AB) % 2 == 1:
                    attention((m - AB) // 2, odd=True)

            for k in range(WO_STEPS):
                s = len(WI_STEPS) - AB + k
                if s % 2 == 0:
                    attention(s // 2, odd=False)
                if k == 8:
                    ln_square(2)
                    sqrt_table(2)
                if k == 9:
                    ln_std(2)
                split_after(T_WO + k)
                if s % 2:
                    attention(s // 2, odd=True)
                if k == 6:
                    act.wait_ge(ut_done, 1)
                    for j in range(2):
                        nc.scalar.activation(u_rows[:, j, :], aux[2 + j][0:DEC_BATCH, :], ACT.Copy).then_inc(ut_copied, 1)
                    nc.scalar.activation(u_rows[0:2, 2, :], aux[1][0:2, :], ACT.Copy).then_inc(ut_copied, 1)
                if k in WO_PIECES:
                    ln_hi(2, WO_PIECES[k])
            feed_forward(1)
            ln_square(5)
            sqrt_table(5)
            ln_std(5)
            ln_out(5, range(KT))
            copy_rows(5)


        @block.vector
        def _(dve):
            def weight_lo(n, i=0):
                tiles = tiles_of(n)
                dve.wait_ge(hi_ready, n + 1 + SLOTS * i)
                nc.vector.tensor_tensor(w_lo[:, n % SLOTS, 0:tiles, :], w_raw[:, n % SLOTS, 0:tiles, :],
                                        w_hi[:, n % SLOTS, 0:tiles, :].bitcast(F32), ALU.subtract).then_inc(lo_ready, 1)

            def hidden(f, i, half, ab, first=False):
                m0 = 44 * f + 2 * half + ab
                dve.wait_ge(silu_done, m0 + 1 + 4 * i)
                dve.wait_ge(steps_done, T_GU[f] + 4 * half + 2 * ab + 2 + 8 * i)
                if m0 >= 2 or not first:
                    dve.wait_ge(h_hi_done, m0 - 1 + 4 * i)
                    dve.wait_ge(h_ready, m0 - 1 + 4 * i)
                nc.vector.scalar_tensor_tensor(h_f32[:, ab, :], silu_g[:, ab, :], 0.5, acc[2 * ab + 1][:, 0:HALF],
                                               ALU.mult, ALU.mult).then_inc(h_done, 1)

            def hidden_lo(f, i, half, ab):
                m0 = 44 * f + 2 * half + ab
                dve.wait_ge(h_hi_done, m0 + 1 + 4 * i)
                at = bass.ds(2 * i + ab, 1)
                nc.vector.tensor_tensor(h_lo[:, at, cols(half)], h_f32[:, ab:ab + 1, :],
                                        h_hi[:, at, cols(half)].bitcast(F32), ALU.subtract).then_inc(h_ready, 1)

            def gate_up_group(f, i, split, first=False, ahead=0):
                if ahead < 1:
                    hidden(f, i, 0, 0, first)
                hidden_lo(f, i, 0, 0)
                if ahead < 2:
                    hidden(f, i, 0, 1, first)
                hidden_lo(f, i, 0, 1)
                hidden(f, i, 1, 0)
                split(0)
                hidden_lo(f, i, 1, 0)
                split(1)
                hidden(f, i, 1, 1)
                split(2)
                hidden_lo(f, i, 1, 1)
                split(3)

            def residual(L, c, bank, step, first=False, last=False):
                half = L % 2
                dve.wait_ge(steps_done, step)
                x = x_res[:, bass.ds(c, 1), cols(half)]
                a = acc[bank][:, 0:HALF].unsqueeze(1)
                s = ln_sum[:, half:half + 1, :]
                nc.vector.scalar_tensor_tensor(x, x, ALPHA, a, ALU.mult, ALU.add).then_inc(r_done, 1)
                if last or L in POOL_SUMS:
                    return
                dve.wait_ge(r_done, R0 * L + c + 1)
                if first:
                    if L >= 2:
                        dve.wait_ge(var_done, L - 1)
                    nc.vector.tensor_copy(s, x).then_inc(sum_done, 1)
                else:
                    dve.wait_ge(sum_done, L0 * L + c)
                    nc.vector.tensor_tensor(s, s, x, ALU.add).then_inc(sum_done, 1)

            def ln_center(L, chunks=range(KT)):
                dve.wait_ge(mean_done, L + 1)
                for c in chunks:
                    x = x_res[:, c, cols(L % 2)]
                    nc.vector.tensor_tensor(x, x, aux[0][:, 0:HALF], ALU.subtract).then_inc(centered, 1)

            def ln_sum_squares(L):
                s = squares_of(4)
                for c in range(5, KT):
                    dve.wait_ge(squared, KT * L + c + 1)
                    if c >= 6:
                        dve.wait_ge(sq_dve, 3 * L + c - 5)
                    nc.vector.tensor_tensor(s, s, squares_of(c), ALU.add).then_inc(sq_dve, 1)

            def ln_rstd(L):
                dve.wait_ge(std_done, L + 1)
                nc.vector.reciprocal(rstd[:, :], rstd[:, :]).then_inc(rstd_done, 1)
                dve.wait_ge(rstd_done, L + 1)

            def ln_scale(L, chunks):
                for c in chunks:
                    x = x_res[:, c, cols(L % 2)]
                    g = G0 + 8 * (L // 2) + c
                    nc.vector.scalar_tensor_tensor(x, x, coef[:, g:g + 1], rstd[:, :], ALU.mult, ALU.mult
                                                   ).then_inc(scaled, 1)

            def ln_lo(L, chunks):
                for c in chunks:
                    b = B0 + 8 * (L // 2) + c
                    dve.wait_ge(x_hi_done, KT * (2 + L) + c + 1)
                    nc.vector.scalar_tensor_tensor(x_lo[:, c, cols(L % 2)], x_res[:, c, cols(L % 2)],
                                                   coef[:, b:b + 1], x_hi[:, c, cols(L % 2)].bitcast(F32),
                                                   ALU.add, ALU.subtract).then_inc(x_ready, 1)

            def ln_apply(L, chunks):
                for c in chunks:
                    ln_scale(L, [c])
                    if L < 4 and c > chunks[0]:
                        ln_lo(L, [c - 1])
                if L < 4:
                    ln_lo(L, [chunks[-1]])

            def copy_rows(L):
                for t, (half, t0, w) in enumerate(Y_TILES):
                    if half == L - 4:
                        dve.wait_ge(y_t[0], t + 1)
                        nc.vector.tensor_copy(y_rows[0:w, t, 0:512], y_bank(t, 0)[0:w, :]).then_inc(y_rows_dve, 1)

            def down(f):
                for half in range(2):
                    n0 = U_DN[f] + DN_UNITS * half
                    L, t0 = 4 * f + half, T_DN[f] + DN_UNITS * half + 4
                    if f:
                        dve.wait_ge(res_biased, KT * (3 + half))
                    if half == 0:
                        def chunk(c, c2, i=0, **ends):
                            for d in range(3):
                                weight_lo(n0 + 4 + 4 * c2 + d, 2 * i)
                            residual(L, c, c2 % 2, t0 + 4 * c2 + 8 * i, **ends)
                            weight_lo(n0 + 4 + 4 * c2 + 3, 2 * i)

                        chunk(0, 0, first=True)
                        chunk(1, 1)
                        with dve.Fori(1, KT // 2 - 1) as i:
                            chunk(2 * i, 0, i)
                            chunk(2 * i + 1, 1, i)
                        chunk(KT - 2, KT - 2)
                        chunk(KT - 1, KT - 1, last=True)
                    else:
                        H = 4 * f
                        for c in range(KT):
                            for d in range(4):
                                n = n0 + 4 * (c + 1) + d
                                if d == 3:
                                    residual(L, c, c % 2, t0 + 4 * c, first=c == 0, last=c == KT - 1)
                                if n < U_END:
                                    weight_lo(n)
                                if (c, d) == (0, 0):
                                    ln_center(H)
                                if (c, d) == (0, 3):
                                    ln_sum_squares(H)
                                if (c, d) == (1, 0):
                                    ln_rstd(H)
                                if (c, d) in LN_PIECES:
                                    ln_apply(H, LN_PIECES[c, d])
                            if f == 1 and c == KT - 3:
                                copy_rows(4)

            def parameters():
                dve.wait_ge(params_t, 1)
                nc.vector.tensor_copy(coef[:, 0:60], aux[0][:, 0:60]).then_inc(coef_ready, 1)
                dve.wait_ge(params_t, 2)
                nc.vector.tensor_tensor(bias_row[:, :], bias_row[:, :], aux[1][0:N_HEADS, 0:T_W], ALU.add
                                        ).then_inc(table_ready, 1)

            def feed_forward(f):
                if f == 1:
                    ln_center(3)
                    ln_sum_squares(3)
                    ln_rstd(3)
                    hidden(f, 0, 0, 0)
                    hidden(f, 0, 0, 1)
                    ln_apply(3, range(KT))
                gate_up_group(f, 0, lambda u: weight_lo(U_GU[f] + 4 + u), first=f == 0, ahead=f + 1)
                if f == 0:
                    parameters()
                with dve.Fori(1, GU_GROUPS - 1) as i:
                    gate_up_group(f, i, lambda u: weight_lo(U_GU[f] + 4 + u, i))
                gate_up_group(f, GU_GROUPS - 1, lambda u: weight_lo(U_DN[f] + u))
                down(f)

            nc.vector.memset(mean_of[:, :], 1.0 / D_MODEL).then_inc(memset_done, 1)
            nc.vector.memset(eps[:, :], LN_EPS).then_inc(memset_done, 1)

            def token_copy(part, c):
                cs = x_cols(part)
                dve.wait_ge(xt_done, KT * part + c + 1)
                nc.vector.tensor_copy(x_res[:, c, cs], x_bank(part, c)[:, 0:cs.stop - cs.start]).then_inc(x0_dve, 1)

            def token_lo(part, c):
                cs = x_cols(part)
                dve.wait_ge(x_hi_done, KT * part + c + 1)
                nc.vector.tensor_tensor(x_lo[:, c, cs], x_res[:, c, cs], x_hi[:, c, cs].bitcast(F32), ALU.subtract
                                        ).then_inc(x_ready, 1)

            for c in (0, 2, 4):
                token_copy(0, c)
            token_lo(0, 0)
            weight_lo(0)
            token_lo(0, 1)
            token_copy(0, 6)
            token_lo(0, 2)
            token_lo(0, 3)
            weight_lo(1)
            for c in range(4, KT):
                token_lo(0, c)
            weight_lo(2)
            weight_lo(3)
            for c0 in (0, 4):
                token_copy(1, c0)
                token_copy(1, c0 + 2)
                for c in range(c0, c0 + 4):
                    token_lo(1, c)
                if c0 == 0:
                    hidden(0, 0, 0, 0, first=True)

            feed_forward(0)
            ln_center(1)
            ln_sum_squares(1)
            ln_rstd(1)
            ln_apply(1, range(KT))

            def conv_input(m):
                u, half = WI_STEPS[m]
                c = WI_ORDER[u][1]
                dve.wait_ge(steps_done, T_WI + m + 1)
                cg_step = WI_STEPS.index((WI_ORDER.index(("cg", c)), half))
                dve.wait_ge(z_act, z_count(cg_step, "act"))
                cg = cg_sb[:, half, c % 2, :]
                src = acc[z_bank(m)]
                if half == 0:
                    last = nc.vector.tensor_tensor(u_p[:, c, 2:2 + HALF], cg, src[:, 0:HALF], ALU.mult)
                else:
                    n = PROMPT - HALF
                    nc.vector.tensor_tensor(u_p[:, c, 2 + HALF:2 + PROMPT], cg[:, 0:n], src[:, 0:n], ALU.mult)
                    last = nc.vector.tensor_tensor(
                        u_s[:, c, :, 2:2 + DEC_SEQ], cg[:, n:HALF].rearrange("p (b t) -> p b t", b=DEC_BATCH),
                        src[:, n:HALF].rearrange("p (b t) -> p b t", b=DEC_BATCH), ALU.mult)
                last.then_inc(z_dve, 1)

            def gate(m):
                u, half = WI_STEPS[m]
                c = WI_ORDER[u][1]
                e = BG_ORDER.index((c, half))
                dve.wait_ge(steps_done, T_WI + m + 1)
                dve.wait_ge(taps_added, 2 * CONV_ORDER.index((c, half)) + 2)
                if e >= 2:
                    dve.wait_ge(gated_hi, e - 1)
                    dve.wait_ge(gated_lo, e - 1)
                nc.vector.tensor_tensor(h_f32[:, e % 2, :], conv[:, half, c % 2, :], acc[z_bank(m)][:, 0:HALF], ALU.mult
                                        ).then_inc(z_dve, 1)
                dve.wait_ge(gated_hi, e + 1)
                nc.vector.tensor_tensor(mix_lo[:, 4 + c, cols(half)], h_f32[:, e % 2, :],
                                        mix_hi[:, 4 + c, cols(half)].bitcast(F32), ALU.subtract).then_inc(gated_lo, 1)

            def mask_and_max(a):
                b, g = ITEMS[a]
                rows, heads, span = item_shape(a)
                dve.wait_ge(scores_done, a + 1)
                if a == 0:
                    dve.wait_ge(bias_in, 16)
                    dve.wait_ge(kct_copied, 1)
                    dve.wait_ge(kct_done, 1)
                if a >= 3:
                    dve.wait_ge(pt_done, a - 2)
                if b == "s":
                    if g == 0:
                        dve.wait_ge(bias_s_in, 16 * 16)
                    nc.vector.scalar_tensor_tensor(probs[:, a % 3, 0, 0:span], aux[0][:, 0:span], SCALE,
                                                   bias_s[:, g, :], ALU.mult, ALU.add).then_inc(masked, 1)
                    sk = sink_row[:, :]
                else:
                    q0, nq = BLOCKS[b]
                    first = WINDOW - min(WINDOW, q0)
                    for i in range(2):
                        s = aux[i][0:rows, :].rearrange("p (h s) -> p h s", h=2)[:, :, 0:span]
                        last = nc.vector.scalar_tensor_tensor(
                            probs[0:rows, a % 3, 2 * i:2 * i + 2, 0:span], s, SCALE,
                            bias[0:rows, 4 * g + 2 * i:4 * g + 2 * i + 2, first:first + span], ALU.mult, ALU.add)
                    last.then_inc(masked, 1)
                    sk = sinks[0:rows, 4 * g:4 * g + 4]
                dve.wait_ge(masked, a + 1)
                mx, neg = row_max[0:rows, a % 3, 0:heads], neg_max[0:rows, a % 3, 0:heads]
                nc.vector.tensor_reduce(mx, probs[0:rows, a % 3, 0:heads, 0:span], AX_X, ALU.max).then_inc(max_done, 1)
                dve.wait_ge(max_done, a + 1)
                nc.vector.tensor_tensor(mx, mx, sk, ALU.max).then_inc(max_sink, 1)
                dve.wait_ge(max_sink, a + 1)
                nc.vector.tensor_scalar(neg, mx, -1.0, None, ALU.mult).then_inc(neg_ready, 1)

            def denominators(a):
                rows, heads, span = item_shape(a)
                dve.wait_ge(exps_done, a + 1)
                den, rd = row_sum[0:rows, a % 3, 0:heads], r_den[0:rows, a % 3, 0:heads]
                nc.vector.tensor_tensor(den, den, sink_exp[0:rows, a % 3, 0:heads], ALU.add).then_inc(den_done, 1)
                dve.wait_ge(den_done, a + 1)
                nc.vector.reciprocal(rd, den).then_inc(rden_done, 1)
                dve.wait_ge(rden_done, a + 1)
                for h in range(heads):
                    p = probs[0:rows, a % 3, h, 0:span]
                    last = nc.vector.tensor_scalar(p, p, r_den[0:rows, a % 3, h:h + 1], None, ALU.mult)
                last.then_inc(probs_ready, 1)

            def attended_lo(a):
                b, g = ITEMS[a]
                dve.wait_ge(att_hi, a + 1)
                if b == "s":
                    for kv in range(N_KV):
                        rows = slice(kv * HEAD_DIM, (kv + 1) * HEAD_DIM)
                        for h in range(GQA):
                            lo = nc.vector.tensor_tensor(sample_cols(mix_lo, rows, h, g), sample_out(rows, kv, h),
                                                         sample_cols(mix_hi, rows, h, g).bitcast(F32), ALU.subtract)
                else:
                    q0, nq = BLOCKS[b]
                    rows = slice(g * HEAD_DIM, (g + 1) * HEAD_DIM)
                    lo = nc.vector.tensor_tensor(mix_lo[rows, 0:GQA, q0:q0 + nq],
                                                 acc[3][rows, 0:GQA * nq].rearrange("p (h q) -> p h q", h=GQA),
                                                 mix_hi[rows, 0:GQA, q0:q0 + nq].bitcast(F32), ALU.subtract)
                lo.then_inc(att_lo, 1)

            def attention(k, odd):
                if odd:
                    if k < len(ITEMS):
                        mask_and_max(k)
                    if 3 <= k < len(ITEMS) + 3:
                        attended_lo(k - 3)
                elif 1 <= k < len(ITEMS) + 1:
                    denominators(k - 1)

            def split_after(step):
                for n in range(U_WI + SLOTS, U_GU[1] + SLOTS):
                    if free_after(n - SLOTS) == step + 1:
                        weight_lo(n)

            dve.wait_ge(steps_done, T_WI)
            nc.vector.memset(bias_s[:, :, WINDOW:S_COLS], MASKED).then_inc(zero_done, 1)
            nc.vector.memset(q_diag[:, :, :], 0.0)
            nc.vector.memset(u_p[:, :, 0:2], 0.0).then_inc(zero_done, 1)
            for m in range(len(WI_STEPS)):
                kind = WI_ORDER[WI_STEPS[m][0]][0]
                if m >= AB and (m - AB) % 2 == 0:
                    attention((m - AB) // 2, odd=False)
                if kind == "h":
                    conv_input(m)
                if kind == "bg":
                    gate(m)
                split_after(T_WI + m)
                if m == AB - 1:
                    dve.wait_ge(z_act, z_count(AB - 1, "act"))
                    dve.wait_ge(zero_done, 2)
                    for kv in range(N_KV):
                        rows = slice(kv * HEAD_DIM, (kv + 1) * HEAD_DIM)
                        for h in range(GQA):
                            dst = q_diag[rows, :, :].rearrange("p j (b g t) -> p (j b) g t", b=4, t=DEC_SEQ)[:, :, GQA * kv + h]
                            last = nc.vector.tensor_copy(
                                dst, q_t[rows, h, PROMPT:TOK].rearrange("p (b t) -> p b t", t=DEC_SEQ))
                    last.then_inc(qd_ready, 1)
                if m > AB and (m - AB) % 2 == 1:
                    attention((m - AB) // 2, odd=True)

            for k in range(WO_STEPS):
                s = len(WI_STEPS) - AB + k
                if s % 2 == 0:
                    attention(s // 2, odd=False)
                if k % KT == 0:
                    dve.wait_ge(res_biased, KT * (1 + k // KT))
                if k == 8:
                    ln_center(2)
                residual(2 + k // KT, k % KT, k % 3, T_WO + k + 1, first=k % KT == 0, last=k % KT == KT - 1)
                if k == 8:
                    ln_sum_squares(2)
                if k == 9:
                    ln_rstd(2)
                split_after(T_WO + k)
                if s % 2:
                    attention(s // 2, odd=True)
                if k in WO_PIECES:
                    ln_apply(2, WO_PIECES[k])
            feed_forward(1)
            ln_center(5)
            ln_sum_squares(5)
            ln_rstd(5)
            ln_apply(5, range(KT))
            copy_rows(5)

        @block.gpsimd
        def _(pool):
            def residual_shift(L):
                for c in range(KT):
                    pool.wait_ge(x_ready, KT * (2 + L) + c + 1)
                    b = B0 + 8 * (L // 2) + c
                    x = x_res[:, c, cols(L % 2)]
                    nc.gpsimd.tensor_scalar(x, x, coef[:, b:b + 1], None, ALU.add).then_inc(res_biased, 1)

            def residual_sum(L):
                s = ln_sum[:, L % 2, :]
                pool.wait_ge(r_done, R0 * L + 2)
                pool.wait_ge(var_done, L - 1)
                nc.gpsimd.tensor_tensor(s, x_res[:, 0, cols(L % 2)], x_res[:, 1, cols(L % 2)], ALU.add
                                        ).then_inc(sum_done, 2)
                for c in range(2, KT - 1):
                    pool.wait_ge(r_done, R0 * L + c + 1)
                    pool.wait_ge(sum_done, L0 * L + c)
                    nc.gpsimd.tensor_tensor(s, s, x_res[:, c, cols(L % 2)], ALU.add).then_inc(sum_done, 1)

            def ln_sum_squares(L):
                s = ln_sum[:, L % 2, :]
                for c in range(1, 4):
                    pool.wait_ge(squared, KT * L + c + 1)
                    if c >= 2:
                        pool.wait_ge(sq_pool, 3 * L + c - 1)
                    nc.gpsimd.tensor_tensor(s, squares_of(0) if c == 1 else s, squares_of(c), ALU.add
                                            ).then_inc(sq_pool, 1)

            def convolve(e):
                c, half = CONV_ORDER[e]
                pool.wait_ge(z_dve, step_count("h", c, half))
                if e >= 1:
                    pool.wait_ge(taps_added, 2 * e)
                if c >= 2:
                    pool.wait_ge(z_dve, step_count("bg", c - 2, half))
                n = HALF if half == 0 else PROMPT - HALF
                for j in range(3):
                    w = C0 + CT * j + c
                    at = half * HALF + j
                    last = nc.gpsimd.tensor_scalar(taps[:, j, 0:n], u_p[:, c, at:at + n], coef[:, w:w + 1], None, ALU.mult)
                    if half:
                        last = nc.gpsimd.tensor_scalar(
                            taps[:, j, n:HALF].rearrange("p (b t) -> p b t", b=DEC_BATCH),
                            u_s[:, c, :, j:j + DEC_SEQ], coef[:, w:w + 1], None, ALU.mult)
                last.then_inc(taps_done, 1)
                pool.wait_ge(taps_done, e + 1)
                nc.gpsimd.tensor_tensor(taps[:, 0, :], taps[:, 0, :], taps[:, 1, :], ALU.add).then_inc(taps_added, 1)
                pool.wait_ge(taps_added, 2 * e + 1)
                nc.gpsimd.tensor_tensor(conv[:, half, c % 2, :], taps[:, 0, :], taps[:, 2, :], ALU.add
                                        ).then_inc(taps_added, 1)

            pool.wait_ge(coef_ready, 1)
            for L in range(2):
                ln_sum_squares(L)
                residual_shift(L)
            for m in range(AB, len(WI_STEPS)):
                u, half = WI_STEPS[m]
                if WI_ORDER[u][0] == "h":
                    if m == WI_STEPS.index((WI_ORDER.index(("h", 0)), 0)):
                        pool.wait_ge(zero_done, 2)
                        pool.wait_ge(kct_copied, 1)
                    convolve(CONV_ORDER.index((WI_ORDER[u][1], half)))
            residual_sum(2)
            ln_sum_squares(2)
            residual_sum(3)
            ln_sum_squares(3)
            residual_shift(2)
            residual_shift(3)
            for L in range(4, 6):
                ln_sum_squares(L)


_INS = ["x_prompt", "x_sample", "cache_k", "cache_v", "state_conv", "meta_tokens", "rel_bias", "w_in", "conv_w",
        "attn_sink", "w_out", "ffn_w_gate", "ffn_w_up", "ffn_w_down", "ln_g", "ln_b"]
_OUTS = [(1, SEQ, D_MODEL), (DEC_BATCH, DEC_SEQ, D_MODEL), (1, 1, WINDOW, N_KV, HEAD_DIM),
         (1, 1, WINDOW, N_KV, HEAD_DIM), (1, 1, 2, D_CONV), (1, DEC_BATCH, WINDOW, N_KV, HEAD_DIM),
         (1, DEC_BATCH, WINDOW, N_KV, HEAD_DIM), (1, DEC_BATCH, 2, D_CONV)]


def kernel(**inputs):
    import concourse.bacc as bacc
    from concourse.bass_utils import run_bass_kernel_spmd

    nc = bacc.Bacc("TRN2", target_bir_lowering=False, num_devices=1, dynamic_dma_scratch_size=1024)
    one_hot, mask = bias_constants()
    arrays = {name: np.ascontiguousarray(inputs[name]) for name in _INS}
    arrays |= {"identity": np.eye(P, dtype=np.float32), "one_hot": one_hot, "mask_row": mask}
    args = [nc.dram_tensor(f"in_{n}", a.shape, mybir.dt.from_np(a.dtype), kind="ExternalInput").ap()
            for n, a in arrays.items()]
    args += [nc.dram_tensor(f"out_{i}", s, F32, kind="ExternalOutput").ap() for i, s in enumerate(_OUTS)]
    build(nc, *args)
    r = run_bass_kernel_spmd(nc, [{f"in_{n}": a for n, a in arrays.items()}], core_ids=[0])
    return tuple(r.results[0][f"out_{i}"] for i in range(len(_OUTS)))
```

```python
from contextlib import ExitStack

import numpy as np

import concourse.bass as bass
from concourse import mybir
from concourse.alu_op_type import AluOpType as ALU

ACT = mybir.ActivationFunctionType
F32 = mybir.dt.float32
F32R = mybir.dt.float32r
AX_X = mybir.AxisListType.X

P = 128
D_MODEL = 1024
SEQ = 512
N_META = 16
DEC_BATCH = 8
DEC_SEQ = 4
N_HEADS = 8
N_KV = 2
GQA = N_HEADS // N_KV
HEAD_DIM = 64
D_ATTN = N_HEADS * HEAD_DIM
D_CONV = D_MODEL - D_ATTN
D_KV = N_KV * HEAD_DIM
WINDOW = 128
N_BUCKETS = 32
MAX_DISTANCE = 128
D_FF = 2816
ALPHA = float(2.0 ** 0.25)
LN_EPS = 1e-5
SCALE = HEAD_DIM ** -0.5
MASKED = -1.0e30

PROMPT = N_META + SEQ
SAMPLE = DEC_BATCH * DEC_SEQ
TOK = PROMPT + SAMPLE
HALF = TOK // 2
KT = D_MODEL // P
FT = D_FF // P
CT = D_CONV // P
XT = 112
N_XT = TOK // XT
LAST_KEYS = PROMPT - WINDOW

SLOTS = 4
GU_UNITS = 2 * FT
DN_CUT = (0, 6, 12, 17, 22)
DN_SHARED = 4
DN_UNITS = 4 * (KT + KT - DN_SHARED)
DN_STEPS = 8 * KT
WI_ORDER = (("k", 0), ("v", 0), ("q", 0), ("q", 1), ("q", 2), ("q", 3),
            ("cg", 0), ("h", 0), ("cg", 1), ("h", 1), ("bg", 0), ("bg", 1),
            ("cg", 2), ("h", 2), ("cg", 3), ("h", 3), ("bg", 2), ("bg", 3))
WI_GROUPS = (4, 2, 4, 4, 4)
U_GU = (0, GU_UNITS + DN_UNITS + len(WI_ORDER) + 2 * KT)
U_DN = (U_GU[0] + GU_UNITS, U_GU[1] + GU_UNITS)
U_WI = U_DN[0] + DN_UNITS
U_WO = U_WI + len(WI_ORDER)
U_END = U_DN[1] + DN_UNITS
GU_GROUPS = FT // 2
T_GU = (0, 2 * GU_UNITS + DN_STEPS + 2 * len(WI_ORDER) + 2 * KT)
T_DN = (T_GU[0] + 2 * GU_UNITS, T_GU[1] + 2 * GU_UNITS)
T_WI = T_DN[0] + DN_STEPS
T_WO = T_WI + 2 * len(WI_ORDER)

COL0 = {"q": 0, "k": D_ATTN, "v": D_ATTN + D_KV, "bg": D_ATTN + 2 * D_KV,
        "cg": D_ATTN + 2 * D_KV + D_CONV, "h": D_ATTN + 2 * D_KV + 2 * D_CONV}

BLOCKS = ((0, 96), (96, 96), (192, 88), (280, 124), (404, 124))
ITEMS = [(b, g) for b in range(len(BLOCKS)) for g in range(N_KV)] + [("s", 0), ("s", 1)]
ITEMS_H0 = 6
QMAX = 124
SPAN = QMAX + WINDOW
S_COLS = WINDOW + SAMPLE
T_W = WINDOW - 1 + SPAN + 1


def wi_steps():
    out, u0 = [], 0
    for size in WI_GROUPS:
        for half in range(2):
            out += [(u0 + u, half) for u in range(size)]
        u0 += size
    return out


WI_STEPS = wi_steps()

Y_TILES = [(0, 16, 96), (0, 112, 112), (0, 224, 56), (1, 280, 56), (1, 336, 112), (1, 448, 112)]
X_DMAS = [2, 1, 1, 1, 2]
X_PARTS = ((0, 1, 2), (3, 4))
N_CONSTS = 2 + 1 + 3 + 1 + 4
V_TILES = ([(0, "v", 0, 96), (1, "v", 0, 96), (2, "v", 96, 96), (3, "v", 64, 128), (4, "v", 192, 88)],
           [(5, "v", 152, 128), (6, "v", 280, 124), (7, "v", 276, 128), (8, "v", 404, 124),
            (9, "v", PROMPT, SAMPLE), (10, "k", LAST_KEYS, P), (11, "v", LAST_KEYS, P),
            (12, "k", PROMPT, SAMPLE)])
PREP = 2 * WI_GROUPS[0] - 1
Z_KV = (1, WI_GROUPS[0] + 1)
CONV_ORDER = [(WI_ORDER[u][1], half) for u, half in WI_STEPS if WI_ORDER[u][0] == "h"]
BG_ORDER = [(WI_ORDER[u][1], half) for u, half in WI_STEPS if WI_ORDER[u][0] == "bg"]


def free_after(n):
    for f in range(2):
        if U_GU[f] <= n < U_GU[f] + GU_UNITS:
            i, u = divmod(n - U_GU[f], 4)
            return T_GU[f] + 8 * i + 4 + u + 1
        if U_DN[f] <= n < U_DN[f] + DN_UNITS:
            m = n - U_DN[f]
            return T_DN[f] + (2 * m + 2 if m < 4 * DN_SHARED else 4 * DN_SHARED + m + 1)
    if n < U_WO:
        return T_WI + WI_STEPS.index((n - U_WI, 1)) + 1
    return T_WO + n - U_WO + 1


def tiles_of(n):
    for f in range(2):
        if U_DN[f] <= n < U_DN[f] + DN_UNITS:
            d = (n - U_DN[f]) % 4
            return DN_CUT[d + 1] - DN_CUT[d]
    return KT


def r_count(L, c):
    if L in (2, 3):
        return R_FREE + KT * L + c + 1
    half = L % 2
    return R_FREE + KT * (L - half) + 1 + (2 * c + half if c < DN_SHARED else DN_SHARED + c + half * (KT - DN_SHARED))


def sum_count(L, c):
    if L >= 2:
        return (KT - 1) * L + c + 1
    return 1 + (2 * c + L if c < DN_SHARED else DN_SHARED + c + L * (KT - 1 - DN_SHARED))


def arrived_values():
    total, out = [0] * SLOTS, []
    for n in range(U_END):
        is_q = U_WI <= n < U_WO and WI_ORDER[n - U_WI][0] == "q"
        total[n % SLOTS] += 48 if U_WO <= n < U_GU[1] else 32 if is_q else 16
        out.append(total[n % SLOTS])
    return out


ARRIVED = arrived_values()


R_FREE = 4


def bias_constants():
    d = 2 * WINDOW - 1 - np.arange(T_W)
    valid = (d >= 0) & (d <= WINDOW)
    exact = N_BUCKETS // 2
    df = np.maximum(d, 1).astype(np.float32)
    large = exact + (np.log(df / np.float32(exact)) / np.float32(np.log(MAX_DISTANCE / exact))
                     * np.float32(N_BUCKETS - exact)).astype(np.int32)
    bucket = np.where(d < exact, np.maximum(d, 0), np.minimum(large, N_BUCKETS - 1))
    one_hot = ((np.arange(N_BUCKETS)[:, None] == bucket[None, :]) & valid[None, :]).astype(np.float32)
    mask = np.broadcast_to(np.where(valid, 0.0, MASKED).astype(np.float32), (N_HEADS, T_W))
    return one_hot, np.ascontiguousarray(mask)


def build(nc, x_prompt, x_sample, cache_k, cache_v, state_conv, meta_tokens, rel_bias, w_in, conv_w,
          attn_sink, w_out, w_gate, w_up, w_down, ln_g, ln_b, identity, one_hot, mask_row,
          y_prompt, y_sample, new_k_prompt, new_v_prompt, new_conv_prompt,
          new_k_sample, new_v_sample, new_conv_sample):
    ctx = ExitStack()
    with ctx:
        def sb(name, shape, dt=F32, stack=ctx):
            return stack.enter_context(nc.sbuf_tensor(name, shape, dt))

        def sem(name):
            return ctx.enter_context(nc.semaphore(name))

        x_res = sb("x_res", [P, KT, TOK])
        w_raw = sb("w_raw", [P, SLOTS, KT, P])
        w_hi = sb("w_hi", [P, SLOTS, KT, P], F32R)
        w_lo = sb("w_lo", [P, SLOTS, KT, P], F32R)
        ident = sb("ident", [P, P])
        mean_of = sb("mean_of", [P, P])
        coef = sb("coef", [P, 64])
        sinks = sb("sinks", [P, N_HEADS])
        sink_row = sb("sink_row", [P, 1])
        eps = sb("eps", [P, 1])
        ln_sum = sb("ln_sum", [P, 2, HALF])
        ln_sq = sb("ln_sq", [P, 2, HALF])
        rstd = sb("rstd", [P, HALF])
        warm = sb("warm", [P, 8])
        silu_g = sb("silu_g", [P, 2, HALF])
        h_f32 = sb("h_f32", [P, 2, HALF])
        ffn = ExitStack()
        x_hi = sb("x_hi", [P, KT, TOK], F32R, ffn)
        x_lo = sb("x_lo", [P, KT, TOK], F32R, ffn)
        h_hi = sb("h_hi", [P, FT, TOK], F32R, ffn)
        h_lo = sb("h_lo", [P, FT, TOK], F32R, ffn)
        ffn.close()
        late = ExitStack()
        y_rows = sb("y_rows", [XT, 6, D_MODEL], F32, late)
        g_row = sb("g_row", [XT, D_MODEL], F32, late)
        b_row = sb("b_row", [XT, D_MODEL], F32, late)
        row_stats = sb("row_stats", [XT, 6, 3, 6], F32, late)
        row_mv = sb("row_mv", [XT, 6, 2], F32, late)
        row_std = sb("row_std", [XT, 6], F32, late)
        row_rstd = sb("row_rstd", [XT, 6], F32, late)
        row_shift = sb("row_shift", [XT, 6], F32, late)
        sb("pad_to_h", [P, 2 * KT * TOK - 8 * D_MODEL - 6 * 23], F32, late)
        early = ExitStack()
        x_rows = sb("x_rows", [XT, N_XT, D_MODEL], F32, early)
        sb("pad_to_last_h", [P, (FT - 2) * TOK - N_XT * D_MODEL], F32, early)
        param_rows = sb("param_rows", [60, P], F32, early)
        rel_tab = sb("rel_tab", [N_BUCKETS, N_HEADS], F32, early)
        hot = sb("hot", [N_BUCKETS, T_W], F32, early)
        bias_row = sb("bias_row", [N_HEADS, T_W], F32, early)
        early.close()
        mix_hi = sb("mix_hi", [P, KT, TOK], F32R, late)
        mix_lo = sb("mix_lo", [P, KT, TOK], F32R, late)
        q_t = sb("q_t", [P, GQA, TOK], F32, late)
        k_t = sb("k_t", [P, TOK], F32, late)
        v_t = sb("v_t", [P, TOK], F32, late)
        bias = sb("bias", [P, N_HEADS, SPAN], F32, late)
        bias_s = sb("bias_s", [P, 2, S_COLS], F32, late)
        u_p = sb("u_p", [P, CT, PROMPT + 2], F32, late)
        u_s = sb("u_s", [P, CT, DEC_BATCH, DEC_SEQ + 2], F32, late)
        v_tok = sb("v_tok", [P, 13, P], F32, late)
        kc_t = sb("kc_t", [P, DEC_BATCH, P], F32, late)
        vc = sb("vc", [P, DEC_BATCH, P], F32, late)
        q_diag = sb("q_diag", [P, 2, P], F32, late)
        p_t = sb("p_t", [P, 2, GQA * QMAX], F32, late)
        ut = ExitStack()
        u_rows = sb("u_rows", [DEC_BATCH, 3, D_CONV], F32, ut)
        ut.close()
        taps = sb("taps", [P, 3, HALF], F32, late)
        conv = sb("conv", [P, 2, 2, HALF], F32, late)
        cg_sb = sb("cg_sb", [P, 2, 2, HALF], F32, late)
        row_max = sb("row_max", [P, 3, GQA], F32, late)
        neg_max = sb("neg_max", [P, 3, GQA], F32, late)
        row_sum = sb("row_sum", [P, 3, GQA], F32, late)
        sink_exp = sb("sink_exp", [P, 3, GQA], F32, late)
        r_den = sb("r_den", [P, 3, GQA], F32, late)
        kc = ExitStack()
        kc_rows = sb("kc_rows", [P, DEC_BATCH, P], F32, kc)
        st_rows = sb("st_rows", [DEC_BATCH * 2, D_CONV], F32, kc)
        kc.close()
        probs = sb("probs", [P, 3, GQA, SPAN], F32, late)
        late.close()

        acc = [ctx.enter_context(nc.psum_tensor(f"acc{i}", [P, 512], F32)) for i in range(4)]
        aux = [ctx.enter_context(nc.psum_tensor(f"aux{i}", [P, 512], F32)) for i in range(4)]
        bias_dram = nc.dram_tensor("bias_dram", (N_HEADS, QMAX, T_W), F32, kind="Internal").ap()

        weights_in = [sem(f"weights_in{i}") for i in range(SLOTS)]
        x_in = [sem(f"x_in{i}") for i in range(N_XT)]
        consts_in = sem("consts_in")
        bias_out = sem("bias_out")
        bias_in = sem("bias_in")
        bias_s_in = sem("bias_s_in")
        kc_in = sem("kc_in")
        vc_in = sem("vc_in")
        outputs_out = sem("outputs_out")
        hi_ready = sem("hi_ready")
        lo_ready = sem("lo_ready")
        lo_pool = sem("lo_pool")
        steps_done = sem("steps_done")
        memset_done = sem("memset_done")
        params_t = sem("params_t")
        coef_ready = sem("coef_ready")
        table_ready = sem("table_ready")
        xt_done = sem("xt_done")
        ident_in = sem("ident_in")
        x0_dve = sem("x0_dve")
        x0_act = sem("x0_act")
        x_hi_done = sem("x_hi_done")
        x_ready = sem("x_ready")
        res_biased = sem("res_biased")
        silu_done = sem("silu_done")
        h_done = sem("h_done")
        h_hi_done = sem("h_hi_done")
        h_ready = sem("h_ready")
        r_done = sem("r_done")
        sum_done = sem("sum_done")
        mean_done = sem("mean_done")
        centered = sem("centered")
        squared = sem("squared")
        sq_pool = sem("sq_pool")
        sq_dve = sem("sq_dve")
        var_done = sem("var_done")
        std_done = sem("std_done")
        rstd_done = sem("rstd_done")
        scaled = sem("scaled")
        norm_rows_in = sem("norm_rows_in")
        rows_t = sem("rows_t")
        stats_done = sem("stats_done")
        mv_done = sem("mv_done")
        row_std_done = sem("row_std_done")
        row_rstd_done = sem("row_rstd_done")
        row_shift_done = sem("row_shift_done")
        rows_gained = sem("rows_gained")
        rows_normed = sem("rows_normed")
        rows_pool = sem("rows_pool")
        y_dve = sem("y_dve")
        y_pool = sem("y_pool")
        zero_done = sem("zero_done")
        z_act = sem("z_act")
        z_dve = sem("z_dve")
        kct_done = sem("kct_done")
        kct_copied = sem("kct_copied")
        vt_done = sem("vt_done")
        vt_copied = sem("vt_copied")
        qd_ready = sem("qd_ready")
        taps_done = sem("taps_done")
        taps_added = sem("taps_added")
        gated_hi = sem("gated_hi")
        gated_lo = sem("gated_lo")
        ut_done = sem("ut_done")
        ut_copied = sem("ut_copied")
        scores_done = sem("scores_done")
        masked = sem("masked")
        max_done = sem("max_done")
        max_sink = sem("max_sink")
        neg_ready = sem("neg_ready")
        exps_done = sem("exps_done")
        den_done = sem("den_done")
        rden_done = sem("rden_done")
        probs_ready = sem("probs_ready")
        pt_done = sem("pt_done")
        pt_copied = sem("pt_copied")
        att_done = sem("att_done")
        att_hi = sem("att_hi")
        att_lo = sem("att_lo")

        def cols(half, late=0):
            return slice(N_META if late and not half else half * HALF, (half + 1) * HALF)

        def width(half, late=0):
            return cols(half, late).stop - cols(half, late).start

        def ln_cols(L):
            return cols(L % 2, L >= 2)

        def ln_width(L):
            return width(L % 2, L >= 2)

        G0, B0, C0 = 0, 24, 48

        def z_reader(m):
            return "act" if WI_ORDER[WI_STEPS[m][0]][0] in ("k", "v", "q", "cg") else "dve"

        def z_late(m):
            return WI_ORDER[WI_STEPS[m][0]][0] in ("q", "bg")

        def z_count(m, who):
            return sum(z_reader(i) == who for i in range(m + 1))

        def step_count(kind, c, half):
            return z_count(WI_STEPS.index((WI_ORDER.index((kind, c)), half)), "dve")

        AB = 2 * (WI_GROUPS[0] + WI_GROUPS[1])

        def z_bank(m):
            return m % 4 if m < AB else (m - AB) % 3

        def z_before(m):
            for i in range(m - 1, -1, -1):
                if z_bank(i) == z_bank(m):
                    return i
            return None

        MIXER_OUTS = 2 + 2 + 2 * DEC_BATCH + 3

        WO_STEPS = 2 * KT

        def wo_bank(k):
            return k % 3 if k < KT else k % 4

        def wo_before(k):
            return max(i for i in range(k) if wo_bank(i) == wo_bank(k))

        LN_PIECES = {(1, 2): range(0, 2), (1, 3): range(2, 4), (2, 0): range(4, 6), (2, 1): range(6, 8)}
        WO_PIECES = {10: range(0, 2), 11: range(2, 4), 12: range(4, 6), 13: range(6, 8)}
        POOL_LO = (*range(4), *range(U_WO + 8, U_GU[1] + 4))
        POOL_TILES = 3

        def pool_count(n):
            return POOL_LO.index(n) + 1

        POOL_SUMS = (2, 3)

        def y_bank(t, b):
            return (aux + acc[2:4])[2 * (t % 3) + b]

        STAT_PARTS = ((0, 4), (4, 7), (7, 8))

        def rows_count(t, part):
            return 3 * t + part + 1 if t < 3 else 9 + 3 * part + t - 3 + 1

        def y_units(half, pool):
            return [(3 * half + t, b) for t in range(3) for b in range(2) if (t < 2 and b == 0) == pool]

        def x_bank(part, c):
            return (acc + aux)[c] if part == 0 else aux[c % 4]

        def x_cols(part):
            return slice(X_PARTS[part][0] * XT, (X_PARTS[part][-1] + 1) * XT)

        def squares_of(L, c):
            n = ln_width(L)
            return (ln_sq[:, c % 2, 0:n] if c < 4 else silu_g[:, c - 4, 0:n] if c < 6 else h_f32[:, c - 6, 0:n])

        def copy_v_tiles(act, part):
            act.wait_ge(vt_done, part + 1)
            for i, (slot, src, t0, w) in enumerate(V_TILES[part]):
                last = nc.scalar.activation(v_tok[0:w, slot, :], aux[2 + i // 4][0:w, (i % 4) * P:(i % 4 + 1) * P], ACT.Copy)
            last.then_inc(vt_copied, 1)

        def item_shape(a):
            b, g = ITEMS[a]
            if b == "s":
                return P, 1, S_COLS
            return BLOCKS[b][1], GQA, min(WINDOW, BLOCKS[b][0]) + BLOCKS[b][1]

        def sample_cols(t, rows, h, j):
            at = PROMPT + 16 * j
            return t[rows, h, at:at + 16].rearrange("p (b t) -> p b t", b=4)

        def sample_out(rows, kv, h):
            return acc[3][rows, 0:P].rearrange("p (b g t) -> p b g t", b=4, t=DEC_SEQ)[:, :, GQA * kv + h]

        block = ctx.enter_context(nc.Block())

        @block.sync
        def _(sp):
            def raw_free(n):
                sp.wait_ge(lo_ready, n - SLOTS + 1)
                if n - SLOTS in POOL_LO:
                    sp.wait_ge(lo_pool, pool_count(n - SLOTS))

            def gate_up(f, i, u):
                n0 = U_GU[f] + u
                w = (w_gate, w_up)[u % 2][0, f].rearrange("(k p) n -> p k n", p=P)
                if not isinstance(i, int):
                    sp.wait_ge(lo_ready, n0 + 4 * i - SLOTS + 1)
                elif n0 + 4 * i >= SLOTS:
                    raw_free(n0 + 4 * i)
                sp.dma_start(w_raw[:, n0 % SLOTS, :, :],
                             w[:, :, bass.ds(2 * P * i + (u // 2) * P, P)]).then_inc(weights_in[n0 % SLOTS], 16)

            def down(f, half, c, d):
                n0 = U_DN[f] + (4 * (KT - DN_SHARED) if half else 0) + d
                w = w_down[0, f].rearrange("(k p) n -> p k n", p=P)
                sp.wait_ge(lo_ready, n0 + 4 * c - SLOTS + 1)
                sp.dma_start(w_raw[:, n0 % SLOTS, 0:DN_CUT[d + 1] - DN_CUT[d], :],
                             w[:, DN_CUT[d]:DN_CUT[d + 1], bass.ds(P * c, P)]).then_inc(weights_in[n0 % SLOTS], 16)

            def load_constants():
                for dst, src in ((hot, one_hot), (bias_row, mask_row), (rel_tab, rel_bias),
                                 (param_rows[0:24, :], ln_g[0].rearrange("j (c p) -> (j c) p", p=P)),
                                 (param_rows[24:48, :], ln_b[0].rearrange("j (c p) -> (j c) p", p=P)),
                                 (param_rows[48:60, :], conv_w[0].rearrange("j (c p) -> (j c) p", p=P)),
                                 (sinks[:, :], bass.AP(tensor=attn_sink.tensor, offset=0, ap=[[0, P], [1, N_HEADS]]))):
                    sp.dma_start(dst if isinstance(dst, bass.AP) else dst[:, :], src).then_inc(consts_in, 16)
                for b in range(4):
                    sp.dma_start(sink_row[32 * b:32 * b + 32, :],
                                  bass.AP(tensor=attn_sink.tensor, offset=0,
                                          ap=[[1, N_HEADS], [0, DEC_SEQ], [1, 1]])).then_inc(consts_in, 16)

            def load_tokens(part):
                for t in X_PARTS[part]:
                    first, end = max(t * XT - N_META, 0), min((t + 1) * XT - N_META, SEQ)
                    at = N_META if t == 0 else 0
                    sp.dma_start(x_rows[at:at + end - first, t, :], x_prompt[0, first:end, :]).then_inc(x_in[t], 16)
                    if t == 0:
                        sp.dma_start(x_rows[0:N_META, 0, :], meta_tokens).then_inc(x_in[t], 16)
                    if t == N_XT - 1:
                        sp.dma_start(x_rows[XT - SAMPLE:XT, t, :],
                                     x_sample.rearrange("b t n -> (b t) n")).then_inc(x_in[t], 16)

            def feed_forward(f):
                if f == 0:
                    load_tokens(0)
                for u in range(4):
                    gate_up(f, 0, u)
                if f == 0:
                    load_tokens(1)
                for u in range(4):
                    gate_up(f, 1, u)
                if f == 0:
                    load_constants()
                    sp.wait_ge(table_ready, 1)
                    sp.dma_start(bias_dram, bias_row[:, :].unsqueeze(1).to_broadcast([N_HEADS, QMAX, T_W])
                                 ).then_inc(bias_out, 16)
                with sp.Fori(2, GU_GROUPS) as i:
                    for u in range(4):
                        gate_up(f, i, u)
                for half in range(2):
                    with sp.Fori(DN_SHARED if half else 0, KT) as c:
                        for d in range(4):
                            down(f, half, c, d)
                    if f == 1 and half == 0:
                        sp.wait_ge(steps_done, T_DN[1])
                        for row, src in ((g_row, ln_g), (b_row, ln_b)):
                            sp.dma_start(row[:, :], bass.AP(tensor=src.tensor, offset=2 * D_MODEL, ap=[[0, XT], [1, D_MODEL]])
                                         ).then_inc(norm_rows_in, 16)

            feed_forward(0)
            w_in_k = w_in[0].rearrange("(k p) n -> p k n", p=P)
            for n, (kind, c) in enumerate(WI_ORDER):
                n += U_WI
                raw_free(n)
                if kind == "q":
                    for g in range(N_KV):
                        at = (GQA * g + c) * HEAD_DIM
                        sp.dma_start(w_raw[:, n % SLOTS, :, g * HEAD_DIM:(g + 1) * HEAD_DIM],
                                     w_in_k[:, :, at:at + HEAD_DIM]).then_inc(weights_in[n % SLOTS], 16)
                else:
                    at = COL0[kind] + c * P
                    sp.dma_start(w_raw[:, n % SLOTS, :, :], w_in_k[:, :, at:at + P]).then_inc(weights_in[n % SLOTS], 16)
                if n == U_WI + 7:
                    sp.wait_ge(steps_done, T_WI)
                    sp.dma_start(kc_rows[:, :, :], cache_k[0].rearrange("b s g e -> s b (g e)")).then_inc(kc_in, 16)
                    sp.dma_start(st_rows[:, :], state_conv[0].rearrange("b j n -> (b j) n")).then_inc(kc_in, 16)
                    sp.wait_ge(bias_out, 16)
                    sp.dma_start(bias[0:QMAX, :, :],
                                 bass.AP(tensor=bias_dram.tensor, offset=WINDOW - 1,
                                         ap=[[T_W - 1, QMAX], [QMAX * T_W, N_HEADS], [1, SPAN]])).then_inc(bias_in, 16)
                    for b in range(4):
                        rows = slice(32 * b, 32 * b + 32)
                        for j in range(2):
                            sp.dma_start(bias_s[rows, j, 0:WINDOW],
                                         bass.AP(tensor=bias_dram.tensor, offset=WINDOW - 1,
                                                 ap=[[QMAX * T_W, N_HEADS], [T_W - 1, DEC_SEQ], [1, WINDOW]])).then_inc(bias_s_in, 16)
                    sp.wait_ge(zero_done, 2)
                    for b in range(4):
                        rows = slice(32 * b, 32 * b + 32)
                        for j in range(2):
                            at = WINDOW + (4 * j + b) * DEC_SEQ
                            sp.dma_start(bias_s[rows, j, at:at + DEC_SEQ],
                                         bass.AP(tensor=bias_dram.tensor, offset=2 * WINDOW - 1,
                                                 ap=[[QMAX * T_W, N_HEADS], [T_W - 1, DEC_SEQ], [1, DEC_SEQ]])).then_inc(bias_s_in, 16)
                    sp.dma_start(vc[:, :, :], cache_v[0].rearrange("b s g e -> s b (g e)")).then_inc(vc_in, 16)
                    for new, old in ((new_k_sample, cache_k), (new_v_sample, cache_v)):
                        sp.dma_start(new[0][:, 0:WINDOW - DEC_SEQ], old[0][:, DEC_SEQ:WINDOW]).then_inc(outputs_out, 16)
            for n in range(U_WO, U_GU[1]):
                c = (n - U_WO) % KT
                raw_free(n)
                for g in range(N_KV):
                    src = w_out[0][g * GQA * HEAD_DIM:(g + 1) * GQA * HEAD_DIM, c * P:(c + 1) * P]
                    sp.dma_start(w_raw[g * HEAD_DIM:(g + 1) * HEAD_DIM, n % SLOTS, 0:GQA, :],
                                 src.rearrange("(k p) n -> p k n", p=HEAD_DIM)).then_inc(weights_in[n % SLOTS], 16)
                sp.dma_start(w_raw[:, n % SLOTS, GQA:KT, :],
                             w_out[0][D_ATTN:, c * P:(c + 1) * P].rearrange("(k p) n -> p k n", p=P)
                             ).then_inc(weights_in[n % SLOTS], 16)
            n_out = MIXER_OUTS
            sp.wait_ge(vt_copied, 2)
            kv = slice(0, N_KV * HEAD_DIM)
            sp.dma_start(new_k_prompt[0, 0].rearrange("s g e -> s (g e)"), v_tok[:, 10, kv]).then_inc(outputs_out, 16)
            sp.dma_start(new_v_prompt[0, 0].rearrange("s g e -> s (g e)"), v_tok[:, 11, kv]).then_inc(outputs_out, 16)
            for new, at in ((new_k_sample, 12), (new_v_sample, 9)):
                for b in range(DEC_BATCH):
                    sp.dma_start(new[0, b, WINDOW - DEC_SEQ:].rearrange("t g e -> t (g e)"),
                                 v_tok[b * DEC_SEQ:(b + 1) * DEC_SEQ, at, kv]).then_inc(outputs_out, 16)
            sp.wait_ge(ut_copied, 3)
            for j in range(2):
                sp.dma_start(new_conv_sample[0][:, j, :], u_rows[:, j, :]).then_inc(outputs_out, 16)
            sp.dma_start(new_conv_prompt[0, 0], u_rows[0:2, 2, :]).then_inc(outputs_out, 16)
            feed_forward(1)
            for half in range(2):
                d, g = y_units(half, False), y_units(half, True)
                for t, b in d[:2] + g[:1] + d[2:] + g[1:]:
                    _, t0, w = Y_TILES[t]
                    feats = slice(b * D_MODEL // 2, (b + 1) * D_MODEL // 2)
                    made, units = (y_pool, y_units(half, True)) if (t, b) in y_units(half, True) else (y_dve, y_units(half, False))
                    sp.wait_ge(made, len(units) * half + units.index((t, b)) + 1)
                    first, end = max(t0, N_META), min(t0 + w, PROMPT)
                    sp.dma_start(y_prompt[0, first - N_META:end - N_META, feats],
                                 y_rows[first - t0:end - t0, t, feats]).then_inc(outputs_out, 16)
                    n_out += 1
                    if t0 + w > PROMPT:
                        sp.dma_start(y_sample.rearrange("b t n -> (b t) n")[:, feats],
                                     y_rows[PROMPT - t0:w, t, feats]).then_inc(outputs_out, 16)
                        n_out += 1
            sp.wait_ge(outputs_out, 16 * n_out)


        @block.tensor
        def _(pe):
            def products(out, slot, ks, rhs_hi, rhs_lo, n, t0=0, ends=(0, KT - 1)):
                for t, k in enumerate(ks, t0):
                    for w, x in ((w_hi, rhs_hi), (w_hi, rhs_lo), (w_lo, rhs_hi)):
                        mm = nc.tensor.matmul(out[:, 0:n], w[:, slot, t, :], x(k),
                                              start=(k == ends[0] and w is w_hi and x is rhs_hi),
                                              stop=(k == ends[1] and w is w_lo))
                return mm

            def unit_split(n):
                pe.wait_ge(lo_ready, n + 1)
                if n in POOL_LO:
                    pe.wait_ge(lo_pool, pool_count(n))

            def operands(hi, lo, half, late):
                return (lambda k: hi[:, k, cols(half, late)]), (lambda k: lo[:, k, cols(half, late)]), width(half, late)

            def x_operands(half, late):
                return operands(x_hi, x_lo, half, late)

            def ln_mean(L):
                half = L % 2
                pe.wait_ge(sum_done, sum_count(L, KT - 2))
                pe.wait_ge(r_done, r_count(L, KT - 1))
                if L >= 1:
                    pe.wait_ge(centered, KT * L)
                nc.tensor.matmul(aux[0][:, 0:ln_width(L)], mean_of[:, :], ln_sum[:, half, 0:ln_width(L)], start=True, stop=False)
                nc.tensor.matmul(aux[0][:, 0:ln_width(L)], mean_of[:, :], x_res[:, KT - 1, ln_cols(L)],
                                 start=False, stop=True).then_inc(mean_done, 1)

            def ln_var(L):
                pe.wait_ge(sq_pool, 3 * (L + 1))
                pe.wait_ge(sq_dve, 3 * (L + 1))
                if L >= 1:
                    pe.wait_ge(std_done, L)
                nc.tensor.matmul(aux[1][:, 0:ln_width(L)], mean_of[:, :], ln_sum[:, L % 2, 0:ln_width(L)], start=True, stop=False)
                nc.tensor.matmul(aux[1][:, 0:ln_width(L)], mean_of[:, :], squares_of(L, 4),
                                 start=False, stop=True).then_inc(var_done, 1)

            def transpose_rows(half, chunks):
                order = ([(t, c) for t in range(3) for c in range(KT)] if half == 0 else
                         [(t, c) for c in chunks for t in range(3, 6)])
                for t, c in order:
                    pe.wait_ge(r_done, r_count(4 + half, c))
                    _, t0, w = Y_TILES[t]
                    tr = nc.tensor.transpose(y_bank(t, c // 4)[0:w, (c % 4) * P:(c % 4 + 1) * P],
                                             x_res[:, c, t0:t0 + w], ident[:, :])
                    if c + 1 in [end for _, end in STAT_PARTS]:
                        tr.then_inc(rows_t, 1)

            def unit_pair(n, accs, half, x0, run=1, chunks=range(KT)):
                x = x_operands(half, 0)
                for k0 in chunks[::run]:
                    for u in range(2):
                        if k0 == 0:
                            unit_split(n + u)
                        for k in range(k0, k0 + run):
                            pe.wait_ge(x_ready, x0 + k + 1)
                            mm = products(accs[u], (n + u) % SLOTS, range(k, k + 1), *x, t0=k)
                        if k == KT - 1:
                            mm.then_inc(steps_done, 1)

            def parameters():
                pe.wait_ge(consts_in, 16 * N_CONSTS)
                pe.wait_ge(x0_dve, KT)
                pe.wait_ge(x0_act, KT)
                nc.tensor.transpose(aux[0][:, 0:60], param_rows[:, :], ident[0:60, 0:60]).then_inc(params_t, 1)
                nc.tensor.matmul(aux[1][0:N_HEADS, 0:T_W], rel_tab[:, :], hot[:, :],
                                 start=True, stop=True).then_inc(params_t, 1)

            def gate_up_first(f):
                if f == 0:
                    unit_pair(0, acc[0:2], 0, 0, run=4)
                    tokens(1, range(0, 4))
                    unit_pair(2, acc[2:4], 0, 0, run=4, chunks=range(0, 4))
                    tokens(1, range(4, KT))
                    unit_pair(2, acc[2:4], 0, 0, run=4, chunks=range(4, KT))
                else:
                    for v in range(4):
                        n = U_GU[f] + v
                        unit_split(n)
                        pe.wait_ge(r_done, r_count(3, KT - 4 + v))
                        for k in range(KT):
                            if v == 0:
                                pe.wait_ge(x_ready, 4 * KT + k + 1)
                            mm = products(acc[v], n % SLOTS, range(k, k + 1), *x_operands(0, f), t0=k)
                            if (v, k) == (0, 3):
                                ln_mean(3)
                            if (v, k) == (2, 2):
                                ln_var(3)
                        mm.then_inc(steps_done, 1)
                for u in (0, 2):
                    pe.wait_ge(silu_done, 44 * f + u // 2 + 1)
                    pe.wait_ge(h_done, 44 * f + u // 2 + 1)
                    unit_pair(U_GU[f] + u, acc[u:u + 2], 1, KT if f == 0 else 2 * KT + KT * 3)

            def gate_up_group(f, i):
                for half in range(2):
                    x = x_operands(half, f)
                    for u in range(4):
                        n0 = U_GU[f] + u
                        if half == 0:
                            pe.wait_ge(lo_ready, n0 + 4 * i + 1)
                        m0 = 44 * f + 2 * half + u // 2
                        pe.wait_ge((silu_done, h_done)[u % 2], m0 + 4 * i - 1)
                        products(acc[u], n0 % SLOTS, range(KT), *x).then_inc(steps_done, 1)

            def down_unit(f, half, bank, d, n, more=0):
                pe.wait_ge(lo_ready, n + 1 + more)
                h = operands(h_hi, h_lo, half, f)
                products(acc[bank], n % SLOTS, range(DN_CUT[d], DN_CUT[d + 1]), *h,
                         ends=(0, FT - 1)).then_inc(steps_done, 1)

            def down(f):
                pe.wait_ge(h_ready, 44 * f + 40)
                pe.wait_ge(silu_done, 44 * f + 43)
                pe.wait_ge(h_done, 44 * f + 43)
                r0 = R_FREE + 4 * KT * f
                with pe.Fori(0, DN_SHARED // 2) as i:
                    for c2 in range(2):
                        for d in range(4):
                            for half in range(2):
                                if d == 0:
                                    pe.wait_ge(r_done, r0 - 4 + 2 * c2 + half + 1 + 4 * i)
                                if d == 3:
                                    pe.wait_ge(h_ready, 44 * f + 42 + 2 * half)
                                down_unit(f, half, 2 * c2 + half, d, U_DN[f] + 4 * c2 + d, 8 * i)
                with pe.Fori(0, (KT - DN_SHARED) // 2) as i:
                    for c2 in range(2):
                        pe.wait_ge(r_done, r0 + 2 * DN_SHARED + c2 - 1 + 2 * i)
                        for d in range(4):
                            down_unit(f, 0, c2, d, U_DN[f] + 4 * (DN_SHARED + c2) + d, 8 * i)
                for c in range(DN_SHARED, KT):
                    pe.wait_ge(r_done, r_count(4 * f + 1, c) - 2)
                    for d in range(4):
                        down_unit(f, 1, c % 2, d, U_DN[f] + 4 * (KT - DN_SHARED + c) + d)
                        e = (c - DN_SHARED, d)
                        if f == 0 and e == (0, 0):
                            ln_mean(0)
                        if f == 0 and e == (1, 1):
                            ln_var(0)
                        if f == 1 and e == (0, 1):
                            transpose_rows(0, range(KT))
                        if f == 1 and e == (3, 1):
                            pe.wait_ge(rows_gained, len(y_units(0, False)))
                            pe.wait_ge(rows_normed, len(y_units(0, True)))
                            transpose_rows(1, range(0, KT - 1))

            def feed_forward(f):
                gate_up_first(f)
                if f == 0:
                    parameters()
                with pe.Fori(1, GU_GROUPS) as i:
                    gate_up_group(f, i)
                down(f)

            def tokens(part, chunks):
                for i, t in enumerate(X_PARTS[part]):
                    pe.wait_ge(x_in[t], 16 * X_DMAS[t])
                    for c in chunks:
                        if part == 0 and t == X_PARTS[0][-1] and c == KT - 1:
                            keep_busy(8)
                        if part and i == 0:
                            pe.wait_ge((x0_dve, x0_act)[c % 2], (KT + c) // 2 - 1)
                        tr = nc.tensor.transpose(x_bank(part, c)[:, i * XT:(i + 1) * XT], x_rows[:, t, c * P:(c + 1) * P],
                                                 ident[0:XT, 0:XT])
                        if t == X_PARTS[part][-1]:
                            tr.then_inc(xt_done, 1)

            def keep_busy(n):
                for _ in range(n):
                    nc.tensor.matmul(aux[3][:, 384:384 + P], mean_of[:, :], mean_of[:, :], start=True, stop=True)

            pe.wait_ge(memset_done, 2)
            keep_busy(7)
            pe.wait_ge(ident_in, 16)
            tokens(0, range(KT))
            feed_forward(0)

            def wi_step(m):
                u, half = WI_STEPS[m]
                n = U_WI + u
                unit_split(n)
                before = z_before(m)
                if before is not None:
                    who = z_reader(before)
                    pe.wait_ge(z_act if who == "act" else z_dve, z_count(before, who))
                if m < 4:
                    pe.wait_ge(r_done, r_count(1, KT - 1 - (m == 0)))
                x = x_operands(half, z_late(m))
                for k in range(KT):
                    mm = products(acc[z_bank(m)], n % SLOTS, range(k, k + 1), *x, t0=k)
                    if (m, k) == (0, 1):
                        ln_mean(1)
                    if (m, k) == (2, 1):
                        ln_var(1)
                mm.then_inc(steps_done, 1)

            def cache_transposes():
                pe.wait_ge(kc_in, 32)
                pe.wait_ge(std_done, 2)
                pe.wait_ge(centered, 2 * KT)
                for b in range(DEC_BATCH):
                    nc.tensor.transpose(aux[b // 4][:, (b % 4) * P:(b % 4 + 1) * P], kc_rows[:, b, :], ident[:, :])
                for c in range(CT):
                    tr = nc.tensor.transpose(aux[2][:, c * 16:(c + 1) * 16], st_rows[:, c * P:(c + 1) * P],
                                             ident[0:16, 0:16])
                tr.then_inc(kct_done, 1)

            def v_transposes(part):
                pe.wait_ge(z_act, z_count(Z_KV[part], "act"))
                if part == 0:
                    pe.wait_ge(kct_copied, 1)
                else:
                    pe.wait_ge(vt_copied, 1)
                for i, (slot, src, t0, w) in enumerate(V_TILES[part]):
                    tr = nc.tensor.transpose(aux[2 + i // 4][0:w, (i % 4) * P:(i % 4 + 1) * P],
                                             (k_t if src == "k" else v_t)[:, t0:t0 + w], ident[:, :])
                tr.then_inc(vt_done, 1)

            def scores(a):
                b, g = ITEMS[a]
                if a >= 1:
                    pe.wait_ge(masked, a)
                if b == "s":
                    pe.wait_ge(qd_ready, 1)
                    nc.tensor.matmul(aux[0][:, WINDOW:S_COLS], q_diag[:, g, :], k_t[:, PROMPT:TOK],
                                     start=True, stop=True)
                    for i in range(4):
                        rows = slice(32 * i, 32 * i + 32)
                        mm = nc.tensor.matmul(aux[0][rows, 0:WINDOW], q_diag[:, g, rows], kc_t[:, 4 * g + i, :],
                                              start=True, stop=True)
                else:
                    q0, nq = BLOCKS[b]
                    la = min(WINDOW, q0)
                    if a == 0:
                        pe.wait_ge(z_act, z_count(AB - 1, "act"))
                        pe.wait_ge(zero_done, 2)
                        pe.wait_ge(kct_copied, 1)
                    head = slice(g * HEAD_DIM, (g + 1) * HEAD_DIM)
                    for h in range(GQA):
                        mm = nc.tensor.matmul(aux[h // 2][0:nq, (h % 2) * 256:(h % 2) * 256 + la + nq],
                                              q_t[head, h, q0:q0 + nq], k_t[head, q0 - la:q0 + nq],
                                              start=True, stop=True)
                mm.then_inc(scores_done, 1)

            def prob_transposes(a):
                b, g = ITEMS[a]
                pe.wait_ge(probs_ready, a + 1)
                pe.wait_ge(pt_copied, 2 * a) if a else pe.wait_ge(vt_copied, 2)
                if b == "s":
                    nc.tensor.transpose(aux[2][:, 0:P], probs[:, a % 3, 0, 0:WINDOW], ident[:, :])
                    tr = nc.tensor.transpose(aux[3][0:SAMPLE, 0:P], probs[:, a % 3, 0, WINDOW:S_COLS], ident[:, :])
                else:
                    q0, nq = BLOCKS[b]
                    la = min(WINDOW, q0)
                    for h in range(GQA):
                        if la:
                            nc.tensor.transpose(aux[2][0:la, h * nq:(h + 1) * nq], probs[0:nq, a % 3, h, 0:la],
                                                ident[0:nq, 0:nq])
                        tr = nc.tensor.transpose(aux[3][0:nq, h * nq:(h + 1) * nq], probs[0:nq, a % 3, h, la:la + nq],
                                                 ident[0:nq, 0:nq])
                tr.then_inc(pt_done, 1)

            def values(a):
                b, g = ITEMS[a]
                pe.wait_ge(pt_copied, 2 * a + 2)
                if a >= 1:
                    pe.wait_ge(att_lo, a)
                else:
                    pe.wait_ge(z_act, z_count(AB - 1, "act"))
                if b == "s":
                    if g == 0:
                        pe.wait_ge(vc_in, 16)
                    nc.tensor.matmul(acc[3][:, 0:P], v_tok[0:SAMPLE, 9, :], p_t[0:SAMPLE, 1, 0:P],
                                     start=True, stop=False)
                    for i in range(4):
                        rows = slice(32 * i, 32 * i + 32)
                        mm = nc.tensor.matmul(acc[3][:, rows], vc[:, 4 * g + i, :], p_t[:, 0, rows],
                                              start=False, stop=i == 3)
                else:
                    q0, nq = BLOCKS[b]
                    la = min(WINDOW, q0)
                    if la:
                        nc.tensor.matmul(acc[3][:, 0:GQA * nq], v_tok[0:la, 2 * b - 1, :], p_t[0:la, 0, 0:GQA * nq],
                                         start=True, stop=False)
                    mm = nc.tensor.matmul(acc[3][:, 0:GQA * nq], v_tok[0:nq, 2 * b, :], p_t[0:nq, 1, 0:GQA * nq],
                                          start=not la, stop=True)
                mm.then_inc(att_done, 1)

            def attention_slot(k):
                if k < len(ITEMS):
                    scores(k)
                if 2 <= k < len(ITEMS) + 2:
                    prob_transposes(k - 2)
                if 3 <= k < len(ITEMS) + 3:
                    values(k - 3)

            pe.wait_ge(x_ready, 3 * KT)
            for m in range(4):
                wi_step(m)
            for u in (0, 2):
                pe.wait_ge(z_act, u + 2)
                unit_pair(U_WI + u, acc[u:u + 2], 1, 3 * KT)
            cache_transposes()
            for m in range(2 * WI_GROUPS[0], len(WI_STEPS)):
                wi_step(m)
                if m == PREP + 1:
                    v_transposes(0)
                if m == PREP + 3:
                    v_transposes(1)
                if m > AB and (m - AB) % 2 == 1:
                    attention_slot((m - AB) // 2)

            for k in range(WO_STEPS):
                half, n = k // KT, U_WO + k
                unit_split(n)
                if k % KT == 0:
                    pe.wait_ge(gated_lo, 6 + 2 * half)
                    pe.wait_ge(att_lo, (ITEMS_H0, len(ITEMS))[half])
                if k >= 3 and k != 11:
                    pe.wait_ge(r_done, r_count(2, wo_before(k)))
                elif k < 3:
                    before = len(WI_STEPS) - 3 + k
                    pe.wait_ge(z_act if z_reader(before) == "act" else z_dve, z_count(before, z_reader(before)))
                mix = operands(mix_hi, mix_lo, half, 1)
                products(acc[wo_bank(k)], n % SLOTS, range(0, 2), *mix)
                if k == 8:
                    ln_mean(2)
                if k == 10:
                    pe.wait_ge(ut_copied, 3)
                    ln_var(2)
                products(acc[wo_bank(k)], n % SLOTS, range(2, KT), *mix, t0=2).then_inc(steps_done, 1)
                if k in (1, 3, 5):
                    attention_slot((len(WI_STEPS) - AB + k) // 2)
                if k == 6:
                    pe.wait_ge(pt_copied, 2 * len(ITEMS))
                    for ch in range(CT):
                        for j in range(2):
                            nc.tensor.transpose(aux[2 + j][0:DEC_BATCH, ch * P:(ch + 1) * P],
                                                u_s[:, ch, :, DEC_SEQ + j], ident[:, :])
                        tr = nc.tensor.transpose(aux[1][0:2, ch * P:(ch + 1) * P],
                                                 u_p[:, ch, PROMPT:PROMPT + 2], ident[:, :])
                    tr.then_inc(ut_done, 1)
            feed_forward(1)
            transpose_rows(1, range(KT - 1, KT))


        @block.scalar
        def _(act):
            def weight_hi(n):
                tiles = tiles_of(n)
                act.wait_ge(weights_in[n % SLOTS], ARRIVED[n])
                if n >= SLOTS:
                    act.wait_ge(steps_done, free_after(n - SLOTS))
                nc.scalar.activation(w_hi[:, n % SLOTS, 0:tiles, :], w_raw[:, n % SLOTS, 0:tiles, :],
                                     ACT.Copy).then_inc(hi_ready, 1)

            def gate_up_hi(f, i, u):
                n0 = U_GU[f] + 4 + u
                act.wait_ge(weights_in[n0 % SLOTS], ARRIVED[n0] + 16 * i)
                act.wait_ge(steps_done, free_after(n0 - SLOTS) + 8 * i)
                nc.scalar.activation(w_hi[:, n0 % SLOTS, :, :], w_raw[:, n0 % SLOTS, :, :],
                                     ACT.Copy).then_inc(hi_ready, 1)

            def silu(f, i, half, ab, first=False):
                m0 = 44 * f + 2 * half + ab
                act.wait_ge(steps_done, T_GU[f] + 4 * half + 2 * ab + 1 + 8 * i)
                if m0 >= 2 or not first:
                    act.wait_ge(h_done, m0 - 1 + 4 * i)
                nc.scalar.activation(silu_g[:, ab, 0:width(half, f)], acc[2 * ab][:, 0:width(half, f)], ACT.Silu).then_inc(silu_done, 1)

            def hidden_hi(f, i, half, ab):
                m0 = 44 * f + 2 * half + ab
                act.wait_ge(h_done, m0 + 1 + 4 * i)
                nc.scalar.activation(h_hi[:, bass.ds(2 * i + ab, 1), cols(half, f)], h_f32[:, ab:ab + 1, 0:width(half, f)],
                                     ACT.Copy).then_inc(h_hi_done, 1)

            def gate_up_group(f, i, split, first=False, ahead=0):
                if ahead < 1:
                    silu(f, i, 0, 0, first)
                hidden_hi(f, i, 0, 0)
                if ahead < 2:
                    silu(f, i, 0, 1, first)
                hidden_hi(f, i, 0, 1)
                silu(f, i, 1, 0)
                split(0)
                hidden_hi(f, i, 1, 0)
                split(1)
                silu(f, i, 1, 1)
                split(2)
                hidden_hi(f, i, 1, 1)
                split(3)

            def ln_square(L, chunks=range(KT)):
                for c in chunks:
                    act.wait_ge(centered, KT * L + c + 1)
                    if c < 4 and 3 * L + c // 2:
                        act.wait_ge(sq_pool, 3 * L + c // 2)
                    nc.scalar.activation(squares_of(L, c), x_res[:, c, ln_cols(L)], ACT.Square).then_inc(squared, 1)

            def sqrt_table(L):
                nc.scalar.activation(warm[:, L:L + 1], eps[:, :], ACT.Sqrt)

            def ln_std(L):
                act.wait_ge(var_done, L + 1)
                if L >= 1:
                    act.wait_ge(scaled, KT * L)
                nc.scalar.activation(rstd[:, 0:ln_width(L)], aux[1][:, 0:ln_width(L)], ACT.Sqrt, bias=eps[:, :]).then_inc(std_done, 1)

            def ln_hi(L, chunks):
                for c in chunks:
                    act.wait_ge(scaled, 8 * L + c + 1)
                    b = B0 + 8 * (L // 2) + c
                    nc.scalar.activation(x_hi[:, c, ln_cols(L)], x_res[:, c, ln_cols(L)], ACT.Identity,
                                         bias=coef[:, b:b + 1]).then_inc(x_hi_done, 1)

            def rows_std(t):
                w = Y_TILES[t][2]
                act.wait_ge(mv_done, t + 1)
                nc.scalar.activation(row_std[0:w, t:t + 1], row_mv[0:w, t, 1:2], ACT.Sqrt, bias=eps[0:w, :]
                                     ).then_inc(row_std_done, 1)

            def rows_norm(t, b):
                w = Y_TILES[t][2]
                act.wait_ge(row_shift_done, t + 1)
                act.wait_ge(rows_t, rows_count(t, b))
                nc.scalar.activation(y_rows[0:w, t, 512 * b:512 * b + 512], y_bank(t, b)[0:w, :], ACT.Identity,
                                     scale=row_rstd[0:w, t:t + 1], bias=row_shift[0:w, t:t + 1]).then_inc(rows_normed, 1)

            def down(f):
                for n0, steps, chunks in ((U_DN[f] + 4, 8, DN_SHARED), (U_DN[f] + 4 * DN_SHARED + 4, 4, KT - DN_SHARED)):
                    with act.Fori(0, chunks) as c:
                        for d in range(4):
                            n = n0 + d
                            act.wait_ge(weights_in[n % SLOTS], ARRIVED[n] + 16 * c)
                            act.wait_ge(steps_done, free_after(n - SLOTS) + steps * c)
                            nc.scalar.activation(w_hi[:, n % SLOTS, 0:tiles_of(n), :],
                                                 w_raw[:, n % SLOTS, 0:tiles_of(n), :], ACT.Copy).then_inc(hi_ready, 1)
                for c in range(KT - DN_SHARED):
                    for d in range(4):
                        n = U_DN[f] + 4 * (KT + c + 1) + d
                        if n < (U_WI + 2, U_END)[f]:
                            weight_hi(n)
                        if f == 1:
                            if (c, d) == (1, 3):
                                for t in range(3):
                                    rows_std(t)
                            if c == 2 and d < 2:
                                rows_norm(*y_units(0, True)[d])
                            continue
                        if (c, d) in ((0, 1), (0, 2)):
                            ln_square(0, range(4 * d - 4, 4 * d))
                        if (c, d) == (0, 3):
                            sqrt_table(0)
                        if (c, d) == (1, 1):
                            ln_std(0)
                        if (c, d) in LN_PIECES:
                            ln_hi(0, LN_PIECES[c, d])

            def feed_forward(f):
                if f == 1:
                    ln_square(3)
                    sqrt_table(3)
                    ln_std(3)
                    silu(f, 0, 0, 0)
                    ln_hi(3, range(0, 4))
                    silu(f, 0, 0, 1)
                    ln_hi(3, range(4, KT))
                    act.wait_ge(outputs_out, 16 * MIXER_OUTS)
                gate_up_group(f, 0, lambda u: gate_up_hi(f, 0, u), first=f == 0, ahead=f + 1)
                with act.Fori(1, GU_GROUPS - 1) as i:
                    gate_up_group(f, i, lambda u: gate_up_hi(f, i, u))
                if f == 0:
                    act.wait_ge(bias_out, 16)
                gate_up_group(f, GU_GROUPS - 1, lambda u: weight_hi(U_DN[f] + u))
                down(f)

            act.dma_start(ident[:, :], identity).then_inc(ident_in, 16)
            def token_copy(part, c):
                cs = x_cols(part)
                act.wait_ge(xt_done, KT * part + c + 1)
                nc.scalar.activation(x_res[:, c, cs], x_bank(part, c)[:, 0:cs.stop - cs.start], ACT.Copy).then_inc(x0_act, 1)

            def token_hi(part, c):
                cs = x_cols(part)
                act.wait_ge((x0_dve, x0_act)[c % 2], (KT * part + c) // 2 + 1)
                nc.scalar.activation(x_hi[:, c, cs], x_res[:, c, cs], ACT.Copy).then_inc(x_hi_done, 1)

            act.wait_ge(memset_done, 2)
            nc.scalar.activation(warm[:, 7:8], eps[:, :], ACT.Silu)
            for c in range(1, KT, 2):
                token_copy(0, c)
                token_hi(0, c - 1)
                if c == 1:
                    weight_hi(0)
                token_hi(0, c)
                if c == 3:
                    weight_hi(1)
            weight_hi(2)
            weight_hi(3)
            for c in range(1, KT, 2):
                token_copy(1, c)
                token_hi(1, c - 1)
                token_hi(1, c)
                if c == 3:
                    silu(0, 0, 0, 0, first=True)
            feed_forward(0)


            def evacuate(m):
                u, half = WI_STEPS[m]
                kind, c = WI_ORDER[u]
                act.wait_ge(steps_done, T_WI + m + 1)
                src = acc[z_bank(m)][:, 0:width(half, z_late(m))]
                if kind == "cg":
                    if c >= 2:
                        act.wait_ge(z_dve, step_count("h", c - 2, half))
                    dst = cg_sb[:, half, c % 2, :]
                else:
                    dst = {"k": k_t, "v": v_t}[kind][:, cols(half)] if kind != "q" else q_t[:, c, cols(half, 1)]
                nc.scalar.activation(dst, src, ACT.Copy).then_inc(z_act, 1)

            def gate_hi(m):
                u, half = WI_STEPS[m]
                c = WI_ORDER[u][1]
                e = BG_ORDER.index((c, half))
                act.wait_ge(z_dve, z_count(m, "dve"))
                nc.scalar.activation(mix_hi[:, 4 + c, cols(half, 1)], h_f32[:, e % 2, 0:width(half, 1)], ACT.Copy
                                     ).then_inc(gated_hi, 1)

            def copy_probs(a):
                b, g = ITEMS[a]
                act.wait_ge(pt_done, a + 1)
                if a >= 1:
                    act.wait_ge(att_done, a)
                if b == "s":
                    nc.scalar.activation(p_t[:, 0, 0:P], aux[2][:, 0:P], ACT.Copy).then_inc(pt_copied, 1)
                    nc.scalar.activation(p_t[0:SAMPLE, 1, 0:P], aux[3][0:SAMPLE, 0:P], ACT.Copy).then_inc(pt_copied, 1)
                    return
                q0, nq = BLOCKS[b]
                la = min(WINDOW, q0) or nq
                src = aux[2] if q0 else aux[3]
                nc.scalar.activation(p_t[0:la, 0, 0:GQA * nq], src[0:la, 0:GQA * nq], ACT.Copy).then_inc(pt_copied, 1)
                nc.scalar.activation(p_t[0:nq, 1, 0:GQA * nq], aux[3][0:nq, 0:GQA * nq], ACT.Copy).then_inc(pt_copied, 1)

            def attended_hi(a):
                b, g = ITEMS[a]
                act.wait_ge(att_done, a + 1)
                if b == "s":
                    for kv in range(N_KV):
                        rows = slice(kv * HEAD_DIM, (kv + 1) * HEAD_DIM)
                        for h in range(GQA):
                            hi = nc.scalar.activation(sample_cols(mix_hi, rows, h, g), sample_out(rows, kv, h), ACT.Copy)
                else:
                    q0, nq = BLOCKS[b]
                    rows = slice(g * HEAD_DIM, (g + 1) * HEAD_DIM)
                    hi = nc.scalar.activation(mix_hi[rows, 0:GQA, q0:q0 + nq],
                                              acc[3][rows, 0:GQA * nq].rearrange("p (h q) -> p h q", h=GQA), ACT.Copy)
                hi.then_inc(att_hi, 1)

            def exps(a):
                b, g = ITEMS[a]
                act.wait_ge(neg_ready, a + 1)
                rows, heads, span = item_shape(a)
                for h in range(heads):
                    nc.scalar.activation(probs[0:rows, a % 3, h, 0:span], probs[0:rows, a % 3, h, 0:span], ACT.Exp,
                                         bias=neg_max[0:rows, a % 3, h:h + 1], accum_out=row_sum[0:rows, a % 3, h:h + 1])
                for h in range(heads):
                    sk = sink_row[:, :] if b == "s" else sinks[0:rows, 4 * g + h:4 * g + h + 1]
                    e = nc.scalar.activation(sink_exp[0:rows, a % 3, h:h + 1], sk, ACT.Exp,
                                             bias=neg_max[0:rows, a % 3, h:h + 1])
                e.then_inc(exps_done, 1)

            def attention(k, odd):
                if odd:
                    if 2 <= k < len(ITEMS) + 2:
                        copy_probs(k - 2)
                    if 3 <= k < len(ITEMS) + 3:
                        attended_hi(k - 3)
                elif 1 <= k < len(ITEMS) + 1:
                    exps(k - 1)

            def split_after(step):
                for n in range(U_WI + SLOTS, U_GU[1] + SLOTS):
                    if free_after(n - SLOTS) == step + 1:
                        weight_hi(n)

            weight_hi(U_WI + 2)
            ln_square(1)
            sqrt_table(1)
            weight_hi(U_WI + 3)
            evacuate(0)
            evacuate(1)
            ln_std(1)
            evacuate(2)
            ln_hi(1, range(0, 4))
            evacuate(3)
            ln_hi(1, range(4, KT))
            for m in range(4, len(WI_STEPS)):
                kind = WI_ORDER[WI_STEPS[m][0]][0]
                if m >= AB and (m - AB) % 2 == 0:
                    attention((m - AB) // 2, odd=False)
                if kind == "bg":
                    gate_hi(m)
                elif kind != "h":
                    evacuate(m)
                split_after(T_WI + m)
                if m == PREP:
                    act.wait_ge(kct_done, 1)
                    for i in range(2):
                        nc.scalar.activation(kc_t[:, 4 * i:4 * i + 4, :],
                                             aux[i][:, :].rearrange("p (b s) -> p b s", b=4), ACT.Copy)
                    nc.scalar.activation(u_s[:, :, :, 0:2], aux[2][:, 0:64].rearrange("p (c b j) -> p c b j", c=CT, b=DEC_BATCH),
                                         ACT.Copy).then_inc(kct_copied, 1)
                if m == PREP + 1:
                    copy_v_tiles(act, 0)
                if m == PREP + 3:
                    copy_v_tiles(act, 1)
                if m > AB and (m - AB) % 2 == 1:
                    attention((m - AB) // 2, odd=True)

            for k in range(WO_STEPS):
                s = len(WI_STEPS) - AB + k
                if s % 2 == 0:
                    attention(s // 2, odd=False)
                if k == 8:
                    ln_square(2)
                    sqrt_table(2)
                if k == 9:
                    ln_std(2)
                split_after(T_WO + k)
                if s % 2:
                    attention(s // 2, odd=True)
                if k == 6:
                    act.wait_ge(ut_done, 1)
                    for j in range(2):
                        nc.scalar.activation(u_rows[:, j, :], aux[2 + j][0:DEC_BATCH, :], ACT.Copy).then_inc(ut_copied, 1)
                    nc.scalar.activation(u_rows[0:2, 2, :], aux[1][0:2, :], ACT.Copy).then_inc(ut_copied, 1)
                if k in WO_PIECES:
                    ln_hi(2, WO_PIECES[k])
            feed_forward(1)
            rows_std(3)
            rows_std(4)
            rows_norm(*y_units(1, True)[0])
            rows_std(5)
            rows_norm(*y_units(1, True)[1])


        @block.vector
        def _(dve):
            def weight_lo(n, i=0):
                tiles = tiles_of(n)
                if n in POOL_LO:
                    tiles -= POOL_TILES
                dve.wait_ge(hi_ready, n + 1 + SLOTS * i)
                nc.vector.tensor_tensor(w_lo[:, n % SLOTS, 0:tiles, :], w_raw[:, n % SLOTS, 0:tiles, :],
                                        w_hi[:, n % SLOTS, 0:tiles, :].bitcast(F32), ALU.subtract).then_inc(lo_ready, 1)

            def hidden(f, i, half, ab, first=False):
                m0 = 44 * f + 2 * half + ab
                dve.wait_ge(silu_done, m0 + 1 + 4 * i)
                dve.wait_ge(steps_done, T_GU[f] + 4 * half + 2 * ab + 2 + 8 * i)
                if m0 >= 2 or not first:
                    dve.wait_ge(h_hi_done, m0 - 1 + 4 * i)
                    dve.wait_ge(h_ready, m0 - 1 + 4 * i)
                w = width(half, f)
                nc.vector.scalar_tensor_tensor(h_f32[:, ab, 0:w], silu_g[:, ab, 0:w], 0.5, acc[2 * ab + 1][:, 0:w],
                                               ALU.mult, ALU.mult).then_inc(h_done, 1)

            def hidden_lo(f, i, half, ab):
                m0 = 44 * f + 2 * half + ab
                dve.wait_ge(h_hi_done, m0 + 1 + 4 * i)
                at = bass.ds(2 * i + ab, 1)
                nc.vector.tensor_tensor(h_lo[:, at, cols(half, f)], h_f32[:, ab:ab + 1, 0:width(half, f)],
                                        h_hi[:, at, cols(half, f)].bitcast(F32), ALU.subtract).then_inc(h_ready, 1)

            def gate_up_group(f, i, split, first=False, ahead=0):
                if ahead < 1:
                    hidden(f, i, 0, 0, first)
                hidden_lo(f, i, 0, 0)
                if ahead < 2:
                    hidden(f, i, 0, 1, first)
                hidden_lo(f, i, 0, 1)
                hidden(f, i, 1, 0)
                split(0)
                hidden_lo(f, i, 1, 0)
                split(1)
                hidden(f, i, 1, 1)
                split(2)
                hidden_lo(f, i, 1, 1)
                split(3)

            def residual(L, c, bank, step, first=False, last=False):
                half = L % 2
                dve.wait_ge(steps_done, step)
                x = x_res[:, bass.ds(c, 1), ln_cols(L)]
                a = acc[bank][:, 0:ln_width(L)].unsqueeze(1)
                s = ln_sum[:, half:half + 1, 0:ln_width(L)]
                nc.vector.scalar_tensor_tensor(x, x, ALPHA, a, ALU.mult, ALU.add).then_inc(r_done, 1)
                if last or L in POOL_SUMS or L >= 4:
                    return
                dve.wait_ge(r_done, r_count(L, c))
                if first:
                    if L >= 2:
                        dve.wait_ge(var_done, L - 1)
                    nc.vector.tensor_copy(s, x).then_inc(sum_done, 1)
                else:
                    dve.wait_ge(sum_done, sum_count(L, c - 1))
                    nc.vector.tensor_tensor(s, s, x, ALU.add).then_inc(sum_done, 1)

            def ln_center(L, chunks=range(KT)):
                dve.wait_ge(mean_done, L + 1)
                for c in chunks:
                    x = x_res[:, c, ln_cols(L)]
                    nc.vector.tensor_tensor(x, x, aux[0][:, 0:ln_width(L)], ALU.subtract).then_inc(centered, 1)

            def ln_sum_squares(L):
                s = squares_of(L, 4)
                for c in range(5, KT):
                    dve.wait_ge(squared, KT * L + c + 1)
                    if c >= 6:
                        dve.wait_ge(sq_dve, 3 * L + c - 5)
                    nc.vector.tensor_tensor(s, s, squares_of(L, c), ALU.add).then_inc(sq_dve, 1)

            def ln_rstd(L):
                dve.wait_ge(std_done, L + 1)
                nc.vector.reciprocal(rstd[:, 0:ln_width(L)], rstd[:, 0:ln_width(L)]).then_inc(rstd_done, 1)
                dve.wait_ge(rstd_done, L + 1)

            def ln_scale(L, chunks):
                for c in chunks:
                    x = x_res[:, c, ln_cols(L)]
                    g = G0 + 8 * (L // 2) + c
                    nc.vector.scalar_tensor_tensor(x, x, coef[:, g:g + 1], rstd[:, 0:ln_width(L)], ALU.mult, ALU.mult
                                                   ).then_inc(scaled, 1)

            def ln_lo(L, chunks):
                for c in chunks:
                    b = B0 + 8 * (L // 2) + c
                    dve.wait_ge(x_hi_done, KT * (2 + L) + c + 1)
                    nc.vector.scalar_tensor_tensor(x_lo[:, c, ln_cols(L)], x_res[:, c, ln_cols(L)],
                                                   coef[:, b:b + 1], x_hi[:, c, ln_cols(L)].bitcast(F32),
                                                   ALU.add, ALU.subtract).then_inc(x_ready, 1)

            def ln_apply(L, chunks):
                for c in chunks:
                    ln_scale(L, [c])
                    if L < 4 and c > chunks[0]:
                        ln_lo(L, [c - 1])
                if L < 4:
                    ln_lo(L, [chunks[-1]])

            def rows_stats(t, part):
                w, (c0, c1) = Y_TILES[t][2], STAT_PARTS[part]
                dve.wait_ge(rows_t, rows_count(t, part))
                nc.vector.bn_stats(row_stats[0:w, t, part, :], y_bank(t, c0 // 4)[0:w, P * (c0 % 4):P * (c0 % 4 + c1 - c0)]
                                   ).then_inc(stats_done, 1)
                if part == 2:
                    dve.wait_ge(stats_done, rows_count(t, part))
                    nc.vector.bn_aggr(row_mv[0:w, t, :], row_stats[0:w, t, :, :].rearrange("p b s -> p (b s)")
                                      ).then_inc(mv_done, 1)

            def rows_rstd(t):
                w = Y_TILES[t][2]
                dve.wait_ge(row_std_done, t + 1)
                nc.vector.reciprocal(row_rstd[0:w, t:t + 1], row_std[0:w, t:t + 1]).then_inc(row_rstd_done, 1)
                dve.wait_ge(row_rstd_done, t + 1)
                dve.wait_ge(mv_done, t + 1)
                nc.vector.scalar_tensor_tensor(row_shift[0:w, t:t + 1], row_mv[0:w, t, 0:1], -1.0, row_rstd[0:w, t:t + 1],
                                               ALU.mult, ALU.mult).then_inc(row_shift_done, 1)

            def rows_gain(half, i):
                t, b = y_units(half, False)[i]
                w, feats = Y_TILES[t][2], slice(512 * b, 512 * b + 512)
                dve.wait_ge(norm_rows_in, 32)
                dve.wait_ge(mv_done, t + 1)
                nc.vector.scalar_tensor_tensor(y_rows[0:w, t, feats], y_bank(t, b)[0:w, :], row_mv[0:w, t, 0:1],
                                               g_row[0:w, feats], ALU.subtract, ALU.mult).then_inc(rows_gained, 1)

            def rows_out(half, i):
                units = y_units(half, False)
                t, b = units[i]
                w, feats = Y_TILES[t][2], slice(512 * b, 512 * b + 512)
                dve.wait_ge(rows_gained, len(units) * half + i + 1)
                dve.wait_ge(row_rstd_done, t + 1)
                nc.vector.scalar_tensor_tensor(y_rows[0:w, t, feats], y_rows[0:w, t, feats], row_rstd[0:w, t:t + 1],
                                               b_row[0:w, feats], ALU.mult, ALU.add).then_inc(y_dve, 1)

            def down(f):
                n0, t0 = U_DN[f], T_DN[f]
                if f:
                    dve.wait_ge(res_biased, 4 * KT)
                for c in range(DN_SHARED):
                    for d in range(4):
                        if d == 3:
                            for half in range(2):
                                residual(4 * f + half, c, 2 * (c % 2) + half, t0 + 8 * c + 7 + half, first=c == 0)
                        weight_lo(n0 + 4 * (c + 1) + d)
                t0 += 8 * DN_SHARED
                for c in range(DN_SHARED, KT):
                    for d in range(4):
                        if d == 3:
                            residual(4 * f, c, c % 2, t0 + 4 * (c - DN_SHARED) + 4, last=c == KT - 1)
                        weight_lo(n0 + 4 * (c + 1) + d)
                t0 += 4 * (KT - DN_SHARED)
                for c in range(KT - DN_SHARED):
                    for d in range(4):
                        n = n0 + 4 * (KT + c + 1) + d
                        if d == 3:
                            residual(4 * f + 1, DN_SHARED + c, c % 2, t0 + 4 * c + 4, last=DN_SHARED + c == KT - 1)
                        if n < (U_WI + 2, U_END)[f]:
                            weight_lo(n)
                        if f == 1:
                            if c == 1 and d < 3:
                                for part in range(3):
                                    rows_stats(d, part)
                            if (c, d) == (1, 3):
                                for t in range(3):
                                    rows_rstd(t)
                            if c == 2:
                                rows_gain(0, d)
                            if c == 3 and d < 2:
                                rows_out(0, 2 * d)
                                rows_out(0, 2 * d + 1)
                            if (c, d) == (3, 2):
                                for part in range(2):
                                    for t in range(3, 6):
                                        rows_stats(t, part)
                            continue
                        if (c, d) == (0, 0):
                            ln_center(0)
                        if (c, d) == (0, 3):
                            ln_sum_squares(0)
                        if (c, d) == (1, 1):
                            ln_rstd(0)
                        if (c, d) in LN_PIECES:
                            ln_apply(0, LN_PIECES[c, d])

            def parameters():
                dve.wait_ge(params_t, 1)
                nc.vector.tensor_copy(coef[:, 0:60], aux[0][:, 0:60]).then_inc(coef_ready, 1)
                dve.wait_ge(params_t, 2)
                nc.vector.tensor_tensor(bias_row[:, :], bias_row[:, :], aux[1][0:N_HEADS, 0:T_W], ALU.add
                                        ).then_inc(table_ready, 1)

            def feed_forward(f):
                if f == 1:
                    ln_center(3)
                    ln_sum_squares(3)
                    ln_rstd(3)
                    hidden(f, 0, 0, 0)
                    ln_apply(3, range(0, 4))
                    hidden(f, 0, 0, 1)
                    ln_apply(3, range(4, KT))
                    dve.wait_ge(outputs_out, 16 * MIXER_OUTS)
                gate_up_group(f, 0, lambda u: weight_lo(U_GU[f] + 4 + u), first=f == 0, ahead=f + 1)
                if f == 0:
                    parameters()
                with dve.Fori(1, GU_GROUPS - 1) as i:
                    gate_up_group(f, i, lambda u: weight_lo(U_GU[f] + 4 + u, i))
                gate_up_group(f, GU_GROUPS - 1, lambda u: weight_lo(U_DN[f] + u))
                down(f)

            nc.vector.memset(mean_of[:, :], 1.0 / D_MODEL).then_inc(memset_done, 1)
            nc.vector.memset(eps[:, :], LN_EPS).then_inc(memset_done, 1)
            nc.vector.memset(warm[:, 0:1], 0.0).then_inc(r_done, R_FREE)

            def token_copy(part, c):
                cs = x_cols(part)
                dve.wait_ge(xt_done, KT * part + c + 1)
                nc.vector.tensor_copy(x_res[:, c, cs], x_bank(part, c)[:, 0:cs.stop - cs.start]).then_inc(x0_dve, 1)

            def token_lo(part, c):
                cs = x_cols(part)
                dve.wait_ge(x_hi_done, KT * part + c + 1)
                nc.vector.tensor_tensor(x_lo[:, c, cs], x_res[:, c, cs], x_hi[:, c, cs].bitcast(F32), ALU.subtract
                                        ).then_inc(x_ready, 1)

            for c in (0, 2, 4):
                token_copy(0, c)
            token_lo(0, 0)
            weight_lo(0)
            token_lo(0, 1)
            token_copy(0, 6)
            token_lo(0, 2)
            token_lo(0, 3)
            weight_lo(1)
            for c in range(4, KT):
                token_lo(0, c)
            weight_lo(2)
            weight_lo(3)
            for c0 in (0, 4):
                token_copy(1, c0)
                token_copy(1, c0 + 2)
                for c in range(c0, c0 + 4):
                    token_lo(1, c)
                if c0 == 0:
                    hidden(0, 0, 0, 0, first=True)

            feed_forward(0)
            ln_center(1)
            weight_lo(U_WI + 2)
            ln_sum_squares(1)
            weight_lo(U_WI + 3)
            ln_rstd(1)
            ln_apply(1, range(KT))

            def conv_input(m):
                u, half = WI_STEPS[m]
                c = WI_ORDER[u][1]
                dve.wait_ge(steps_done, T_WI + m + 1)
                cg_step = WI_STEPS.index((WI_ORDER.index(("cg", c)), half))
                dve.wait_ge(z_act, z_count(cg_step, "act"))
                cg = cg_sb[:, half, c % 2, :]
                src = acc[z_bank(m)]
                if half == 0:
                    last = nc.vector.tensor_tensor(u_p[:, c, 2:2 + HALF], cg, src[:, 0:HALF], ALU.mult)
                else:
                    n = PROMPT - HALF
                    nc.vector.tensor_tensor(u_p[:, c, 2 + HALF:2 + PROMPT], cg[:, 0:n], src[:, 0:n], ALU.mult)
                    last = nc.vector.tensor_tensor(
                        u_s[:, c, :, 2:2 + DEC_SEQ], cg[:, n:HALF].rearrange("p (b t) -> p b t", b=DEC_BATCH),
                        src[:, n:HALF].rearrange("p (b t) -> p b t", b=DEC_BATCH), ALU.mult)
                last.then_inc(z_dve, 1)

            def gate(m):
                u, half = WI_STEPS[m]
                c = WI_ORDER[u][1]
                e = BG_ORDER.index((c, half))
                dve.wait_ge(steps_done, T_WI + m + 1)
                dve.wait_ge(taps_added, 2 * CONV_ORDER.index((c, half)) + 2)
                if e >= 2:
                    dve.wait_ge(gated_hi, e - 1)
                    dve.wait_ge(gated_lo, e - 1)
                w = width(half, 1)
                nc.vector.tensor_tensor(h_f32[:, e % 2, 0:w], conv[:, half, c % 2, HALF - w:HALF], acc[z_bank(m)][:, 0:w], ALU.mult
                                        ).then_inc(z_dve, 1)
                dve.wait_ge(gated_hi, e + 1)
                nc.vector.tensor_tensor(mix_lo[:, 4 + c, cols(half, 1)], h_f32[:, e % 2, 0:w],
                                        mix_hi[:, 4 + c, cols(half, 1)].bitcast(F32), ALU.subtract).then_inc(gated_lo, 1)

            def mask_and_max(a):
                b, g = ITEMS[a]
                rows, heads, span = item_shape(a)
                dve.wait_ge(scores_done, a + 1)
                if a == 0:
                    dve.wait_ge(bias_in, 16)
                    dve.wait_ge(kct_copied, 1)
                    dve.wait_ge(kct_done, 1)
                if a >= 3:
                    dve.wait_ge(pt_done, a - 2)
                if b == "s":
                    if g == 0:
                        dve.wait_ge(bias_s_in, 16 * 16)
                    nc.vector.scalar_tensor_tensor(probs[:, a % 3, 0, 0:span], aux[0][:, 0:span], SCALE,
                                                   bias_s[:, g, :], ALU.mult, ALU.add).then_inc(masked, 1)
                    sk = sink_row[:, :]
                else:
                    q0, nq = BLOCKS[b]
                    first = WINDOW - min(WINDOW, q0)
                    for i in range(2):
                        s = aux[i][0:rows, :].rearrange("p (h s) -> p h s", h=2)[:, :, 0:span]
                        last = nc.vector.scalar_tensor_tensor(
                            probs[0:rows, a % 3, 2 * i:2 * i + 2, 0:span], s, SCALE,
                            bias[0:rows, 4 * g + 2 * i:4 * g + 2 * i + 2, first:first + span], ALU.mult, ALU.add)
                    last.then_inc(masked, 1)
                    sk = sinks[0:rows, 4 * g:4 * g + 4]
                dve.wait_ge(masked, a + 1)
                mx, neg = row_max[0:rows, a % 3, 0:heads], neg_max[0:rows, a % 3, 0:heads]
                nc.vector.tensor_reduce(mx, probs[0:rows, a % 3, 0:heads, 0:span], AX_X, ALU.max).then_inc(max_done, 1)
                dve.wait_ge(max_done, a + 1)
                nc.vector.tensor_tensor(mx, mx, sk, ALU.max).then_inc(max_sink, 1)
                dve.wait_ge(max_sink, a + 1)
                nc.vector.tensor_scalar(neg, mx, -1.0, None, ALU.mult).then_inc(neg_ready, 1)

            def denominators(a):
                rows, heads, span = item_shape(a)
                dve.wait_ge(exps_done, a + 1)
                den, rd = row_sum[0:rows, a % 3, 0:heads], r_den[0:rows, a % 3, 0:heads]
                nc.vector.tensor_tensor(den, den, sink_exp[0:rows, a % 3, 0:heads], ALU.add).then_inc(den_done, 1)
                dve.wait_ge(den_done, a + 1)
                nc.vector.reciprocal(rd, den).then_inc(rden_done, 1)
                dve.wait_ge(rden_done, a + 1)
                for h in range(heads):
                    p = probs[0:rows, a % 3, h, 0:span]
                    last = nc.vector.tensor_scalar(p, p, r_den[0:rows, a % 3, h:h + 1], None, ALU.mult)
                last.then_inc(probs_ready, 1)

            def attended_lo(a):
                b, g = ITEMS[a]
                dve.wait_ge(att_hi, a + 1)
                if b == "s":
                    for kv in range(N_KV):
                        rows = slice(kv * HEAD_DIM, (kv + 1) * HEAD_DIM)
                        for h in range(GQA):
                            lo = nc.vector.tensor_tensor(sample_cols(mix_lo, rows, h, g), sample_out(rows, kv, h),
                                                         sample_cols(mix_hi, rows, h, g).bitcast(F32), ALU.subtract)
                else:
                    q0, nq = BLOCKS[b]
                    rows = slice(g * HEAD_DIM, (g + 1) * HEAD_DIM)
                    lo = nc.vector.tensor_tensor(mix_lo[rows, 0:GQA, q0:q0 + nq],
                                                 acc[3][rows, 0:GQA * nq].rearrange("p (h q) -> p h q", h=GQA),
                                                 mix_hi[rows, 0:GQA, q0:q0 + nq].bitcast(F32), ALU.subtract)
                lo.then_inc(att_lo, 1)

            def attention(k, odd):
                if odd:
                    if k < len(ITEMS):
                        mask_and_max(k)
                    if 3 <= k < len(ITEMS) + 3:
                        attended_lo(k - 3)
                elif 1 <= k < len(ITEMS) + 1:
                    denominators(k - 1)

            def split_after(step):
                for n in range(U_WI + SLOTS, U_GU[1] + SLOTS):
                    if free_after(n - SLOTS) == step + 1:
                        weight_lo(n)

            dve.wait_ge(steps_done, T_WI)
            nc.vector.memset(bias_s[:, :, WINDOW:S_COLS], MASKED).then_inc(zero_done, 1)
            nc.vector.memset(q_diag[:, :, :], 0.0)
            nc.vector.memset(q_t[:, :, 0:N_META], 0.0)
            nc.vector.memset(u_p[:, :, 0:2], 0.0).then_inc(zero_done, 1)
            for m in range(len(WI_STEPS)):
                kind = WI_ORDER[WI_STEPS[m][0]][0]
                if m >= AB and (m - AB) % 2 == 0:
                    attention((m - AB) // 2, odd=False)
                if kind == "h":
                    conv_input(m)
                if kind == "bg":
                    gate(m)
                split_after(T_WI + m)
                if m == AB - 1:
                    dve.wait_ge(z_act, z_count(AB - 1, "act"))
                    dve.wait_ge(zero_done, 2)
                    for kv in range(N_KV):
                        rows = slice(kv * HEAD_DIM, (kv + 1) * HEAD_DIM)
                        for h in range(GQA):
                            dst = q_diag[rows, :, :].rearrange("p j (b g t) -> p (j b) g t", b=4, t=DEC_SEQ)[:, :, GQA * kv + h]
                            last = nc.vector.tensor_copy(
                                dst, q_t[rows, h, PROMPT:TOK].rearrange("p (b t) -> p b t", t=DEC_SEQ))
                    last.then_inc(qd_ready, 1)
                if m > AB and (m - AB) % 2 == 1:
                    attention((m - AB) // 2, odd=True)

            for k in range(WO_STEPS):
                s = len(WI_STEPS) - AB + k
                if s % 2 == 0:
                    attention(s // 2, odd=False)
                if k % KT == 0:
                    dve.wait_ge(res_biased, KT * (1 + k // KT))
                if k == 8:
                    ln_center(2)
                residual(2 + k // KT, k % KT, wo_bank(k), T_WO + k + 1, first=k % KT == 0, last=k % KT == KT - 1)
                if k == 8:
                    ln_sum_squares(2)
                if k == 9:
                    ln_rstd(2)
                split_after(T_WO + k)
                if s % 2:
                    attention(s // 2, odd=True)
                if k in WO_PIECES:
                    ln_apply(2, WO_PIECES[k])
            feed_forward(1)
            for t in range(3, 6):
                rows_stats(t, 2)
            rows_rstd(3)
            rows_rstd(4)
            rows_gain(1, 0)
            rows_gain(1, 1)
            rows_rstd(5)
            rows_out(1, 0)
            rows_gain(1, 2)
            rows_out(1, 1)
            rows_gain(1, 3)
            rows_out(1, 2)
            rows_out(1, 3)

        @block.gpsimd
        def _(pool):
            def residual_shift(L):
                for c in range(KT):
                    pool.wait_ge(x_ready, KT * (2 + L) + c + 1)
                    b = B0 + 8 * (L // 2) + c
                    x = x_res[:, c, ln_cols(L)]
                    nc.gpsimd.tensor_scalar(x, x, coef[:, b:b + 1], None, ALU.add).then_inc(res_biased, 1)

            def residual_sum(L, c):
                s = ln_sum[:, L % 2, 0:ln_width(L)]
                pool.wait_ge(r_done, r_count(L, c))
                if c == 1:
                    pool.wait_ge(var_done, L - 1)
                    nc.gpsimd.tensor_tensor(s, x_res[:, 0, ln_cols(L)], x_res[:, 1, ln_cols(L)], ALU.add
                                            ).then_inc(sum_done, 2)
                else:
                    pool.wait_ge(sum_done, sum_count(L, c - 1))
                    nc.gpsimd.tensor_tensor(s, s, x_res[:, c, ln_cols(L)], ALU.add).then_inc(sum_done, 1)

            def weight_lo(n):
                pool.wait_ge(hi_ready, n + 1)
                nc.gpsimd.tensor_tensor(w_lo[:, n % SLOTS, KT - POOL_TILES:KT, :], w_raw[:, n % SLOTS, KT - POOL_TILES:KT, :],
                                        w_hi[:, n % SLOTS, KT - POOL_TILES:KT, :].bitcast(F32), ALU.subtract
                                        ).then_inc(lo_pool, 1)

            def ln_sum_squares(L):
                s = ln_sum[:, L % 2, 0:ln_width(L)]
                for c in range(1, 4):
                    pool.wait_ge(squared, KT * L + c + 1)
                    if c >= 2:
                        pool.wait_ge(sq_pool, 3 * L + c - 1)
                    nc.gpsimd.tensor_tensor(s, squares_of(L, 0) if c == 1 else s, squares_of(L, c), ALU.add
                                            ).then_inc(sq_pool, 1)

            def convolve(e):
                c, half = CONV_ORDER[e]
                pool.wait_ge(z_dve, step_count("h", c, half))
                if e >= 1:
                    pool.wait_ge(taps_added, 2 * e)
                if c >= 2:
                    pool.wait_ge(z_dve, step_count("bg", c - 2, half))
                n = HALF if half == 0 else PROMPT - HALF
                for j in range(3):
                    w = C0 + CT * j + c
                    at = half * HALF + j
                    last = nc.gpsimd.tensor_scalar(taps[:, j, 0:n], u_p[:, c, at:at + n], coef[:, w:w + 1], None, ALU.mult)
                    if half:
                        last = nc.gpsimd.tensor_scalar(
                            taps[:, j, n:HALF].rearrange("p (b t) -> p b t", b=DEC_BATCH),
                            u_s[:, c, :, j:j + DEC_SEQ], coef[:, w:w + 1], None, ALU.mult)
                last.then_inc(taps_done, 1)
                pool.wait_ge(taps_done, e + 1)
                nc.gpsimd.tensor_tensor(taps[:, 0, :], taps[:, 0, :], taps[:, 1, :], ALU.add).then_inc(taps_added, 1)
                pool.wait_ge(taps_added, 2 * e + 1)
                nc.gpsimd.tensor_tensor(conv[:, half, c % 2, :], taps[:, 0, :], taps[:, 2, :], ALU.add
                                        ).then_inc(taps_added, 1)

            for n in range(4):
                weight_lo(n)
            pool.wait_ge(coef_ready, 1)
            for L in range(2):
                ln_sum_squares(L)
                residual_shift(L)
            for m in range(AB, len(WI_STEPS)):
                u, half = WI_STEPS[m]
                if WI_ORDER[u][0] == "h":
                    if m == WI_STEPS.index((WI_ORDER.index(("h", 0)), 0)):
                        pool.wait_ge(zero_done, 2)
                        pool.wait_ge(kct_copied, 1)
                    convolve(CONV_ORDER.index((WI_ORDER[u][1], half)))
            for k in range(WO_STEPS):
                if 1 <= k % KT <= KT - 2:
                    residual_sum(2 + k // KT, k % KT)
                if k == 8:
                    ln_sum_squares(2)
                if U_WO + k + SLOTS in POOL_LO:
                    weight_lo(U_WO + k + SLOTS)
            ln_sum_squares(3)
            residual_shift(2)
            residual_shift(3)
            pool.wait_ge(norm_rows_in, 32)
            for half in range(2):
                for i, (t, b) in enumerate(y_units(half, True)):
                    w, feats = Y_TILES[t][2], slice(512 * b, 512 * b + 512)
                    y = y_rows[0:w, t, feats]
                    pool.wait_ge(rows_normed, 2 * half + i + 1)
                    nc.gpsimd.tensor_tensor(y, y, g_row[0:w, feats], ALU.mult).then_inc(rows_pool, 1)
                    pool.wait_ge(rows_pool, 2 * half + i + 1)
                    nc.gpsimd.tensor_tensor(y, y, b_row[0:w, feats], ALU.add).then_inc(y_pool, 1)


_INS = ["x_prompt", "x_sample", "cache_k", "cache_v", "state_conv", "meta_tokens", "rel_bias", "w_in", "conv_w",
        "attn_sink", "w_out", "ffn_w_gate", "ffn_w_up", "ffn_w_down", "ln_g", "ln_b"]
_OUTS = [(1, SEQ, D_MODEL), (DEC_BATCH, DEC_SEQ, D_MODEL), (1, 1, WINDOW, N_KV, HEAD_DIM),
         (1, 1, WINDOW, N_KV, HEAD_DIM), (1, 1, 2, D_CONV), (1, DEC_BATCH, WINDOW, N_KV, HEAD_DIM),
         (1, DEC_BATCH, WINDOW, N_KV, HEAD_DIM), (1, DEC_BATCH, 2, D_CONV)]


def kernel(**inputs):
    import concourse.bacc as bacc
    from concourse.bass_utils import run_bass_kernel_spmd

    nc = bacc.Bacc("TRN2", target_bir_lowering=False, num_devices=1, dynamic_dma_scratch_size=1024)
    one_hot, mask = bias_constants()
    arrays = {name: np.ascontiguousarray(inputs[name]) for name in _INS}
    arrays |= {"identity": np.eye(P, dtype=np.float32), "one_hot": one_hot, "mask_row": mask}
    args = [nc.dram_tensor(f"in_{n}", a.shape, mybir.dt.from_np(a.dtype), kind="ExternalInput").ap()
            for n, a in arrays.items()]
    args += [nc.dram_tensor(f"out_{i}", s, F32, kind="ExternalOutput").ap() for i, s in enumerate(_OUTS)]
    build(nc, *args)
    r = run_bass_kernel_spmd(nc, [{f"in_{n}": a for n, a in arrays.items()}], core_ids=[0])
    return tuple(r.results[0][f"out_{i}"] for i in range(len(_OUTS)))
```
